# Optimizing a Trainium2 kernel written in Bass

```python
import math
import jax, jax.numpy as jnp
from jax import lax
import numpy as np

D_MODEL = 1024
BATCH = 1
SEQ = 256
DEPTH = 2

N_MIXERS = 3
GRID_W = 64
Q_BLOCK = 128
EPS = 1e-6
D_FF = 2816
FFN_RES = 0.5

DIFF_HEAD_DIM = 64
DIFF_HEADS = D_MODEL // (2 * DIFF_HEAD_DIM)
ROPE_THETA = 500000.0
ROPE_DIMS = DIFF_HEAD_DIM // 4

NA_HEAD_DIM = 64
NA_HEADS = D_MODEL // NA_HEAD_DIM
NA_WIN_H = 8
NA_WIN_W = 16

GQA_HEAD_DIM = 64
GQA_Q_HEADS = D_MODEL // GQA_HEAD_DIM
GQA_KV_HEADS = GQA_Q_HEADS // 4
AXIAL_THETA = 10000.0

N_A = len(range(0, DEPTH, N_MIXERS))
N_B = len(range(1, DEPTH, N_MIXERS))
N_C = len(range(2, DEPTH, N_MIXERS))


def _rmsnorm(x, g):
    xf = x.astype(jnp.float32)
    y = xf * lax.rsqrt(jnp.mean(xf * xf, axis=-1, keepdims=True) + EPS)
    return (y * g.astype(jnp.float32)).astype(x.dtype)

def _swiglu(x, wg, wu, wd):
    return (jax.nn.silu(x @ wg) * (x @ wu)) @ wd

def _rope_angles(pos, dims, theta):
    inv = theta ** (-jnp.arange(0, dims, 2, dtype=jnp.float32) / dims)
    return pos[:, None] * inv[None, :]

def _rotate(x, ang):
    m = ang.shape[1]
    ang = ang.reshape((1, ang.shape[0]) + (1,) * (x.ndim - 3) + (m,))
    cos = jnp.cos(ang).astype(x.dtype)
    sin = jnp.sin(ang).astype(x.dtype)
    x1, x2 = x[..., :m], x[..., m:]
    return jnp.concatenate([x1 * cos - x2 * sin, x2 * cos + x1 * sin], axis=-1)

def _to_blocks(q):
    b, s = q.shape[:2]
    return jnp.moveaxis(q.reshape((b, s // Q_BLOCK, Q_BLOCK) + q.shape[2:]), 1, 0)

def _from_blocks(o):
    o = jnp.moveaxis(o, 0, 1)
    return o.reshape((o.shape[0], o.shape[1] * o.shape[2]) + o.shape[3:])

def _diff_attention(h, w_in, w_out, lam_vecs, subln_g, layer_idx):
    b, s, _ = h.shape
    nh, dh = DIFF_HEADS, DIFF_HEAD_DIM
    q, k, v = jnp.split(h @ w_in, 3, axis=-1)
    q = q.reshape(b, s, nh, 2, dh)
    k = k.reshape(b, s, nh, 2, dh)
    v = v.reshape(b, s, nh, 2 * dh)
    ang = _rope_angles(jnp.arange(s, dtype=jnp.float32), ROPE_DIMS, ROPE_THETA)
    q = jnp.concatenate([_rotate(q[..., :ROPE_DIMS], ang), q[..., ROPE_DIMS:]], axis=-1)
    k = jnp.concatenate([_rotate(k[..., :ROPE_DIMS], ang), k[..., ROPE_DIMS:]], axis=-1)
    lam_init = 0.8 - 0.6 * math.exp(-0.3 * layer_idx)
    lv = lam_vecs.astype(jnp.float32)
    lam = jnp.exp(jnp.sum(lv[0] * lv[1])) - jnp.exp(jnp.sum(lv[2] * lv[3])) + lam_init
    scale = dh ** -0.5

    def block(qb):
        sc = jnp.einsum('bqhcd,bshcd->bhcqs', qb, k).astype(jnp.float32) * scale
        p = jax.nn.softmax(sc, axis=-1)
        a = (p[:, :, 0] - lam * p[:, :, 1]).astype(v.dtype)
        return jnp.einsum('bhqs,bshe->bqhe', a, v)

    o = _from_blocks(lax.map(block, _to_blocks(q)))
    o = _rmsnorm(o, subln_g) * (1.0 - lam_init)
    return o.reshape(b, s, nh * 2 * dh) @ w_out

def _neighborhood_attention(h, w_in, w_out, rpb):
    b, s, _ = h.shape
    nh, dh = NA_HEADS, NA_HEAD_DIM
    rows = s // GRID_W
    kh = min(NA_WIN_H, rows)
    kw = NA_WIN_W
    q, k, v = jnp.split(h @ w_in, 3, axis=-1)
    q = q.reshape(b, rows, GRID_W, nh, dh)
    k = k.reshape(b, rows, GRID_W, nh, dh)
    v = v.reshape(b, rows, GRID_W, nh, dh)
    cols = jnp.arange(GRID_W)
    col_start = jnp.clip(cols - kw // 2, 0, GRID_W - kw)
    col_idx = col_start[:, None] + jnp.arange(kw)[None, :]
    dc = col_idx - cols[:, None] + (NA_WIN_W - 1)
    scale = dh ** -0.5

    def row_step(r):
        r0 = jnp.clip(r - kh // 2, 0, rows - kh)
        dr = r0 + jnp.arange(kh) - r + (NA_WIN_H - 1)
        k_band = lax.dynamic_slice_in_dim(k, r0, kh, axis=1)
        v_band = lax.dynamic_slice_in_dim(v, r0, kh, axis=1)
        k_win = k_band[:, :, col_idx]
        v_win = v_band[:, :, col_idx]
        q_row = lax.dynamic_index_in_dim(q, r, axis=1, keepdims=False)
        bias = rpb[:, dr[None, :, None], dc[:, None, :]]
        sc = jnp.einsum('bqhd,brqjhd->bhqrj', q_row, k_win).astype(jnp.float32) * scale
        sc = sc + bias.astype(jnp.float32)[None]
        p = jax.nn.softmax(sc.reshape(b, nh, GRID_W, kh * kw), axis=-1)
        p = p.reshape(sc.shape).astype(v.dtype)
        return jnp.einsum('bhqrj,brqjhd->bqhd', p, v_win)

    o = lax.map(row_step, jnp.arange(rows))
    o = jnp.moveaxis(o, 0, 1).reshape(b, s, nh * dh)
    return o @ w_out

def _gqa_axial(h, w_in, w_out, qk_g):
    b, s, _ = h.shape
    nq, nkv, dh = GQA_Q_HEADS, GQA_KV_HEADS, GQA_HEAD_DIM
    grp = nq // nkv
    qkv = h @ w_in
    q = qkv[..., :nq * dh].reshape(b, s, nkv, grp, dh)
    k = qkv[..., nq * dh:(nq + nkv) * dh].reshape(b, s, nkv, dh)
    v = qkv[..., (nq + nkv) * dh:].reshape(b, s, nkv, dh)
    q = _rmsnorm(q, qk_g[0])
    k = _rmsnorm(k, qk_g[1])
    t = jnp.arange(s)
    half = dh // 2
    ang_r = _rope_angles((t // GRID_W).astype(jnp.float32), half, AXIAL_THETA)
    ang_c = _rope_angles((t % GRID_W).astype(jnp.float32), half, AXIAL_THETA)
    q = jnp.concatenate([_rotate(q[..., :half], ang_r), _rotate(q[..., half:], ang_c)], axis=-1)
    k = jnp.concatenate([_rotate(k[..., :half], ang_r), _rotate(k[..., half:], ang_c)], axis=-1)
    scale = dh ** -0.5

    def block(qb):
        sc = jnp.einsum('bqkgd,bskd->bkgqs', qb, k).astype(jnp.float32) * scale
        p = jax.nn.softmax(sc, axis=-1).astype(v.dtype)
        return jnp.einsum('bkgqs,bskd->bqkgd', p, v)

    o = _from_blocks(lax.map(block, _to_blocks(q)))
    return o.reshape(b, s, nq * dh) @ w_out

def first_inputs(seed: int = 0) -> dict:
    key = jax.random.key(seed)
    ks = jax.random.split(key, 20)

    def w(k, shape, fan_in):
        return jax.random.normal(k, shape, jnp.float32) * fan_in ** -0.5

    def gain(k, shape):
        return 1.0 + 0.05 * jax.random.normal(k, shape, jnp.float32)

    diff_w = DIFF_HEADS * 2 * DIFF_HEAD_DIM
    na_w = NA_HEADS * NA_HEAD_DIM
    gqa_q = GQA_Q_HEADS * GQA_HEAD_DIM
    gqa_in = (GQA_Q_HEADS + 2 * GQA_KV_HEADS) * GQA_HEAD_DIM
    return {
        'x': jax.random.normal(ks[0], (BATCH, SEQ, D_MODEL), jnp.float32),
        'norm_g': gain(ks[1], (DEPTH, 6, D_MODEL)),
        'ffn1_wg': w(ks[2], (DEPTH, D_MODEL, D_FF), D_MODEL),
        'ffn1_wu': w(ks[3], (DEPTH, D_MODEL, D_FF), D_MODEL),
        'ffn1_wd': w(ks[4], (DEPTH, D_FF, D_MODEL), D_FF),
        'ffn2_wg': w(ks[5], (DEPTH, D_MODEL, D_FF), D_MODEL),
        'ffn2_wu': w(ks[6], (DEPTH, D_MODEL, D_FF), D_MODEL),
        'ffn2_wd': w(ks[7], (DEPTH, D_FF, D_MODEL), D_FF),
        'diff_w_in': w(ks[8], (N_A, D_MODEL, 3 * diff_w), D_MODEL),
        'diff_w_out': w(ks[9], (N_A, diff_w, D_MODEL), diff_w),
        'diff_lambda': 0.1 * jax.random.normal(ks[10], (N_A, 4, DIFF_HEAD_DIM), jnp.float32),
        'diff_subln': gain(ks[11], (N_A, 2 * DIFF_HEAD_DIM)),
        'na_w_in': w(ks[12], (N_B, D_MODEL, 3 * na_w), D_MODEL),
        'na_w_out': w(ks[13], (N_B, na_w, D_MODEL), na_w),
        'na_rpb': 0.1 * jax.random.normal(ks[14], (N_B, NA_HEADS, 2 * NA_WIN_H - 1, 2 * NA_WIN_W - 1), jnp.float32),
        'gqa_w_in': w(ks[15], (N_C, D_MODEL, gqa_in), D_MODEL),
        'gqa_w_out': w(ks[16], (N_C, gqa_q, D_MODEL), gqa_q),
        'gqa_qk_norm': gain(ks[17], (N_C, 2, GQA_HEAD_DIM)),
    }

def first_block(x, norm_g, ffn1_wg, ffn1_wu, ffn1_wd, ffn2_wg, ffn2_wu, ffn2_wd,
              diff_w_in, diff_w_out, diff_lambda, diff_subln,
              na_w_in, na_w_out, na_rpb,
              gqa_w_in, gqa_w_out, gqa_qk_norm):
    h = x
    for i in range(DEPTH):
        g = norm_g[i]
        h = h + FFN_RES * _rmsnorm(_swiglu(_rmsnorm(h, g[0]), ffn1_wg[i], ffn1_wu[i], ffn1_wd[i]), g[1])
        u = _rmsnorm(h, g[2])
        kind, j = i % N_MIXERS, i // N_MIXERS
        if kind == 0:
            m = _diff_attention(u, diff_w_in[j], diff_w_out[j], diff_lambda[j], diff_subln[j], i)
        elif kind == 1:
            m = _neighborhood_attention(u, na_w_in[j], na_w_out[j], na_rpb[j])
        else:
            m = _gqa_axial(u, gqa_w_in[j], gqa_w_out[j], gqa_qk_norm[j])
        h = h + _rmsnorm(m, g[3])
        h = h + FFN_RES * _rmsnorm(_swiglu(_rmsnorm(h, g[4]), ffn2_wg[i], ffn2_wu[i], ffn2_wd[i]), g[5])
    return h


DEPTH_2 = 1

HEAD_DIM = 64
N_MOBA_HEADS = 8
N_FOX_HEADS = 8
MOBA_WIDTH = N_MOBA_HEADS * HEAD_DIM
FOX_WIDTH = N_FOX_HEADS * HEAD_DIM
MOBA_BLOCK = 256
MOBA_TOPK = 3
Q_CHUNK = 128
ROPE_DIM = HEAD_DIM // 4
D_FF_2 = 11 * D_MODEL // 4
CONV_WIDTH = 3
NORM_EPS = 1e-6
N_BRANCH = 2
NEG_INF = -1e30
IN_SPLITS = (MOBA_WIDTH, MOBA_WIDTH, MOBA_WIDTH, FOX_WIDTH, FOX_WIDTH, FOX_WIDTH, N_FOX_HEADS, N_BRANCH * D_MODEL)
IN_COLS = sum(IN_SPLITS)


def rms_norm(x, g):
    xf = x.astype(jnp.float32)
    y = xf * lax.rsqrt(jnp.mean(xf * xf, axis=-1, keepdims=True) + NORM_EPS)
    return (y * g.astype(jnp.float32)).astype(x.dtype)

def split_heads(t, n_heads):
    b, s, _ = t.shape
    return t.reshape(b, s, n_heads, HEAD_DIM).transpose(0, 2, 1, 3)

def merge_heads(t):
    b, h, s, d = t.shape
    return t.transpose(0, 2, 1, 3).reshape(b, s, h * d)

def partial_rope(x, pos):
    half = ROPE_DIM // 2
    inv_freq = jnp.power(ROPE_THETA, -jnp.arange(half, dtype=jnp.float32) * 2.0 / ROPE_DIM)
    ang = pos.astype(jnp.float32)[:, None] * inv_freq[None, :]
    cos, sin = jnp.cos(ang), jnp.sin(ang)
    xr = x[..., :ROPE_DIM].astype(jnp.float32)
    x1, x2 = xr[..., :half], xr[..., half:]
    rot = jnp.concatenate([x1 * cos - x2 * sin, x2 * cos + x1 * sin], axis=-1).astype(x.dtype)
    return jnp.concatenate([rot, x[..., ROPE_DIM:]], axis=-1)

def moba_attention(q, k, v):
    B, H, S, Dh = q.shape
    nb = -(-S // MOBA_BLOCK)
    pad = nb * MOBA_BLOCK - S
    nqc = S // Q_CHUNK
    scale = Dh ** -0.5
    kp = jnp.pad(k, ((0, 0), (0, 0), (0, pad), (0, 0)))
    vp = jnp.pad(v, ((0, 0), (0, 0), (0, pad), (0, 0)))
    kb = kp.reshape(B, H, nb, MOBA_BLOCK, Dh)
    vb = vp.reshape(B, H, nb, MOBA_BLOCK, Dh)
    k_mean = jnp.mean(kb, axis=3, dtype=jnp.float32)
    gate = jnp.einsum('bhsd,bhnd->bhsn', q.astype(jnp.float32), k_mean)
    pos = jnp.arange(S)
    q_blk = pos // MOBA_BLOCK
    fully_past = jnp.arange(nb)[None, :] < q_blk[:, None]
    gate = jnp.where(fully_past, gate, -jnp.inf)
    k_sel = min(MOBA_TOPK, nb)
    top_val, top_idx = lax.top_k(gate, k_sel)
    top_ok = jnp.isfinite(top_val)
    own = jnp.broadcast_to(q_blk[None, None, :, None], (B, H, S, 1)).astype(top_idx.dtype)
    sel_idx = jnp.concatenate([top_idx, own], axis=-1)
    sel_ok = jnp.concatenate([top_ok, jnp.ones((B, H, S, 1), dtype=bool)], axis=-1)
    ns = k_sel + 1

    def to_chunks(t):
        tail = t.shape[3:]
        t = t.reshape((B, H, nqc, Q_CHUNK) + tail)
        t = jnp.moveaxis(t, 2, 1)
        return t.reshape((B * nqc, H, Q_CHUNK) + tail)

    q_c = to_chunks(q)
    idx_c = to_chunks(sel_idx)
    ok_c = to_chunks(sel_ok)
    b_ids = jnp.repeat(jnp.arange(B), nqc)
    qpos_c = jnp.tile(pos.reshape(nqc, Q_CHUNK), (B, 1))
    head_ix = jnp.arange(H)[:, None, None]
    key_off = jnp.arange(MOBA_BLOCK)

    def step(args):
        b, qi, idx, ok, qp = args
        k_g = kb[b][head_ix, idx]
        v_g = vb[b][head_ix, idx]
        s = jnp.einsum('hcd,hcnld->hcnl', qi, k_g, preferred_element_type=jnp.float32) * scale
        kpos = idx[..., None] * MOBA_BLOCK + key_off
        mask = ok[..., None] & (kpos <= qp[None, :, None, None])
        s = jnp.where(mask, s, NEG_INF)
        p = jax.nn.softmax(s.reshape(H, Q_CHUNK, ns * MOBA_BLOCK), axis=-1)
        p = p.reshape(H, Q_CHUNK, ns, MOBA_BLOCK).astype(v_g.dtype)
        o = jnp.einsum('hcnl,hcnld->hcd', p, v_g, preferred_element_type=jnp.float32)
        return o.astype(qi.dtype)

    out = lax.map(step, (b_ids, q_c, idx_c, ok_c, qpos_c))
    out = out.reshape(B, nqc, H, Q_CHUNK, Dh)
    return jnp.moveaxis(out, 1, 2).reshape(B, H, S, Dh)

def forgetting_attention(q, k, v, log_f):
    B, H, S, Dh = q.shape
    nqc = S // Q_CHUNK
    scale = Dh ** -0.5
    c = jnp.cumsum(log_f, axis=-1)
    pos = jnp.arange(S)
    q_c = jnp.moveaxis(q.reshape(B, H, nqc, Q_CHUNK, Dh), 2, 0)
    c_c = jnp.moveaxis(c.reshape(B, H, nqc, Q_CHUNK), 2, 0)
    qpos_c = pos.reshape(nqc, Q_CHUNK)

    def step(args):
        qi, ci, qp = args
        s = jnp.einsum('bhcd,bhsd->bhcs', qi, k, preferred_element_type=jnp.float32) * scale
        s = s + ci[..., None] - c[:, :, None, :]
        s = jnp.where(pos[None, :] <= qp[:, None], s, NEG_INF)
        p = jax.nn.softmax(s, axis=-1).astype(v.dtype)
        o = jnp.einsum('bhcs,bhsd->bhcd', p, v, preferred_element_type=jnp.float32)
        return o.astype(qi.dtype)

    out = lax.map(step, (q_c, c_c, qpos_c))
    return jnp.moveaxis(out, 0, 2).reshape(B, H, S, Dh)

def causal_depthwise_conv(t, w, bias):
    kern = w.reshape(CONV_WIDTH, 1, w.shape[-1]).astype(t.dtype)
    y = lax.conv_general_dilated(t, kern, window_strides=(1,), padding=[(CONV_WIDTH - 1, 0)],
                                 dimension_numbers=('NWC', 'WIO', 'NWC'),
                                 feature_group_count=t.shape[-1])
    return y + bias.astype(t.dtype)

def second_inputs(seed: int = 0) -> dict:
    key = jax.random.key(seed)
    ks = jax.random.split(key, 18)
    f32 = jnp.float32

    def nrm(k, shape, scale):
        return jax.random.normal(k, shape, f32) * scale

    def gain(k, shape):
        return 1.0 + 0.02 * jax.random.normal(k, shape, f32)

    return {
        "x": nrm(ks[0], (BATCH, SEQ, D_MODEL), 1.0),
        "attn_norm_g": gain(ks[1], (DEPTH_2, D_MODEL)),
        "w_in": nrm(ks[2], (DEPTH_2, D_MODEL, IN_COLS), D_MODEL ** -0.5),
        "b_forget": nrm(ks[3], (DEPTH_2, N_FOX_HEADS), 0.1),
        "b_gate": nrm(ks[4], (DEPTH_2, N_BRANCH, D_MODEL), 0.1),
        "moba_q_norm_g": gain(ks[5], (DEPTH_2, HEAD_DIM)),
        "moba_k_norm_g": gain(ks[6], (DEPTH_2, HEAD_DIM)),
        "fox_q_norm_g": gain(ks[7], (DEPTH_2, HEAD_DIM)),
        "fox_k_norm_g": gain(ks[8], (DEPTH_2, HEAD_DIM)),
        "w_branch_moba": nrm(ks[9], (DEPTH_2, MOBA_WIDTH, D_MODEL), MOBA_WIDTH ** -0.5),
        "w_branch_fox": nrm(ks[10], (DEPTH_2, FOX_WIDTH, D_MODEL), FOX_WIDTH ** -0.5),
        "w_out": nrm(ks[11], (DEPTH_2, D_MODEL, D_MODEL), D_MODEL ** -0.5),
        "ffn_norm_g": gain(ks[12], (DEPTH_2, D_MODEL)),
        "w_ffn_up": nrm(ks[13], (DEPTH_2, D_MODEL, 2 * D_FF_2), D_MODEL ** -0.5),
        "ffn_conv_w": nrm(ks[14], (DEPTH_2, CONV_WIDTH, D_FF_2), CONV_WIDTH ** -0.5),
        "ffn_conv_b": nrm(ks[15], (DEPTH_2, D_FF_2), 0.02),
        "w_ffn_down": nrm(ks[16], (DEPTH_2, D_FF_2, D_MODEL), D_FF_2 ** -0.5),
    }

def second_block(x, attn_norm_g, w_in, b_forget, b_gate, moba_q_norm_g, moba_k_norm_g,
              fox_q_norm_g, fox_k_norm_g, w_branch_moba, w_branch_fox, w_out,
              ffn_norm_g, w_ffn_up, ffn_conv_w, ffn_conv_b, w_ffn_down):
    B, S, D = x.shape
    pos = jnp.arange(S)
    bounds = []
    acc = 0
    for w in IN_SPLITS[:-1]:
        acc += w
        bounds.append(acc)
    for l in range(DEPTH_2):
        h = rms_norm(x, attn_norm_g[l])
        proj = jnp.einsum('bsd,de->bse', h, w_in[l])
        qa, ka, va, qb, kb, vb, f_logit, g_logit = jnp.split(proj, bounds, axis=-1)
        qa = partial_rope(rms_norm(split_heads(qa, N_MOBA_HEADS), moba_q_norm_g[l]), pos)
        ka = partial_rope(rms_norm(split_heads(ka, N_MOBA_HEADS), moba_k_norm_g[l]), pos)
        va = split_heads(va, N_MOBA_HEADS)
        o_a = merge_heads(moba_attention(qa, ka, va))
        qb = rms_norm(split_heads(qb, N_FOX_HEADS), fox_q_norm_g[l])
        kb = rms_norm(split_heads(kb, N_FOX_HEADS), fox_k_norm_g[l])
        vb = split_heads(vb, N_FOX_HEADS)
        log_f = jax.nn.log_sigmoid(f_logit.astype(jnp.float32) + b_forget[l].astype(jnp.float32))
        log_f = log_f.transpose(0, 2, 1)
        o_b = merge_heads(forgetting_attention(qb, kb, vb, log_f))
        br_a = jnp.einsum('bse,ed->bsd', o_a, w_branch_moba[l])
        br_b = jnp.einsum('bse,ed->bsd', o_b, w_branch_fox[l])
        gates = jax.nn.sigmoid(g_logit.astype(jnp.float32).reshape(B, S, N_BRANCH, D)
                               + b_gate[l].astype(jnp.float32)).astype(x.dtype)
        merged = gates[:, :, 0] * br_a + gates[:, :, 1] * br_b
        x = x + jnp.einsum('bsd,de->bse', merged, w_out[l])
        h2 = rms_norm(x, ffn_norm_g[l])
        up = jnp.einsum('bsd,df->bsf', h2, w_ffn_up[l])
        u, g = jnp.split(up, 2, axis=-1)
        g = causal_depthwise_conv(g, ffn_conv_w[l], ffn_conv_b[l])
        x = x + jnp.einsum('bsf,fd->bsd', jax.nn.silu(g) * u, w_ffn_down[l])
    return x


def setup_inputs(seed=0):
    out = dict(first_inputs(seed))
    for name, value in second_inputs(seed + 1).items():
        if name != "x":
            out[name + "_2"] = value
    return out


def reference(
    x, norm_g, ffn1_wg, ffn1_wu, ffn1_wd, ffn2_wg, ffn2_wu, ffn2_wd, diff_w_in, diff_w_out,
    diff_lambda, diff_subln, na_w_in, na_w_out, na_rpb, gqa_w_in, gqa_w_out, gqa_qk_norm,
    attn_norm_g_2, w_in_2, b_forget_2, b_gate_2, moba_q_norm_g_2, moba_k_norm_g_2,
    fox_q_norm_g_2, fox_k_norm_g_2, w_branch_moba_2, w_branch_fox_2, w_out_2, ffn_norm_g_2,
    w_ffn_up_2, ffn_conv_w_2, ffn_conv_b_2, w_ffn_down_2,
):
    x = first_block(
        x, norm_g, ffn1_wg, ffn1_wu, ffn1_wd, ffn2_wg, ffn2_wu, ffn2_wd, diff_w_in, diff_w_out,
        diff_lambda, diff_subln, na_w_in, na_w_out, na_rpb, gqa_w_in, gqa_w_out, gqa_qk_norm,
    )
    return second_block(
        x, attn_norm_g_2, w_in_2, b_forget_2, b_gate_2, moba_q_norm_g_2, moba_k_norm_g_2,
        fox_q_norm_g_2, fox_k_norm_g_2, w_branch_moba_2, w_branch_fox_2, w_out_2, ffn_norm_g_2,
        w_ffn_up_2, ffn_conv_w_2, ffn_conv_b_2, w_ffn_down_2,
    )


_drawn_inputs = setup_inputs


def setup_inputs(seed=0):
    import zlib

    import numpy as np

    out = dict(_drawn_inputs(seed))
    spreads = {}
    factors = {'attn_norm_g_2': 8.0,
     'b_forget_2': 8.0,
     'b_gate_2': 5.538,
     'moba_q_norm_g_2': 8.0,
     'moba_k_norm_g_2': 8.0,
     'fox_q_norm_g_2': 8.0,
     'fox_k_norm_g_2': 8.0,
     'ffn_norm_g_2': 6.829,
     'ffn_conv_b_2': 8.0}
    for name, (base, spread) in spreads.items():
        noise = np.random.default_rng([zlib.crc32(name.encode()), seed]).standard_normal(out[name].shape)
        drawn = base * np.exp(spread * noise) if base else spread * noise
        out[name] = __import__('jax').numpy.asarray(drawn.astype(out[name].dtype))
    for name, factor in factors.items():
        out[name] = (out[name] * factor).astype(out[name].dtype)
    return out
```

```python
from contextlib import ExitStack

import concourse.bass as bass
from concourse import mybir

F32 = mybir.dt.float32
F32R = mybir.dt.float32r
ALU = mybir.AluOpType
ACT = mybir.ActivationFunctionType
AX_X = mybir.AxisListType.X

P = 128
S = 256
NT = S // P
D = 1024
KT = D // P
F = 2816
FC = 256
NCH = F // FC
FT = F // P
RING = 6
DMA2 = 32
UP = KT // 2
EPS = 1e-6
LAM_INIT = 0.8 - 0.6 * 1.0
HD = 64
GW = 64
GR = S // GW
NAH = 16
MASKED = -1e30
TAPS = 3

C_ID, C_ROPE, C_WIN, C_CAUS, C_TRI, C_FLIP, C_END = 0, 128, 192, 256, 384, 896, 1024
B_ATTN, B_FFN, B_SUB, B_CONV, B_END = 0, 8, 16, 17, 17 + 4 * 22


def build(nc, x, norm_g, ffn1_wg, ffn1_wu, ffn1_wd, ffn2_wg, ffn2_wu, ffn2_wd, diff_w_in, diff_w_out,
          diff_lambda, diff_subln, na_w_in, na_w_out, na_rpb, attn_norm_g_2, w_in_2, b_forget_2,
          b_gate_2, moba_q_norm_g_2, moba_k_norm_g_2, fox_q_norm_g_2, fox_k_norm_g_2,
          w_branch_moba_2, w_branch_fox_2, w_out_2, ffn_norm_g_2, w_ffn_up_2, ffn_conv_w_2,
          ffn_conv_b_2, w_ffn_down_2, const_pack, const_sel, out, stage=99):
    ctx = ExitStack()
    with ctx:
        def sb(name, shape, dt=F32):
            return ctx.enter_context(nc.sbuf_tensor(name, shape, dt))

        def sem(name):
            return ctx.enter_context(nc.semaphore(name))

        raw = sb("raw", [P, RING, 2, 512])
        whi = sb("whi", [P, RING, 2, 512], F32R)
        wlo = sb("wlo", [P, RING, 2, 512], F32R)
        h = sb("h", [P, NT, D])
        xhi = sb("xhi", [P, KT, S], F32R)
        xlo = sb("xlo", [P, KT, S], F32R)
        thi = sb("thi", [P, 2, S], F32R)
        tlo = sb("tlo", [P, 2, S], F32R)
        qkv = sb("qkv", [P, NT, 3 * D])
        qT = sb("qT", [P, KT, S])
        kT = sb("kT", [P, KT, S])
        osb = sb("osb", [P, NT, D])
        kT1 = osb[:].rearrange("p t (k s) -> p (t k) s", s=S)
        sqa = sb("sqa", [P, D])
        aux = sb("aux", [P, 8192])
        gpost = sb("gpost", [P, D])
        ex = sb("ex", [P, 2, 2, S])
        aT = sb("aT", [P, 2, 4, P])
        cst = sb("cst", [P, C_END])
        rowsA = sqa[0:96, 0:P]
        rowsB = sqa[0:B_END, P:2 * P]
        gA = sb("gA", [P, 96])
        gB = sb("gB", [P, B_END])
        qkg = sb("qkg", [P, 4, HD])
        lamv = sb("lamv", [P, 4, HD])
        lamp = sb("lamp", [P, 2, HD])
        lam = sb("lam", [P, 8])
        nh = sb("nh", [P, 32])
        ssx = sb("ssx", [P, NT])
        rx = sb("rx", [P, NT])
        ssy = sb("ssy", [P, NT])
        ry = sb("ry", [P, NT])
        sso = sb("sso", [P, NT, 32])
        ro = sb("ro", [P, NT, 32])
        mx = sb("mx", [P, 2, 2])
        nmx = sb("nmx", [P, 2, 2])
        rs = sb("rs", [P, NT, 16])
        ri = sb("ri", [P, NT, 16])
        wf = sb("wf", [P, KT, 8])
        wfh = sb("wfh", [P, KT, 8], F32R)
        wfl = sb("wfl", [P, KT, 8], F32R)
        bfg = sb("bfg", [P, 8])
        lf = sb("lf", [P, 3, NT, 8])
        cT = sb("cT", [8, 2, S])
        cw = sb("cw", [P, 4, 2])

        ident = cst[:, C_ID:C_ID + P]
        rope = cst[:, C_ROPE:C_ROPE + 64].rearrange("p (t c) -> p t c", t=NT)
        win = cst[:, C_WIN:C_WIN + GW]
        flip = cst[:, C_FLIP:C_FLIP + P]
        caus = cst[:, C_CAUS:C_CAUS + P]
        tri = cst[:, C_TRI:C_TRI + 2 * S].rearrange("p (t c) -> p t c", t=NT)
        silu = qkv[:, 0, 0:512].rearrange("p (t c) -> p t c", t=NT)
        hs = qkv[:, 0, 512:1024].rearrange("p (t c) -> p t c", t=NT)
        ug = qkv[:, 0, 1024:2048].rearrange("p (t c) -> p t c", t=NT)
        cv0 = qkv[:, 1, 0:512].rearrange("p (f c) -> p f c", f=2)
        cv1 = qkv[:, 1, 512:1024].rearrange("p (f c) -> p f c", f=2)
        cv2 = qkv[:, 1, 1024:1536].rearrange("p (f c) -> p f c", f=2)
        cv3 = qkv[:, 1, 1536:2048].rearrange("p (f c) -> p f c", f=2)
        nab = aux[:, :].rearrange("p (t h c) -> p t h c", t=NT, h=NAH)
        gates = aux[:, 0:4096].rearrange("p (t c) -> p t c", t=NT)
        bgate = aux[:, 4096:6144]
        sel = aux[0:8, 6144:8192].rearrange("p (h c) -> p h c", h=8)
        pad = qT[0:120, :, :].rearrange("p k c -> p (k c)")[:, 0:254].rearrange("p (a c) -> p a c", a=2)

        ps = ctx.enter_context(nc.psum_tensor("ps", [P, 8, 512], F32))
        Y, Z = 0, 4

        scratch = nc.dram_tensor("rpb_scratch", (240, 127), F32, kind="Internal").ap()

        s_dma = [sem(f"unit_landed{i}") for i in range(RING)]
        s_hi = sem("hi_done")
        s_lo = sem("lo_done")
        s_used = sem("unit_used")
        s_cst = sem("consts_landed")
        s_x = sem("x_landed")
        s_rows = sem("rows_landed")
        s_nh = sem("half_exponent_set")
        s_gT = sem("gains_transposed")
        s_gev = sem("gains_ready")
        s_gp = sem("post_gain_landed")
        s_src = sem("xt_source_ready")
        s_tr = sem("xt_transposed")
        s_xh = sem("xt_hi")
        s_xl = sem("xt_lo")
        s_ssx = sem("pre_norm_sum")
        s_rx = sem("pre_norm_rstd")
        s_si = sem("silu_done")
        s_hc = sem("hidden_ready")
        s_ht = sem("hidden_transposed")
        s_hth = sem("hidden_hi")
        s_htl = sem("hidden_lo")
        s_ssy = sem("post_norm_sum")
        s_ry = sem("post_norm_rstd")
        s_qa = sem("chunk_evac_act")
        s_qv = sem("chunk_evac_dve")
        s_qr = sem("qkv_ready")
        s_qt = sem("qk_transposed")
        s_qta = sem("qT_ready")
        s_ktv = sem("kT_ready")
        s_kta = sem("kT1_ready")
        s_kz = sem("kT_rest_zero")
        s_sc = sem("scores_done")
        s_mx = sem("max_done")
        s_ex = sem("exp_done")
        s_a = sem("probs_ready")
        s_at = sem("probs_transposed")
        s_ate = sem("probsT_ready")
        s_pv = sem("pv_done")
        s_sq = sem("head_squares")
        s_ss = sem("head_sums")
        s_ro = sem("head_rstd")
        s_v = sem("dve_step")
        s_p = sem("pool_step")
        s_ac = sem("act_step")
        s_pad = sem("pad_set")
        s_rp = sem("rpb_landed")
        s_scr = sem("scratch_written")
        s_nab = sem("bias_landed")
        s_nar = sem("bias_ready")
        s_lam = sem("lambda_landed")
        s_lsum = sem("lambda_sums")
        s_lexp = sem("lambda_exp")
        s_b2 = sem("block2_small_landed")
        s_aux2 = sem("block2_aux_landed")
        s_wf = sem("forget_weights_landed")
        s_wfh = sem("forget_hi")
        s_wfl = sem("forget_lo")
        s_fz = sem("forget_logits")
        s_fe = sem("forget_act")
        s_fv = sem("forget_dve")
        s_fc = sem("forget_cumsum")
        s_g = sem("gate_logits")
        s_sg = sem("gates_ready")
        s_cw = sem("conv_taps")
        s_ug = sem("up_copied")
        s_ut = sem("up_transposed")
        s_c0 = sem("conv_tap2")
        s_c1 = sem("conv_tap1")
        s_cc = sem("conv_hidden")
        s_t1 = sem("conv_tap1_half")
        s_si2 = sem("conv_silu")
        s_out = sem("out_written")

        block = ctx.enter_context(nc.Block())

        def bank(b, t=0, w=2):
            return ps[:, b:b + w, :].rearrange("p b c -> p (b c)")

        def used(n0):
            return RING + n0 + 1

        def slot(n0):
            return n0 % RING

        def load(sp, n0, it, dsts_srcs):
            s = slot(n0)
            sp.wait_ge(s_lo, n0 + 1 + RING * it)
            for dst, src in dsts_srcs(raw[:, s]):
                sp.dma_start(dst, src).then_inc(s_dma[s], 16)

        def hi(act, n0, it=0):
            if isinstance(it, int) and n0 + RING * it >= N_UNITS:
                return
            s = slot(n0)
            act.wait_ge(s_dma[s], DMA2 * (n0 // RING + 1) + DMA2 * it)
            act.wait_ge(s_used, n0 + 1 + RING * it)
            nc.scalar.copy(whi[:, s], raw[:, s]).then_inc(s_hi, 1)

        def lo(dve, n0, it=0):
            if isinstance(it, int) and n0 + RING * it >= N_UNITS:
                return
            s = slot(n0)
            dve.wait_ge(s_hi, n0 + 1 + RING * it)
            nc.vector.tensor_tensor(wlo[:, s], raw[:, s], whi[:, s].bitcast(F32), ALU.subtract).then_inc(s_lo, 1)

        def mm3(outs, ahi, alo, s, i, start, stop):
            last = None
            for t in range(NT):
                c = slice(t * P, (t + 1) * P)
                nc.tensor.matmul(outs[t], ahi[:, c], whi[:, s, i], start=start, stop=False)
                nc.tensor.matmul(outs[t], ahi[:, c], wlo[:, s, i], start=False, stop=False)
                last = nc.tensor.matmul(outs[t], alo[:, c], whi[:, s, i], start=False, stop=stop)
            return last

        def col_unit(pe, n0, it, j, banks):
            s = slot(n0)
            pe.wait_ge(s_lo, RING + n0 + 1 + RING * it)
            for i in range(2):
                k = 2 * j + i
                last = mm3([ps[:, b] for b in banks], xhi[:, k], xlo[:, k], s, i, k == 0, k == KT - 1)
            last.then_inc(s_used, 1)
            return last

        def row_unit(pe, n0, it, ahi, alo, base, start, stop):
            s = slot(n0)
            pe.wait_ge(s_lo, RING + n0 + 1 + RING * it)
            for i in range(2):
                last = mm3([ps[:, base + i], ps[:, base + 2 + i]], ahi, alo, s, i, start, stop)
            last.then_inc(s_used, 1)

        def xt_pe(pe, r, src, whole=False):
            for t in range(NT):
                if r:
                    pe.wait_ge(s_src, 2 * (r - 1) + (NT if whole else t + 1))
                for k in range(KT):
                    ins = nc.tensor.transpose(ps[:, Z + k // 2, (k % 2) * S + t * P:(k % 2) * S + (t + 1) * P],
                                              src[:, t, k * P:(k + 1) * P], ident)
                    if t == NT - 1 and k % 2 == 1:
                        ins.then_inc(s_tr, 1)

        def xt_act(act, r, gain):
            for b in range(4):
                act.wait_ge(s_tr, 4 * r + b + 1)
                if gain is None:
                    ins = nc.scalar.copy(xhi[:, 2 * b:2 * b + 2, :].rearrange("p k c -> p (k c)"), ps[:, Z + b])
                else:
                    for i in range(2):
                        ins = nc.scalar.activation(xhi[:, 2 * b + i], ps[:, Z + b, i * S:(i + 1) * S], ACT.Copy,
                                                   scale=gain(2 * b + i))
                ins.then_inc(s_xh, 1)

        def xt_dve(dve, r, gain):
            for b in range(4):
                dve.wait_ge(s_xh, 4 * r + b + 1)
                if gain is None:
                    ins = nc.vector.tensor_tensor(xlo[:, 2 * b:2 * b + 2, :].rearrange("p k c -> p (k c)"), ps[:, Z + b],
                                                  xhi[:, 2 * b:2 * b + 2, :].rearrange("p k c -> p (k c)").bitcast(F32),
                                                  ALU.subtract)
                else:
                    for i in range(2):
                        ins = nc.vector.scalar_tensor_tensor(
                            out=xlo[:, 2 * b + i], in0=ps[:, Z + b, i * S:(i + 1) * S], scalar=gain(2 * b + i),
                            in1=xhi[:, 2 * b + i].bitcast(F32), op0=ALU.mult, op1=ALU.subtract)
                ins.then_inc(s_xl, 1)

        def gainA(layer, j):
            return lambda k: gA[:, (layer * 6 + j) * KT + k:(layer * 6 + j) * KT + k + 1]

        def gainB(c0):
            return lambda k: gB[:, c0 + k:c0 + k + 1]

        def gain_sub(k):
            return gB[:, B_SUB:B_SUB + 1]

        def pre_act(act, r):
            for t in range(NT):
                nc.scalar.activation(sqa[:], h[:, t], ACT.Square, accum_out=ssx[:, t:t + 1]).then_inc(s_ssx, 1)
                act.wait_ge(s_ssx, 2 * r + t + 1)

        class Steps:
            def __init__(self, eng, s):
                self.eng, self.s, self.n = eng, s, 0

            def done(self, ins):
                ins.then_inc(self.s, 1)
                self.n += 1
                self.eng.wait_ge(self.s, self.n)

        def rstd(steps, out_, ss, n, factor=1.0):
            g = 1.0 / (factor * factor)
            w = out_.shape[-1]
            steps.done(nc.gpsimd.tensor_scalar(out_, ss, g / n, EPS * g, ALU.mult, ALU.add))
            return nc.gpsimd.tensor_tensor(out_, out_, nh[:, 0:w], ALU.pow)

        def pre_pool(pool, steps, r):
            pool.wait_ge(s_ssx, 2 * r + 2)
            rstd(steps, rx[:], ssx[:], D).then_inc(s_rx, 1)

        def post_act(act, q, ydone):
            act.wait_ge(s_used, used(ydone))
            for t in range(NT):
                nc.scalar.activation(sqa[:], bank(Y + 2 * t), ACT.Square, accum_out=ssy[:, t:t + 1]).then_inc(s_ssy, 1)
                act.wait_ge(s_ssy, 2 * q + t + 1)

        def zero_pool(pool, m, r):
            pool.wait_ge(s_rx, r + 1)
            nc.gpsimd.memset(kT[HD:P], 0.0).then_inc(s_kz, 1)
            pool.wait_ge(s_kz, 2 * m + 1)
            nc.gpsimd.memset(kT1[0:HD], 0.0).then_inc(s_kz, 1)
            pool.wait_ge(s_kz, 2 * m + 2)

        def post_pool(pool, steps, q, factor):
            for t in range(NT):
                pool.wait_ge(s_ssy, 2 * q + t + 1)
                rstd(steps, ry[:, t:t + 1], ssy[:, t:t + 1], D, factor).then_inc(s_ry, 1)

        def post_dve(dve, steps, q):
            dve.wait_ge(s_gp, 16 * (q + 1))
            for t in range(NT):
                dve.wait_ge(s_ry, 2 * q + t + 1)
                steps.done(nc.vector.scalar_tensor_tensor(out=osb[:, t], in0=bank(Y + 2 * t), scalar=ry[:, t:t + 1],
                                                          in1=gpost[:], op0=ALU.mult, op1=ALU.mult))
                nc.vector.tensor_tensor(h[:, t], h[:, t], osb[:, t], ALU.add).then_inc(s_src, 1)

        def chunks(eng, n0, body):
            more = n0 + 66 < N_UNITS
            with eng.Fori(0, NCH - 1 if more else NCH - 2) as it:
                body(it)
            if not more:
                body(NCH - 2)

        def gu_unit(sp, n0, it, j, c, wg, wu):
            def parts(dst):
                return [(dst[:, :, 0:FC], wg.rearrange("(k p) f -> p k f", p=P)[:, 2 * j:2 * j + 2, bass.ds(c * FC, FC)]),
                        (dst[:, :, FC:2 * FC], wu.rearrange("(k p) f -> p k f", p=P)[:, 2 * j:2 * j + 2, bass.ds(c * FC, FC)])]
            load(sp, n0, it, parts)

        def down_unit(sp, n0, it, w, row):
            def parts(dst):
                return [(dst[:, i], w[bass.ds(row, P), i * 512:(i + 1) * 512]) for i in range(2)]
            load(sp, n0, it, parts)

        def ffn_sp(sp, n0, wg, wu, wd, gain=None):
            for j in range(UP):
                gu_unit(sp, n0 + j, 0, j, 0, wg, wu)
            with sp.Fori(0, NCH - 1) as it:
                for j in range(UP):
                    gu_unit(sp, n0 + 4 + j, it, j, it + 1, wg, wu)
                for j in range(2):
                    down_unit(sp, n0 + 8 + j, it, wd, it * FC + j * P)
            if gain is not None:
                post_gain(sp, gain)
            for j in range(2):
                down_unit(sp, n0 + 64 + j, 0, wd, (NCH - 1) * FC + j * P)

        def gate_up(pe, n0, it):
            for j in range(UP):
                last = col_unit(pe, n0 + j, it, j, [Z, Z + 1])
            return last

        def down(pe, n0, it, start, stop):
            for j in range(2):
                row_unit(pe, n0 + j, it, thi[:, j], tlo[:, j], Y, start and j == 0, stop and j == 1)

        def ffn_pe(pe, f, n0, r):
            b = NCH * f
            pe.wait_ge(s_xl, 4 * r + 4)

            def hidden_t(c):
                pe.wait_ge(s_hc, 2 * b + 2 * c + 2)
                for j in range(2):
                    for t in range(NT):
                        ins = nc.tensor.transpose(ps[:, Z + 2, j * S + t * P:j * S + (t + 1) * P],
                                                  hs[:, t, j * P:(j + 1) * P], ident)
                ins.then_inc(s_ht, 1)

            gate_up(pe, n0, 0)
            hidden_t(0)

            def body(it, start):
                gate_up(pe, n0 + 4, it)
                pe.wait_ge(s_htl, b + it + 1)
                down(pe, n0 + 8, it, start, False)
                hidden_t(it + 1)
            body(0, True)
            with pe.Fori(1, NCH - 1) as it:
                body(it, False)
            pe.wait_ge(s_htl, b + NCH)
            down(pe, n0 + 64, 0, False, True)

        def ffn_act(act, f, n0, r):
            b = NCH * f

            def swish(last):
                act.wait_ge(s_used, used(last))
                for t in range(NT):
                    nc.scalar.activation(silu[:, t], ps[:, Z + t, 0:FC], ACT.Silu, scale=rx[:, t:t + 1]).then_inc(s_si, 1)

            def hidden(c):
                act.wait_ge(s_ht, b + c + 1)
                nc.scalar.copy(thi[:, :, :].rearrange("p f c -> p (f c)"), ps[:, Z + 2]).then_inc(s_hth, 1)
            for j in range(3):
                hi(act, n0 + RING + j)
            act.wait_ge(s_rx, r + 1)
            swish(n0 + 3)
            hi(act, n0 + RING + 3)
            hidden(0)

            def body(it):
                for j in range(3):
                    hi(act, n0 + RING + 4 + j, it)
                swish(n0 + 7 + RING * it)
                for j in range(3, 6):
                    hi(act, n0 + RING + 4 + j, it)
                hidden(it + 1)
            chunks(act, n0, body)
            for j in range(2):
                hi(act, n0 + RING + 64 + j)

        def ffn_dve(dve, f, n0):
            b = NCH * f

            def gated(c):
                for t in range(NT):
                    dve.wait_ge(s_si, 2 * b + 2 * c + t + 1)
                    nc.vector.scalar_tensor_tensor(out=hs[:, t], in0=ps[:, Z + t, FC:2 * FC], scalar=rx[:, t:t + 1],
                                                   in1=silu[:, t], op0=ALU.mult, op1=ALU.mult).then_inc(s_hc, 1)

            def hidden(c):
                dve.wait_ge(s_hth, b + c + 1)
                nc.vector.tensor_tensor(tlo[:, :, :].rearrange("p f c -> p (f c)"), ps[:, Z + 2],
                                        thi[:, :, :].rearrange("p f c -> p (f c)").bitcast(F32), ALU.subtract).then_inc(s_htl, 1)
            for j in range(3):
                lo(dve, n0 + RING + j)
            gated(0)
            lo(dve, n0 + RING + 3)
            hidden(0)

            def body(it):
                for j in range(3):
                    lo(dve, n0 + RING + 4 + j, it)
                gated(it + 1)
                for j in range(3, 6):
                    lo(dve, n0 + RING + 4 + j, it)
                hidden(it + 1)
            chunks(dve, n0, body)
            for j in range(2):
                lo(dve, n0 + RING + 64 + j)

        def chunk_sp(sp, n0, w, cols):
            for c, c0 in enumerate(cols):
                for j in range(UP):
                    load(sp, n0 + UP * c + j, 0, lambda dst: [
                        (dst[:, i], w[(2 * j + i) * P:(2 * j + i + 1) * P, c0:c0 + 512]) for i in range(2)])

        def row_sp(sp, n0, w, rows):
            for j in range(rows // P):
                down_unit(sp, n0 + j, 0, w, j * P)

        def qkv_pe(pe, m, n0, r, nch=6):
            pe.wait_ge(s_xl, 4 * r + 4)
            for c in range(6):
                g = 6 * m + c
                if c >= 2:
                    pe.wait_ge(s_qa, g - 1)
                    pe.wait_ge(s_qv, g - 1)
                for j in range(UP):
                    col_unit(pe, n0 + UP * c + j, 0, j, [Z + 2 * (c % 2), Z + 2 * (c % 2) + 1])

        def qkv_act(act, m, n0, r):
            for c in range(6):
                for j in range(UP):
                    hi(act, n0 + RING + UP * c + j)
                act.wait_ge(s_used, used(n0 + UP * c + 3))
                if c == 0:
                    act.wait_ge(s_rx, r + 1)
                nc.scalar.activation(qkv[:, 0, c * 512:(c + 1) * 512], ps[:, Z + 2 * (c % 2)], ACT.Copy,
                                     scale=rx[:, 0:1]).then_inc(s_qa, 1)

        def qkv_dve(dve, m, n0, r):
            for c in range(6):
                for j in range(UP):
                    lo(dve, n0 + RING + UP * c + j)
                dve.wait_ge(s_used, used(n0 + UP * c + 3))
                if c == 0:
                    dve.wait_ge(s_rx, r + 1)
                nc.vector.tensor_scalar(qkv[:, 1, c * 512:(c + 1) * 512], ps[:, Z + 2 * (c % 2) + 1], rx[:, 1:2],
                                        None, ALU.mult).then_inc(s_qv, 1)

        def proj_pe(pe, n0, r, kts, base, first=0):
            pe.wait_ge(s_xl, 4 * r + 4)
            for j in range(kts):
                row_unit(pe, n0 + j, 0, xhi[:, first + j], xlo[:, first + j], base, j == 0, j == kts - 1)

        TASKS = [(p, t) for p in range(8) for t in range(NT)]
        NTASK = len(TASKS)

        def qk_cols(kind, p):
            if kind == "b2":
                b = 0 if p < 4 else 3 * 512
                return b + (p % 4) * P, b + 512 + (p % 4) * P, b + 1024 + (p % 4) * P
            return p * P, D + p * P, 2 * D + p * P

        def keys(kind, t):
            return t + 1 if kind == "b2" else NT

        def attn_pe(pe, m, kind):
            b = NTASK * m
            pe.wait_ge(s_qa, 6 * m + 6)
            pe.wait_ge(s_qv, 6 * m + 6)
            if kind != "na":
                pe.wait_ge(s_qr, 1 if kind == "diff" else 2)
            for which in range(2):
                for bk in range(4):
                    for p in (2 * bk, 2 * bk + 1):
                        c0 = qk_cols(kind, p)[which]
                        for t in range(NT):
                            ins = nc.tensor.transpose(
                                ps[:, 4 * which + bk, (p % 2) * S + t * P:(p % 2) * S + (t + 1) * P],
                                qkv[:, t, c0:c0 + P], ident)
                    ins.then_inc(s_qt, 1)
            pe.wait_ge(s_qta, 4 * (m + 1))
            pe.wait_ge(s_ktv, 4 * (m + 1))
            pe.wait_ge(s_kta, 4 * (m + 1))
            pe.wait_ge(s_kz, 2 * (m + 1))
            if kind == "na":
                pe.wait_ge(s_nar, 2)
            if kind == "b2":
                pe.wait_ge(s_fc, 3)

            def scores(i):
                p, t = TASKS[i]
                if i >= 2:
                    pe.wait_ge(s_ex, 2 * (b + i - 1))
                w = keys(kind, t) * P
                for c in range(2):
                    o = ps[:, Z + i % 2, c * S:c * S + w]
                    plain = kind == "diff" or (kind == "b2" and p < 4)
                    ins = nc.tensor.matmul(o, qT[:, p, t * P:(t + 1) * P], (kT, kT1)[c][:, p, 0:w], start=True, stop=plain)
                    if kind == "na":
                        ins = nc.tensor.matmul(o, flip, nab[:, t, 2 * p + c, :], start=False, stop=True)
                    if kind == "b2":
                        if p >= 4:
                            hh = 2 * (p - 4) + c
                            nc.tensor.matmul(o, cT[:, 0, t * P:(t + 1) * P], sel[:, hh, 0:w], start=False, stop=False)
                            nc.tensor.matmul(o, sel[:, hh, 0:P], cT[:, 1, 0:w], start=False, stop=True)
                        ins = nc.tensor.matmul(ps[:, Z + i % 2, c * S + t * P:c * S + (t + 1) * P], ident, caus,
                                               start=False, stop=True, skip_group_check=True)
                ins.then_inc(s_sc, 1)

            def turn(i):
                p, t = TASKS[i]
                if kind == "diff":
                    pe.wait_ge(s_a, b + i + 1)
                else:
                    pe.wait_ge(s_ex, 2 * (b + i + 1))
                if i >= 2:
                    pe.wait_ge(s_ate, b + i - 1)
                for c in range(1 if kind == "diff" else 2):
                    for st in range(keys(kind, t)):
                        ins = nc.tensor.transpose(ps[:, Z + 2 + i % 2, (2 * c + st) * P:(2 * c + st + 1) * P],
                                                  ex[:, i % 2, c, st * P:(st + 1) * P], ident)
                ins.then_inc(s_at, 1)

            def pv(i):
                p, t = TASKS[i]
                pe.wait_ge(s_ate, b + i + 1)
                v0 = qk_cols(kind, p)[2]
                n, w = (1, P) if kind == "diff" else (2, HD)
                for c in range(n):
                    for st in range(keys(kind, t)):
                        ins = nc.tensor.matmul(ps[:, Y + 2 * t + p // 4, (p % 4) * P + c * w:(p % 4) * P + (c + 1) * w],
                                               aT[:, i % 2, 2 * c + st], qkv[:, st, v0 + c * w:v0 + (c + 1) * w],
                                               start=st == 0, stop=st == keys(kind, t) - 1)
                ins.then_inc(s_pv, 1)

            for i in range(NTASK + 2):
                if i < NTASK:
                    scores(i)
                if 1 <= i <= NTASK:
                    turn(i - 1)
                if i >= 2:
                    pv(i - 2)

        def attn_act(act, m, kind):
            b = NTASK * m
            if m == 0 and stage >= 5:
                act.wait_ge(s_scr, 16)
            for bk in range(4):
                act.wait_ge(s_qt, 8 * m + bk + 1)
                nc.scalar.activation(qT[:, 2 * bk:2 * bk + 2, :].rearrange("p k c -> p (k c)"), ps[:, Y + bk],
                                     ACT.Copy, scale=HD ** -0.5).then_inc(s_qta, 1)
            for bk in range(4):
                act.wait_ge(s_qt, 8 * m + 4 + bk + 1)
                nc.scalar.copy(kT1[HD:P, 2 * bk:2 * bk + 2, :].rearrange("p k c -> p (k c)"),
                               ps[HD:P, Z + bk]).then_inc(s_kta, 1)
            for i in range(NTASK + 1):
                if i < NTASK:
                    p, t = TASKS[i]
                    w = keys(kind, t) * P
                    act.wait_ge(s_mx, b + i + 1)
                    if i >= 2:
                        if kind == "diff":
                            act.wait_ge(s_a, b + i - 1)
                        act.wait_ge(s_at, b + i - 1)
                    for c in range(2):
                        nc.scalar.activation(ex[:, i % 2, c, 0:w], ps[:, Z + i % 2, c * S:c * S + w], ACT.Exp,
                                             bias=nmx[:, i % 2, c:c + 1],
                                             accum_out=rs[:, t, 2 * p + c:2 * p + c + 1]).then_inc(s_ex, 1)
                if i >= 1:
                    j = i - 1
                    act.wait_ge(s_at, b + j + 1)
                    if j >= 2:
                        act.wait_ge(s_pv, b + j - 1)
                    n = 1 if kind == "diff" else 2
                    k = keys(kind, TASKS[j][1])
                    src = ps[:, Z + 2 + j % 2].rearrange("p (c s q) -> p c s q", c=2, s=2)
                    dst = aT[:, j % 2].rearrange("p (c s) q -> p c s q", c=2)
                    nc.scalar.copy(dst[:, 0:n, 0:k], src[:, 0:n, 0:k]).then_inc(s_ate, 1)

        def attn_dve(dve, steps, m, kind):
            b = NTASK * m
            for bk in range(4):
                dve.wait_ge(s_qt, 8 * m + 4 + bk + 1)
                nc.vector.tensor_copy(kT[0:HD, 2 * bk:2 * bk + 2, :].rearrange("p k c -> p (k c)"),
                                      ps[0:HD, Z + bk]).then_inc(s_ktv, 1)
            for i in range(NTASK + 1):
                if i < NTASK:
                    p, t = TASKS[i]
                    w = keys(kind, t) * P
                    dve.wait_ge(s_sc, b + i + 1)
                    if i >= 2:
                        dve.wait_ge(s_ex, 2 * (b + i - 1))
                    sc = ps[:, Z + i % 2].rearrange("p (c k) -> p c k", c=2)[:, :, 0:w]
                    steps.done(nc.vector.tensor_reduce(mx[:, i % 2], sc, AX_X, ALU.max))
                    nc.vector.tensor_scalar(nmx[:, i % 2], mx[:, i % 2], -1.0, None, ALU.mult).then_inc(s_mx, 1)
                if i >= 1 and kind == "diff":
                    j = i - 1
                    p, t = TASKS[j]
                    dve.wait_ge(s_ex, 2 * (b + j + 1))
                    r2 = ri[:, t, 2 * p:2 * p + 2]
                    steps.done(nc.vector.reciprocal(r2, rs[:, t, 2 * p:2 * p + 2]))
                    steps.done(nc.vector.tensor_scalar(ex[:, j % 2, 1], ex[:, j % 2, 1], ri[:, t, 2 * p + 1:2 * p + 2],
                                                       lam[:, 4:5], ALU.mult, ALU.mult))
                    nc.vector.scalar_tensor_tensor(out=ex[:, j % 2, 0], in0=ex[:, j % 2, 0],
                                                   scalar=ri[:, t, 2 * p:2 * p + 1], in1=ex[:, j % 2, 1],
                                                   op0=ALU.mult, op1=ALU.subtract).then_inc(s_a, 1)
            dve.wait_ge(s_pv, b + NTASK)
            if kind == "diff":
                for t in range(NT):
                    dve.wait_ge(s_sq, t + 1)
                    nc.vector.tensor_reduce(sso[:, t, 0:8], sqa[:].rearrange("p (g c) -> p g c", c=P), AX_X,
                                            ALU.add).then_inc(s_ss, 1)
                for t in range(NT):
                    dve.wait_ge(s_ro, t + 1)
                    nc.vector.tensor_tensor(osb[:, t].rearrange("p (g c) -> p g c", c=P),
                                            bank(Y + 2 * t).rearrange("p (g c) -> p g c", c=P),
                                            ro[:, t, 0:8].unsqueeze(2).broadcast_to([P, 8, P]),
                                            ALU.mult).then_inc(s_src, 1)
            else:
                dve.wait_ge(s_ex, 2 * (b + NTASK))
                steps.done(nc.vector.reciprocal(ri[:], rs[:]))
                for t in range(NT):
                    nc.vector.tensor_tensor(osb[:, t].rearrange("p (g c) -> p g c", c=HD),
                                            bank(Y + 2 * t).rearrange("p (g c) -> p g c", c=HD),
                                            ri[:, t].unsqueeze(2).broadcast_to([P, 16, HD]),
                                            ALU.mult).then_inc(s_src, 1)

        def rope_dve(dve, steps, c0, groups):
            tmp = [qT[:, 0:4, :].rearrange("p k c -> p (k c)")[:, 0:groups * 16].rearrange("p (g c) -> p g c", c=16),
                   qT[:, 4:8, :].rearrange("p k c -> p (k c)")[:, 0:groups * 16].rearrange("p (g c) -> p g c", c=16)]
            for t in range(NT):
                v = qkv[:, t, c0:c0 + groups * HD].rearrange("p (g c) -> p g c", c=HD)
                cos = rope[:, t, 0:16].unsqueeze(1).broadcast_to([P, groups, 16])
                nsin = rope[:, t, 16:24].unsqueeze(1).broadcast_to([P, groups, 8])
                psin = rope[:, t, 24:32].unsqueeze(1).broadcast_to([P, groups, 8])
                steps.done(nc.vector.tensor_tensor(tmp[0], v[:, :, 0:16], cos, ALU.mult))
                steps.done(nc.vector.tensor_tensor(tmp[1][:, :, 0:8], v[:, :, 8:16], nsin, ALU.mult))
                steps.done(nc.vector.tensor_tensor(tmp[1][:, :, 8:16], v[:, :, 0:8], psin, ALU.mult))
                last = nc.vector.tensor_tensor(v[:, :, 0:16], tmp[0], tmp[1], ALU.add)
                if t == 0:
                    steps.done(last)
            last.then_inc(s_qr, 1)

        def conv_ffn_pe(pe):
            b, n0 = NCH * 4, n["f4"]
            pe.wait_ge(s_xl, 4 * 11 + 4)

            def turn(c):
                pe.wait_ge(s_ug, 2 * c + 2)
                for g in range(2):
                    for j in range(2):
                        for t in range(NT):
                            ins = nc.tensor.transpose(ps[:, Z + 2 + g, j * S + t * P:j * S + (t + 1) * P],
                                                      ug[:, t, g * FC + j * P:g * FC + (j + 1) * P], ident)
                ins.then_inc(s_ut, 1)

            gate_up(pe, n0, 0)
            turn(0)

            def body(it, start):
                gate_up(pe, n0 + 4, it)
                pe.wait_ge(s_htl, b + it + 1)
                down(pe, n0 + 8, it, start, False)
                turn(it + 1)
            body(0, True)
            with pe.Fori(1, NCH - 1) as it:
                body(it, False)
            pe.wait_ge(s_htl, b + NCH)
            down(pe, n0 + 64, 0, False, True)

        def conv_ffn_act(act):
            b, n0 = NCH * 4, n["f4"]

            def copy_up(last):
                act.wait_ge(s_used, used(last))
                for t in range(NT):
                    nc.scalar.activation(ug[:, t], ps[:, Z + t], ACT.Copy, scale=rx[:, t:t + 1]).then_inc(s_ug, 1)

            def conv(c):
                act.wait_ge(s_ut, c + 1)
                act.wait_ge(s_cw, c + 1)
                for j in range(2):
                    nc.scalar.activation(cv0[:, j], ps[:, Z + 3, j * S:(j + 1) * S], ACT.Identity,
                                         scale=cw[:, 2, j:j + 1], bias=cw[:, 3, j:j + 1]).then_inc(s_c0, 1)
                act.wait_ge(s_c1, c + 1)
                nc.scalar.activation(cv1, cv0, ACT.Silu).then_inc(s_si2, 1)
                act.wait_ge(s_cc, c + 1)
                nc.scalar.copy(thi[:], cv2).then_inc(s_hth, 1)

            act.wait_ge(s_rx, 8)
            for j in range(3):
                hi(act, n0 + RING + j)
            copy_up(n0 + 3)
            hi(act, n0 + RING + 3)
            conv(0)

            def body(it):
                for j in range(3):
                    hi(act, n0 + RING + 4 + j, it)
                copy_up(n0 + 7 + RING * it)
                for j in range(3, 6):
                    hi(act, n0 + RING + 4 + j, it)
                conv(it + 1)
            chunks(act, n0, body)

        def conv_ffn_dve(dve, steps):
            b, n0 = NCH * 4, n["f4"]
            taps = gB[:, B_CONV:B_END].rearrange("p (k f) -> p k f", k=TAPS + 1)

            def conv(c):
                nc.vector.tensor_copy(cw[:], taps[:, :, bass.ds(2 * c, 2)]).then_inc(s_cw, 1)
                dve.wait_ge(s_cw, c + 1)
                dve.wait_ge(s_c0, 2 * c + 2)
                for j in range(2):
                    nc.vector.scalar_tensor_tensor(out=cv0[:, j, 1:S], in0=ps[:, Z + 3, j * S:(j + 1) * S - 1],
                                                   scalar=cw[:, 1, j:j + 1], in1=cv0[:, j, 1:S],
                                                   op0=ALU.mult, op1=ALU.add).then_inc(s_t1, 1)
                for j in range(2):
                    dve.wait_ge(s_t1, 2 * c + 1 + j)
                    ins = nc.vector.scalar_tensor_tensor(out=cv0[:, j, 2:S], in0=ps[:, Z + 3, j * S:(j + 1) * S - 2],
                                                         scalar=cw[:, 0, j:j + 1], in1=cv0[:, j, 2:S],
                                                         op0=ALU.mult, op1=ALU.add)
                ins.then_inc(s_c1, 1)
                dve.wait_ge(s_si2, c + 1)
                nc.vector.tensor_tensor(cv2, cv1, ps[:, Z + 2].rearrange("p (f c) -> p f c", f=2), ALU.mult).then_inc(s_cc, 1)
                dve.wait_ge(s_hth, b + c + 1)
                nc.vector.tensor_tensor(tlo[:], cv2, thi[:].bitcast(F32), ALU.subtract).then_inc(s_htl, 1)

            for j in range(4):
                lo(dve, n0 + RING + j)
            conv(0)

            def body(it):
                for j in range(6):
                    lo(dve, n0 + RING + 4 + j, it)
                conv(it + 1)
            chunks(dve, n0, body)
            dve.wait_ge(s_used, used(n0 + 65))
            for t in range(NT):
                nc.vector.tensor_tensor(h[:, t], h[:, t], bank(Y + 2 * t), ALU.add).then_inc(s_src, 1)

        n = {}
        at = 0
        for name, count in (("f0", 66), ("qkv0", 24), ("out0", 8), ("f1", 66), ("f2", 66), ("qkv1", 24), ("out1", 8),
                            ("f3", 66), ("qkv2", 24), ("gates", 16), ("bra", 4), ("brb", 4), ("out2", 8), ("f4", 66)):
            n[name] = at
            at += count
        ends = {1: 66, 2: 98, 3: 164, 4: 230, 5: 262, 6: 328, 7: 384, 8: 450}
        N_UNITS = ends.get(stage, 450)
        ffn_w = [(ffn1_wg[0], ffn1_wu[0], ffn1_wd[0]), (ffn2_wg[0], ffn2_wu[0], ffn2_wd[0]),
                 (ffn1_wg[1], ffn1_wu[1], ffn1_wd[1]), (ffn2_wg[1], ffn2_wu[1], ffn2_wd[1])]
        POST = [(0, 1), (0, 3), (0, 5), (1, 1), (1, 3), (1, 5)]
        POST_SRC = [2 * r for r in (1, 3, 4, 5, 7, 8)]
        FINAL_SRC = {1: 2, 2: 6, 3: 8, 4: 10, 5: 14, 6: 16, 7: 22}.get(stage, 24)

        def post_gain(sp, q):
            if q >= 1:
                sp.wait_ge(s_src, POST_SRC[q - 1])
            i, j = POST[q]
            sp.dma_start(gpost[:], norm_g[i, j:j + 1, :].broadcast_to([P, D])).then_inc(s_gp, 16)

        @block.sync
        def _(sp):
            sp.dma_start(cst[:], const_pack).then_inc(s_cst, 16)
            for t in range(NT):
                sp.dma_start(h[:, t], x[0, t * P:(t + 1) * P, :]).then_inc(s_x, 16)
            sp.dma_start(rowsA, norm_g.rearrange("i j (k c) -> (i j k) c", c=P)).then_inc(s_rows, 16)
            sp.dma_start(rowsB[B_ATTN:B_ATTN + 8], attn_norm_g_2.rearrange("a (k c) -> (a k) c", c=P)).then_inc(s_rows, 16)
            sp.dma_start(rowsB[B_FFN:B_FFN + 8], ffn_norm_g_2.rearrange("a (k c) -> (a k) c", c=P)).then_inc(s_rows, 16)
            sp.dma_start(rowsB[B_SUB:B_SUB + 1], diff_subln).then_inc(s_rows, 16)
            sp.dma_start(rowsB[B_CONV:B_CONV + 66], ffn_conv_w_2.rearrange("a j (k c) -> (a j k) c", c=P)).then_inc(s_rows, 16)
            sp.dma_start(rowsB[B_CONV + 66:B_CONV + 88], ffn_conv_b_2.rearrange("a (k c) -> (a k) c", c=P)).then_inc(s_rows, 16)

            ffn_sp(sp, n["f0"], *ffn_w[0], 0)
            if stage >= 2:
                chunk_sp(sp, n["qkv0"], diff_w_in[0], [512 * c for c in range(6)])
                post_gain(sp, 1)
                row_sp(sp, n["out0"], diff_w_out[0], D)
            if stage >= 3:
                ffn_sp(sp, n["f1"], *ffn_w[1], 2)
            if stage >= 4:
                ffn_sp(sp, n["f2"], *ffn_w[2], 3)
            if stage >= 5:
                chunk_sp(sp, n["qkv1"], na_w_in[0], [512 * c for c in range(6)])
                post_gain(sp, 4)
                row_sp(sp, n["out1"], na_w_out[0], D)
            if stage >= 6:
                ffn_sp(sp, n["f3"], *ffn_w[3], 5)
            if stage >= 7:
                chunk_sp(sp, n["qkv2"], w_in_2[0], [512 * c for c in range(6)])
                chunk_sp(sp, n["gates"], w_in_2[0], [3080 + 512 * c for c in range(4)])
                row_sp(sp, n["bra"], w_branch_moba_2[0], 512)
                row_sp(sp, n["brb"], w_branch_fox_2[0], 512)
                row_sp(sp, n["out2"], w_out_2[0], D)
            if stage >= 8:
                up = w_ffn_up_2[0]
                ffn_sp(sp, n["f4"], up[:, 0:F], up[:, F:2 * F], w_ffn_down_2[0])
            for t in range(NT):
                sp.wait_ge(s_src, FINAL_SRC - 1 + t)
                sp.dma_start(out[0, t * P:(t + 1) * P, :], h[:, t]).then_inc(s_out, 16)
            sp.wait_ge(s_out, 32)

        @block.gpsimd
        def _(pool):
            steps = Steps(pool, s_p)
            nc.gpsimd.memset(nh[:], -0.5).then_inc(s_nh, 1)
            pool.wait_ge(s_nh, 1)
            pre_pool(pool, steps, 0)
            if stage >= 5:
                nc.gpsimd.memset(pad, MASKED).then_inc(s_pad, 1)
                pool.wait_ge(s_pad, 1)
                pool.dma_start(pad[:, :, 48:79], na_rpb[0].rearrange("h d c -> (h d) c").rearrange("(p a) c -> p a c", a=2)).then_inc(s_rp, 16)
                pool.wait_ge(s_rp, 16)
                pool.dma_start(scratch.rearrange("(p a) c -> p a c", a=2), pad).then_inc(s_scr, 16)
                pool.wait_ge(s_scr, 16)
                for r in range(GR):
                    t, half = r // 2, r % 2
                    for kr in range(GR):
                        src = bass.AP(scratch.tensor, (7 - r + kr) * 127, [[1, GW], [15 * 127, NAH], [1, GW]])
                        dst = nab[half * GW:(half + 1) * GW, t, :, kr * GW:(kr + 1) * GW]
                        pool.dma_start(dst, src).then_inc(s_nab, 16)
            if stage >= 2:
                pool.dma_start(lamv[:].rearrange("p a c -> p (a c)"), diff_lambda.rearrange("a b c -> a (b c)").broadcast_to([P, 4 * HD])).then_inc(s_lam, 16)
            if stage >= 7:
                for i, g in enumerate((moba_q_norm_g_2, moba_k_norm_g_2, fox_q_norm_g_2, fox_k_norm_g_2)):
                    pool.dma_start(qkg[:, i], g.broadcast_to([P, HD])).then_inc(s_b2, 16)
                pool.dma_start(bfg[:], b_forget_2.broadcast_to([P, 8])).then_inc(s_b2, 16)
                pool.dma_start(wf[:], w_in_2[0, :, 3072:3080].rearrange("(k p) c -> p k c", p=P)).then_inc(s_wf, 16)
            post_pool(pool, steps, 0, 0.5)
            if stage >= 2:
                pre_pool(pool, steps, 1)
                zero_pool(pool, 0, 1)
                for t in range(NT):
                    pool.wait_ge(s_ss, t + 1)
                    rstd(steps, ro[:, t, 0:8], sso[:, t, 0:8], P).then_inc(s_ro, 1)
                post_pool(pool, steps, 1, 1.0)
            if stage >= 3:
                pre_pool(pool, steps, 2)
                post_pool(pool, steps, 2, 0.5)
            if stage >= 4:
                pre_pool(pool, steps, 3)
                post_pool(pool, steps, 3, 0.5)
            if stage >= 5:
                pre_pool(pool, steps, 4)
                zero_pool(pool, 1, 4)
                pool.wait_ge(s_nab, 16 * GR * GR)
                for t in range(NT):
                    v = nab[:, t].rearrange("p h (r c) -> p (h r) c", r=GR)
                    nc.gpsimd.tensor_tensor(v, v, win.unsqueeze(1).broadcast_to([P, NAH * GR, GW]), ALU.add).then_inc(s_nar, 1)
                post_pool(pool, steps, 4, 1.0)
            if stage >= 6:
                pre_pool(pool, steps, 5)
                post_pool(pool, steps, 5, 0.5)
            if stage >= 7:
                pool.dma_start(bgate, b_gate_2.rearrange("a b c -> a (b c)").broadcast_to([P, 2 * D])).then_inc(s_aux2, 16)
                pool.dma_start(sel, const_sel.rearrange("p (h c) -> p h c", h=8)).then_inc(s_aux2, 16)
                pre_pool(pool, steps, 6)
                zero_pool(pool, 2, 6)
                for t in range(NT):
                    pool.wait_ge(s_ss, 2 + 2 * (t + 1))
                    rstd(steps, ro[:, t], sso[:, t], HD).then_inc(s_ro, 1)
            if stage >= 8:
                pre_pool(pool, steps, 7)

        @block.scalar
        def _(act):
            for i in range(RING):
                act.wait_ge(s_dma[i], DMA2)
                nc.scalar.copy(whi[:, i], raw[:, i]).then_inc(s_hi, 1)
            act.wait_ge(s_gT, 2)
            nc.scalar.copy(gA[:], ps[:, Y, 0:96]).then_inc(s_gev, 1)
            nc.scalar.copy(gB[:], ps[:, Y, 128:128 + B_END]).then_inc(s_gev, 1)
            act.wait_ge(s_gev, 2)
            act.wait_ge(s_x, 32)
            xt_act(act, 0, gainA(0, 0))
            pre_act(act, 0)
            ffn_act(act, 0, n["f0"], 0)
            post_act(act, 0, n["f0"] + 65)
            if stage >= 2:
                xt_act(act, 1, gainA(0, 2))
                pre_act(act, 1)
                act.wait_ge(s_lsum, 1)
                nc.scalar.activation(lam[:, 2:4], lam[:, 0:2], ACT.Exp).then_inc(s_lexp, 1)
                qkv_act(act, 0, n["qkv0"], 1)
                attn_act(act, 0, "diff")
                act.wait_ge(s_pv, NTASK)
                for t in range(NT):
                    if t:
                        act.wait_ge(s_ss, t)
                    nc.scalar.activation(sqa[:], bank(Y + 2 * t), ACT.Square).then_inc(s_sq, 1)
                xt_act(act, 2, gain_sub)
                for j in range(8):
                    hi(act, n["out0"] + RING + j)
                post_act(act, 1, n["out0"] + 7)
            if stage >= 3:
                xt_act(act, 3, gainA(0, 4))
                pre_act(act, 2)
                ffn_act(act, 1, n["f1"], 2)
                post_act(act, 2, n["f1"] + 65)
            if stage >= 4:
                xt_act(act, 4, gainA(1, 0))
                pre_act(act, 3)
                ffn_act(act, 2, n["f2"], 3)
                post_act(act, 3, n["f2"] + 65)
            if stage >= 5:
                xt_act(act, 5, gainA(1, 2))
                pre_act(act, 4)
                qkv_act(act, 1, n["qkv1"], 4)
                attn_act(act, 1, "na")
                xt_act(act, 6, None)
                for j in range(8):
                    hi(act, n["out1"] + RING + j)
                post_act(act, 4, n["out1"] + 7)
            if stage >= 6:
                xt_act(act, 7, gainA(1, 4))
                pre_act(act, 5)
                ffn_act(act, 3, n["f3"], 5)
                post_act(act, 5, n["f3"] + 65)
            if stage >= 7:
                xt_act(act, 8, gainB(B_ATTN))
                pre_act(act, 6)
                act.wait_ge(s_wf, 16)
                nc.scalar.copy(wfh[:], wf[:]).then_inc(s_wfh, 1)
                qkv_act(act, 2, n["qkv2"], 6)
                for c in range(4):
                    for j in range(UP):
                        hi(act, n["gates"] + RING + UP * c + j)
                    act.wait_ge(s_g, 2 * (c + 1))
                    nc.scalar.activation(gates[:, :, c * 512:(c + 1) * 512], gates[:, :, c * 512:(c + 1) * 512],
                                         ACT.Sigmoid).then_inc(s_sg, 1)
                act.wait_ge(s_qa, 18)
                k = 0
                for t in range(NT):
                    for c0 in (0, 1536):
                        if t == 1 and c0 == 0:
                            act.wait_ge(s_qv, 18)
                        if k:
                            act.wait_ge(s_ss, 2 + k)
                        nc.scalar.activation(sqa[:], qkv[:, t, c0:c0 + D], ACT.Square).then_inc(s_sq, 1)
                        k += 1
                act.wait_ge(s_fv, 2)
                nc.scalar.activation(lf[:, 1], lf[:, 1], ACT.Exp, scale=-1.0).then_inc(s_fe, 1)
                act.wait_ge(s_fe, 1)
                nc.scalar.activation(lf[:, 1], lf[:, 1], ACT.Ln, bias=1.0).then_inc(s_fe, 1)
                attn_act(act, 2, "b2")
                xt_act(act, 9, None)
                for j in range(8):
                    hi(act, n["bra"] + RING + j)
                xt_act(act, 10, None)
                for j in range(8):
                    hi(act, n["out2"] + RING + j)
            if stage >= 8:
                xt_act(act, 11, gainB(B_FFN))
                pre_act(act, 7)
                conv_ffn_act(act)

        @block.vector
        def _(dve):
            steps = Steps(dve, s_v)
            dve.sem_inc(s_lo, RING)
            for i in range(RING):
                dve.wait_ge(s_hi, i + 1)
                nc.vector.tensor_tensor(wlo[:, i], raw[:, i], whi[:, i].bitcast(F32), ALU.subtract).then_inc(s_lo, 1)
            dve.wait_ge(s_gev, 2)
            xt_dve(dve, 0, gainA(0, 0))
            dve.wait_ge(s_rx, 1)
            ffn_dve(dve, 0, n["f0"])
            post_dve(dve, steps, 0)
            if stage >= 2:
                xt_dve(dve, 1, gainA(0, 2))
                dve.wait_ge(s_lam, 16)
                steps.done(nc.vector.tensor_tensor(lamp[:], lamv[:].rearrange("p (a b) c -> p a b c", b=2)[:, :, 0],
                                                   lamv[:].rearrange("p (a b) c -> p a b c", b=2)[:, :, 1], ALU.mult))
                nc.vector.tensor_reduce(lam[:, 0:2], lamp[:], AX_X, ALU.add).then_inc(s_lsum, 1)
                qkv_dve(dve, 0, n["qkv0"], 1)
                dve.wait_ge(s_lexp, 1)
                steps.done(nc.vector.tensor_tensor(lam[:, 5:6], lam[:, 2:3], lam[:, 3:4], ALU.subtract))
                steps.done(nc.vector.tensor_scalar(lam[:, 4:5], lam[:, 5:6], LAM_INIT, None, ALU.add))
                steps.done(nc.vector.tensor_scalar(gB[:, B_SUB:B_SUB + 1], gB[:, B_SUB:B_SUB + 1], 1.0 - LAM_INIT, None, ALU.mult))
                dve.wait_ge(s_qa, 6)
                dve.wait_ge(s_qv, 6)
                if stage >= 5:
                    dve.wait_ge(s_scr, 16)
                rope_dve(dve, steps, 0, 32)
                attn_dve(dve, steps, 0, "diff")
                xt_dve(dve, 2, gain_sub)
                for j in range(8):
                    lo(dve, n["out0"] + RING + j)
                post_dve(dve, steps, 1)
            if stage >= 3:
                xt_dve(dve, 3, gainA(0, 4))
                dve.wait_ge(s_rx, 3)
                ffn_dve(dve, 1, n["f1"])
                post_dve(dve, steps, 2)
            if stage >= 4:
                xt_dve(dve, 4, gainA(1, 0))
                dve.wait_ge(s_rx, 4)
                ffn_dve(dve, 2, n["f2"])
                post_dve(dve, steps, 3)
            if stage >= 5:
                xt_dve(dve, 5, gainA(1, 2))
                qkv_dve(dve, 1, n["qkv1"], 4)
                attn_dve(dve, steps, 1, "na")
                xt_dve(dve, 6, None)
                for j in range(8):
                    lo(dve, n["out1"] + RING + j)
                post_dve(dve, steps, 4)
            if stage >= 6:
                xt_dve(dve, 7, gainA(1, 4))
                dve.wait_ge(s_rx, 6)
                ffn_dve(dve, 3, n["f3"])
                post_dve(dve, steps, 5)
            if stage >= 7:
                xt_dve(dve, 8, gainB(B_ATTN))
                dve.wait_ge(s_wfh, 1)
                nc.vector.tensor_tensor(wfl[:], wf[:], wfh[:].bitcast(F32), ALU.subtract).then_inc(s_wfl, 1)
                qkv_dve(dve, 2, n["qkv2"], 6)
                dve.wait_ge(s_aux2, 32)
                dve.wait_ge(s_b2, 80)
                dve.wait_ge(s_fz, 1)
                for t in range(NT):
                    steps.done(nc.vector.scalar_tensor_tensor(out=lf[:, 0, t], in0=ps[:, Y, t * 8:t * 8 + 8], scalar=rx[:, t:t + 1],
                                                              in1=bfg[:], op0=ALU.mult, op1=ALU.add))
                nc.vector.tensor_scalar(lf[:, 2], lf[:, 0], 0.0, None, ALU.min).then_inc(s_fv, 1)
                dve.wait_ge(s_fv, 1)
                nc.vector.scalar_tensor_tensor(out=lf[:, 1], in0=lf[:, 2], scalar=-2.0, in1=lf[:, 0],
                                               op0=ALU.mult, op1=ALU.add).then_inc(s_fv, 1)
                for c in range(4):
                    for j in range(UP):
                        lo(dve, n["gates"] + RING + UP * c + j)
                    dve.wait_ge(s_used, used(n["gates"] + UP * c + 3))
                    for t in range(NT):
                        nc.vector.scalar_tensor_tensor(out=gates[:, t, c * 512:(c + 1) * 512],
                                                       in0=ps[:, Z + 2 * (c % 2) + t], scalar=rx[:, t:t + 1],
                                                       in1=bgate[:, c * 512:(c + 1) * 512], op0=ALU.mult,
                                                       op1=ALU.add).then_inc(s_g, 1)
                k = 0
                for t in range(NT):
                    for half in range(2):
                        dve.wait_ge(s_sq, 2 + k + 1)
                        nc.vector.tensor_reduce(sso[:, t, half * 16:(half + 1) * 16],
                                                sqa[:].rearrange("p (g c) -> p g c", c=HD), AX_X, ALU.add).then_inc(s_ss, 1)
                        k += 1
                dve.wait_ge(s_fe, 2)
                nc.vector.tensor_tensor(lf[:, 0], lf[:, 2], lf[:, 1], ALU.subtract).then_inc(s_fv, 1)
                for t in range(NT):
                    dve.wait_ge(s_ro, 2 + t + 1)
                    for half in range(2):
                        v = qkv[:, t, half * 1536:half * 1536 + D].rearrange("p (g c) -> p g c", c=HD)
                        steps.done(nc.vector.tensor_tensor(v, v, ro[:, t, half * 16:(half + 1) * 16].unsqueeze(2).broadcast_to([P, 16, HD]), ALU.mult))
                        for w in range(2):
                            vv = v[:, 8 * w:8 * w + 8]
                            steps.done(nc.vector.tensor_tensor(vv, vv, qkg[:, 2 * half + w].unsqueeze(1).broadcast_to([P, 8, HD]), ALU.mult))
                rope_dve(dve, steps, 0, 16)
                dve.wait_ge(s_fc, 1)
                nc.vector.tensor_copy(cT[:, 0], ps[0:8, Y, 0:S]).then_inc(s_fc, 1)
                nc.vector.tensor_scalar(cT[:, 1], ps[0:8, Y, 0:S], -1.0, None, ALU.mult).then_inc(s_fc, 1)
                attn_dve(dve, steps, 2, "b2")
                xt_dve(dve, 9, None)
                for j in range(8):
                    lo(dve, n["bra"] + RING + j)
                dve.wait_ge(s_used, used(n["brb"] + 3))
                dve.wait_ge(s_sg, 4)
                for t in range(NT):
                    steps.done(nc.vector.tensor_tensor(sqa[:], gates[:, t, 0:D], bank(Y + 2 * t), ALU.mult))
                    steps.done(nc.vector.tensor_tensor(osb[:, t], gates[:, t, D:2 * D], bank(Z + 2 * t), ALU.mult))
                    nc.vector.tensor_tensor(osb[:, t], osb[:, t], sqa[:], ALU.add).then_inc(s_src, 1)
                    dve.wait_ge(s_src, 18 + t + 1)
                xt_dve(dve, 10, None)
                for j in range(8):
                    lo(dve, n["out2"] + RING + j)
                dve.wait_ge(s_used, used(n["out2"] + 7))
                for t in range(NT):
                    nc.vector.tensor_tensor(h[:, t], h[:, t], bank(Y + 2 * t), ALU.add).then_inc(s_src, 1)
            if stage >= 8:
                xt_dve(dve, 11, gainB(B_FFN))
                conv_ffn_dve(dve, steps)

        @block.tensor
        def _(pe):
            pe.wait_ge(s_cst, 16)
            pe.sem_inc(s_used, RING)
            pe.wait_ge(s_rows, 96)
            nc.tensor.transpose(ps[:, Y, 0:96], rowsA, ident[0:96, 0:96]).then_inc(s_gT, 1)
            nc.tensor.transpose(ps[:, Y, 128:128 + B_END], rowsB, ident[0:B_END, 0:B_END]).then_inc(s_gT, 1)
            pe.wait_ge(s_x, 32)
            xt_pe(pe, 0, h)
            ffn_pe(pe, 0, n["f0"], 0)
            if stage >= 2:
                xt_pe(pe, 1, h)
                qkv_pe(pe, 0, n["qkv0"], 1)
                attn_pe(pe, 0, "diff")
                xt_pe(pe, 2, osb)
                proj_pe(pe, n["out0"], 2, 8, Y)
            if stage >= 3:
                xt_pe(pe, 3, h)
                ffn_pe(pe, 1, n["f1"], 3)
            if stage >= 4:
                xt_pe(pe, 4, h)
                ffn_pe(pe, 2, n["f2"], 4)
            if stage >= 5:
                xt_pe(pe, 5, h)
                qkv_pe(pe, 1, n["qkv1"], 5)
                attn_pe(pe, 1, "na")
                xt_pe(pe, 6, osb)
                proj_pe(pe, n["out1"], 6, 8, Y)
            if stage >= 6:
                xt_pe(pe, 7, h)
                ffn_pe(pe, 3, n["f3"], 7)
            if stage >= 7:
                xt_pe(pe, 8, h)
                qkv_pe(pe, 2, n["qkv2"], 8)
                pe.wait_ge(s_wfl, 1)
                for t in range(NT):
                    c = slice(t * P, (t + 1) * P)
                    o = ps[:, Y, t * 8:t * 8 + 8]
                    for k in range(KT):
                        nc.tensor.matmul(o, xhi[:, k, c], wfh[:, k], start=k == 0, stop=False)
                        nc.tensor.matmul(o, xhi[:, k, c], wfl[:, k], start=False, stop=False)
                        ins = nc.tensor.matmul(o, xlo[:, k, c], wfh[:, k], start=False, stop=k == KT - 1)
                ins.then_inc(s_fz, 1)
                for c in range(4):
                    if c < 2:
                        pe.wait_ge(s_qa, 17 + c)
                        pe.wait_ge(s_qv, 17 + c)
                    else:
                        pe.wait_ge(s_g, 2 * (c - 1))
                    for j in range(UP):
                        col_unit(pe, n["gates"] + UP * c + j, 0, j, [Z + 2 * (c % 2), Z + 2 * (c % 2) + 1])
                pe.wait_ge(s_fv, 3)
                for t in range(NT):
                    ins = nc.tensor.matmul(ps[0:8, Y, 0:S], lf[:, 0, t], tri[:, t], start=t == 0, stop=t == NT - 1)
                ins.then_inc(s_fc, 1)
                pe.wait_ge(s_fc, 3)
                pe.wait_ge(s_g, 8)
                attn_pe(pe, 2, "b2")
                xt_pe(pe, 9, osb)
                proj_pe(pe, n["bra"], 9, 4, Y, 0)
                proj_pe(pe, n["brb"], 9, 4, Z, 4)
                xt_pe(pe, 10, osb, whole=True)
                proj_pe(pe, n["out2"], 10, 8, Y)
            if stage >= 8:
                xt_pe(pe, 11, h)
                conv_ffn_pe(pe)


def constants():
    import numpy as np
    c = np.zeros((P, C_END), np.float32)
    c[:, C_ID:C_ID + P] = np.eye(P, dtype=np.float32)
    half = 8
    inv = np.float32(500000.0) ** (-np.arange(0, 16, 2, dtype=np.float32) / np.float32(16))
    ang = np.arange(S, dtype=np.float32)[:, None] * inv[None, :].astype(np.float32)
    cos, sin = np.cos(ang).astype(np.float32), np.sin(ang).astype(np.float32)
    table = np.concatenate([cos, cos, -sin, sin], axis=1).reshape(NT, P, 4 * half)
    for t in range(NT):
        c[:, C_ROPE + 32 * t:C_ROPE + 32 * (t + 1)] = table[t]
    q = np.arange(P)
    c[:, C_FLIP:C_FLIP + P] = (q[:, None] // GW == q[None] // GW) & (q[:, None] % GW == GW - 1 - q[None] % GW)
    start = np.clip(GW - 1 - q % GW - 8, 0, GW - 16)
    k = np.arange(GW)
    c[:, C_WIN:C_WIN + GW] = np.where((k[None] >= start[:, None]) & (k[None] < start[:, None] + 16), 0.0, MASKED)
    c[:, C_CAUS:C_CAUS + P] = np.where(q[None] <= q[:, None], 0.0, MASKED)
    s = np.arange(S)
    for t in range(NT):
        c[:, C_TRI + S * t:C_TRI + S * (t + 1)] = (q[:, None] + t * P <= s[None])
    sel = np.zeros((8, 8, S), np.float32)
    for i in range(8):
        sel[i, i] = 1.0
    return c, sel.reshape(8, 8 * S)


_INS = ['x', 'norm_g', 'ffn1_wg', 'ffn1_wu', 'ffn1_wd', 'ffn2_wg', 'ffn2_wu', 'ffn2_wd', 'diff_w_in', 'diff_w_out',
        'diff_lambda', 'diff_subln', 'na_w_in', 'na_w_out', 'na_rpb', 'attn_norm_g_2', 'w_in_2', 'b_forget_2',
        'b_gate_2', 'moba_q_norm_g_2', 'moba_k_norm_g_2', 'fox_q_norm_g_2', 'fox_k_norm_g_2',
        'w_branch_moba_2', 'w_branch_fox_2', 'w_out_2', 'ffn_norm_g_2', 'w_ffn_up_2', 'ffn_conv_w_2',
        'ffn_conv_b_2', 'w_ffn_down_2']
_OUTS = [((1, S, D), 'float32')]


def kernel(**inputs):
    import numpy as _np
    import concourse.bacc as _bacc
    from concourse import mybir as _mybir
    from concourse.bass_utils import run_bass_kernel_spmd as _run

    nc = _bacc.Bacc("TRN2", target_bir_lowering=False, num_devices=1)
    arrays, args = {}, []
    given = [(name, _np.ascontiguousarray(inputs[name])) for name in _INS]
    given += list(zip(("const_pack", "const_sel"), constants()))
    for name, a in given:
        arrays[f"in_{name}_dram"] = a
        args.append(nc.dram_tensor(f"in_{name}_dram", a.shape, _mybir.dt.from_np(a.dtype), kind="ExternalInput").ap())
    for i, (shape, dtype) in enumerate(_OUTS):
        dt = _mybir.dt.from_np(_np.dtype(dtype))
        args.append(nc.dram_tensor(f"out_{i}_dram", shape, dt, kind="ExternalOutput").ap())
    build(nc, *args)
    r = _run(nc, [arrays], core_ids=[0])
    got = tuple(r.results[0][f"out_{i}_dram"] for i in range(len(_OUTS)))
    return got[0]
```

```python
from contextlib import ExitStack

import concourse.bass as bass
from concourse import mybir

F32 = mybir.dt.float32
F32R = mybir.dt.float32r
ALU = mybir.AluOpType
ACT = mybir.ActivationFunctionType
AX_X = mybir.AxisListType.X

P = 128
S = 256
NT = S // P
D = 1024
KT = D // P
F = 2816
FC = 256
NCH = F // FC
FT = F // P
RING = 6
DMA2 = 32
UP = KT // 2
EPS = 1e-6
LAM_INIT = 0.8 - 0.6 * 1.0
HD = 64
GW = 64
GR = S // GW
NAH = 16
MASKED = -1e30
TAPS = 3

C_ID, C_ROPE, C_WIN, C_CAUS, C_TRI, C_FLIP, C_HEAD, C_END = 0, 128, 192, 256, 384, 896, 1024, 1032
B_ATTN, B_FFN, B_SUB, B_CONV, B_END = 0, 8, 16, 17, 17 + 4 * 22


def build(nc, x, norm_g, ffn1_wg, ffn1_wu, ffn1_wd, ffn2_wg, ffn2_wu, ffn2_wd, diff_w_in, diff_w_out,
          diff_lambda, diff_subln, na_w_in, na_w_out, na_rpb, attn_norm_g_2, w_in_2, b_forget_2,
          b_gate_2, moba_q_norm_g_2, moba_k_norm_g_2, fox_q_norm_g_2, fox_k_norm_g_2,
          w_branch_moba_2, w_branch_fox_2, w_out_2, ffn_norm_g_2, w_ffn_up_2, ffn_conv_w_2,
          ffn_conv_b_2, w_ffn_down_2, const_pack, out, stage=99):
    ctx = ExitStack()
    with ctx:
        def sb(name, shape, dt=F32):
            return ctx.enter_context(nc.sbuf_tensor(name, shape, dt))

        def sem(name):
            return ctx.enter_context(nc.semaphore(name))

        raw = sb("raw", [P, RING, 2, 512])
        whi = sb("whi", [P, RING, 2, 512], F32R)
        wlo = sb("wlo", [P, RING, 2, 512], F32R)
        h = sb("h", [P, NT, D])
        xhi = sb("xhi", [P, KT, S], F32R)
        xlo = sb("xlo", [P, KT, S], F32R)
        thi = sb("thi", [P, 2, S], F32R)
        tlo = sb("tlo", [P, 2, S], F32R)
        qkv = sb("qkv", [P, NT, 3 * D])
        qT = sb("qT", [P, KT, S])
        kT = sb("kT", [P, KT, S])
        osb = sb("osb", [P, NT, D])
        kT1 = osb[:].rearrange("p t (k s) -> p (t k) s", s=S)
        sqa = sb("sqa", [P, D])
        aux = sb("aux", [P, 8192])
        gpost = sb("gpost", [P, D])
        ex = sb("ex", [P, 3, 2, S])
        aT = sb("aT", [P, 2, 4, P])
        cst = sb("cst", [P, C_END])
        rowsA = sqa[0:96, 0:P]
        rowsB = sqa[0:B_END, P:2 * P]
        o_sb = qkv[:, :, 0:D]
        gA = sb("gA", [P, 96])
        gB = sb("gB", [P, B_END])
        qkg = sb("qkg", [P, 4, HD])
        lamv = sb("lamv", [P, 4, HD])
        lamp = sb("lamp", [P, 2, HD])
        lam = sb("lam", [P, 8])
        nh = sb("nh", [P, 32])
        ssx = sb("ssx", [P, NT])
        rx = sb("rx", [P, NT])
        ssy = sb("ssy", [P, NT])
        ry = sb("ry", [P, NT])
        sso = sb("sso", [P, NT, 32])
        ro = sb("ro", [P, NT, 32])
        nmx = sb("nmx", [P, 2, 2])
        rs = sb("rs", [P, NT, 16])
        ri = sb("ri", [P, NT, 16])
        wf = sb("wf", [P, KT, 8])
        wfh = sb("wfh", [P, KT, 8], F32R)
        wfl = sb("wfl", [P, KT, 8], F32R)
        bfg = sb("bfg", [P, 8])
        lf = sb("lf", [P, 3, NT, 8])
        lf4 = aux[:, 6144:6144 + NT * P].rearrange("p (t c) -> p t c", t=NT)
        cB = aux[:, 6144 + S:6144 + 2 * S]
        cH = thi[:, 0]
        cL = thi[:, 1]
        cR = xlo
        identr = tlo[:, 0, 0:P]
        causr = tlo[:, 0, P:2 * P]
        wgt = sb("wgt", [P, 2])
        cw = sb("cw", [P, 4, 2])

        ident = cst[:, C_ID:C_ID + P]
        rope = cst[:, C_ROPE:C_ROPE + 64].rearrange("p (t c) -> p t c", t=NT)
        win = cst[:, C_WIN:C_WIN + GW]
        flip = cst[:, C_FLIP:C_FLIP + P]
        caus = cst[:, C_CAUS:C_CAUS + P]
        tri = cst[:, C_TRI:C_TRI + 2 * S].rearrange("p (t c) -> p t c", t=NT)
        silu = qkv[:, 0, 0:512].rearrange("p (t c) -> p t c", t=NT)
        hs = qkv[:, 0, 512:1024].rearrange("p (t c) -> p t c", t=NT)
        ug = qkv[:, 0, 1024:2048].rearrange("p (t c) -> p t c", t=NT)
        cv0 = qkv[:, 1, 0:512].rearrange("p (f c) -> p f c", f=2)
        cv1 = qkv[:, 1, 512:1024].rearrange("p (f c) -> p f c", f=2)
        cv2 = qkv[:, 1, 1024:1536].rearrange("p (f c) -> p f c", f=2)
        cv3 = qkv[:, 1, 1536:2048].rearrange("p (f c) -> p f c", f=2)
        nab = aux[:, :].rearrange("p (t h c) -> p t h c", t=NT, h=NAH)
        gates = aux[:, 0:4096].rearrange("p (t c) -> p t c", t=NT)
        bgate = aux[:, 4096:6144]
        head_row = cst[:, C_HEAD:C_HEAD + 8]
        sq4 = [sqa[:]] + [qT[:, 4 * i:4 * i + 4, :].rearrange("p k c -> p (k c)") for i in range(2)] + [sqa[:]]
        pad = qT[0:120, :, :].rearrange("p k c -> p (k c)")[:, 0:254].rearrange("p (a c) -> p a c", a=2)

        ps = ctx.enter_context(nc.psum_tensor("ps", [P, 8, 512], F32))
        Y, Z = 0, 4

        scratch = nc.dram_tensor("rpb_scratch", (240, 127), F32, kind="Internal").ap()

        s_dma = [sem(f"unit_landed{i}") for i in range(RING)]
        s_hi = sem("hi_done")
        s_lo = sem("lo_done")
        s_used = sem("unit_used")
        s_cst = sem("ident_landed")
        s_cst2 = sem("consts_landed")
        s_rowsB = sem("rowsB_landed")
        s_idr = sem("f32r_consts_ready")
        s_yt = sem("first_y_tile_done")
        s_x = sem("x_landed")
        s_rows = sem("rows_landed")
        s_nh = sem("half_exponent_set")
        s_gT = sem("gains_transposed")
        s_gev = sem("gains_ready")
        s_gp = sem("post_gain_landed")
        s_src = sem("xt_source_ready")
        s_tr = sem("xt_transposed")
        s_xh = sem("xt_hi")
        s_xl = sem("xt_lo")
        s_ssx = sem("pre_norm_sum")
        s_rx = sem("pre_norm_rstd")
        s_si = sem("silu_done")
        s_hc = sem("hidden_ready")
        s_ht = sem("hidden_transposed")
        s_hth = sem("hidden_hi")
        s_htl = sem("hidden_lo")
        s_ssy = sem("post_norm_sum")
        s_ry = sem("post_norm_rstd")
        s_qa = sem("chunk_evac_act")
        s_qv = sem("chunk_evac_dve")
        s_qr = sem("qkv_ready")
        s_qt = sem("qk_transposed")
        s_qta = sem("qT_ready")
        s_ktv = sem("kT_ready")
        s_kta = sem("kT1_ready")
        s_kz = sem("kT_rest_zero")
        s_sc = sem("scores_done")
        s_mx = sem("max_done")
        s_ex = sem("exp_done")
        s_a = sem("probs_ready")
        s_at = sem("probs_transposed")
        s_ate = sem("probsT_ready")
        s_pv = sem("pv_done")
        s_sq = sem("head_squares")
        s_ss = sem("head_sums")
        s_ro = sem("head_rstd")
        s_v = sem("dve_step")
        s_p = sem("pool_step")
        s_ac = sem("act_step")
        s_pad = sem("pad_set")
        s_rp = sem("rpb_landed")
        s_scr = sem("scratch_written")
        s_nab = sem("bias_landed")
        s_nar = sem("bias_ready")
        s_lam = sem("lambda_landed")
        s_lsum = sem("lambda_sums")
        s_lexp = sem("lambda_exp")
        s_b2 = sem("block2_small_landed")
        s_aux2 = sem("block2_aux_landed")
        s_wf = sem("forget_weights_landed")
        s_wfh = sem("forget_hi")
        s_wfl = sem("forget_lo")
        s_fz = sem("forget_logits")
        s_fe = sem("forget_act")
        s_fv = sem("forget_dve")
        s_fc = sem("forget_cumsum")
        s_fh = sem("forget_cumsum_hi")
        s_fr = sem("forget_terms_ready")
        s_one = sem("forget_ones_set")
        s_fcv = sem("forget_rows_ready")
        s_sub = sem("sublayer_gain_ready")
        s_g = sem("gate_logits")
        s_sg = sem("gates_ready")
        s_cw = sem("conv_taps")
        s_ug = sem("up_copied")
        s_ut = sem("up_transposed")
        s_c0 = sem("conv_tap2")
        s_c1 = sem("conv_tap1")
        s_cc = sem("conv_hidden")
        s_t1 = sem("conv_tap1_half")
        s_si2 = sem("conv_silu")
        s_out = sem("out_written")

        block = ctx.enter_context(nc.Block())

        def bank(b, t=0, w=2):
            return ps[:, b:b + w, :].rearrange("p b c -> p (b c)")

        def used(n0):
            return RING + n0 + 1

        def slot(n0):
            return n0 % RING

        def load(sp, n0, it, dsts_srcs):
            s = slot(n0)
            sp.wait_ge(s_lo, n0 + 1 + RING * it)
            for dst, src in dsts_srcs(raw[:, s]):
                sp.dma_start(dst, src).then_inc(s_dma[s], 16)

        def hi(act, n0, it=0):
            if isinstance(it, int) and n0 + RING * it >= N_UNITS:
                return
            s = slot(n0)
            act.wait_ge(s_dma[s], DMA2 * (n0 // RING + 1) + DMA2 * it)
            act.wait_ge(s_used, n0 + 1 + RING * it)
            nc.scalar.copy(whi[:, s], raw[:, s]).then_inc(s_hi, 1)

        def lo(dve, n0, it=0):
            if isinstance(it, int) and n0 + RING * it >= N_UNITS:
                return
            s = slot(n0)
            dve.wait_ge(s_hi, n0 + 1 + RING * it)
            nc.vector.tensor_tensor(wlo[:, s], raw[:, s], whi[:, s].bitcast(F32), ALU.subtract).then_inc(s_lo, 1)

        def mm3(outs, ahi, alo, s, i, start, stop):
            last = None
            for t in range(NT):
                c = slice(t * P, (t + 1) * P)
                nc.tensor.matmul(outs[t], ahi[:, c], whi[:, s, i], start=start, stop=False)
                nc.tensor.matmul(outs[t], ahi[:, c], wlo[:, s, i], start=False, stop=False)
                last = nc.tensor.matmul(outs[t], alo[:, c], whi[:, s, i], start=False, stop=stop)
            return last

        def col_unit(pe, n0, it, j, banks, r=None):
            if r is not None:
                pe.wait_ge(s_xl, 4 * r + max(j + 1, 2))
            s = slot(n0)
            pe.wait_ge(s_lo, RING + n0 + 1 + RING * it)
            for i in range(2):
                k = 2 * j + i
                last = mm3([ps[:, b] for b in banks], xhi[:, k], xlo[:, k], s, i, k == 0, k == KT - 1)
            last.then_inc(s_used, 1)
            return last

        def row_unit(pe, n0, it, ahi, alo, base, start, stop):
            s = slot(n0)
            pe.wait_ge(s_lo, RING + n0 + 1 + RING * it)
            for i in range(2):
                last = mm3([ps[:, base + i], ps[:, base + 2 + i]], ahi, alo, s, i, start, stop)
            last.then_inc(s_used, 1)

        def last_rows(pe, n0, acts, base):
            for u in range(2):
                pe.wait_ge(s_lo, RING + n0 + u + 1)
            for t in range(NT):
                c = slice(t * P, (t + 1) * P)
                for u in range(2):
                    ahi, alo = acts[u]
                    for i in range(2):
                        o, w = ps[:, base + 2 * t + i], slot(n0 + u)
                        nc.tensor.matmul(o, ahi[:, c], whi[:, w, i], start=False, stop=False)
                        nc.tensor.matmul(o, ahi[:, c], wlo[:, w, i], start=False, stop=False)
                        last = nc.tensor.matmul(o, alo[:, c], whi[:, w, i], start=False, stop=u == 1)
                    if t == NT - 1:
                        last.then_inc(s_used, 1)
                    elif u == 1:
                        last.then_inc(s_yt, 1)

        def xt_pe(pe, r, src, reverse=False):
            for t in range(NT):
                if r:
                    pe.wait_ge(s_src, 2 * (r - 1) + t + 1)
                for k in range(KT):
                    o = ps[:, Z + k // 2, (k % 2) * S + t * P:(k % 2) * S + (t + 1) * P]
                    a = src[:, t, k * P:(k + 1) * P]
                    ins = nc.tensor.matmul(o, a, flip, start=True, stop=True) if reverse else nc.tensor.transpose(o, a, ident)
                    if t == NT - 1 and k % 2 == 1:
                        ins.then_inc(s_tr, 1)

        def xt_act(act, r, gain):
            for b in range(4):
                act.wait_ge(s_tr, 4 * r + b + 1)
                if gain is None:
                    ins = nc.scalar.copy(xhi[:, 2 * b:2 * b + 2, :].rearrange("p k c -> p (k c)"), ps[:, Z + b])
                else:
                    for i in range(2):
                        ins = nc.scalar.activation(xhi[:, 2 * b + i], ps[:, Z + b, i * S:(i + 1) * S], ACT.Copy,
                                                   scale=gain(2 * b + i))
                ins.then_inc(s_xh, 1)

        def xt_dve(dve, r, gain, late=None):
            for b in range(4):
                dve.wait_ge(s_xh, 4 * r + b + 1)
                if gain is None:
                    ins = nc.vector.tensor_tensor(xlo[:, 2 * b:2 * b + 2, :].rearrange("p k c -> p (k c)"), ps[:, Z + b],
                                                  xhi[:, 2 * b:2 * b + 2, :].rearrange("p k c -> p (k c)").bitcast(F32),
                                                  ALU.subtract)
                else:
                    for i in range(2):
                        ins = nc.vector.scalar_tensor_tensor(
                            out=xlo[:, 2 * b + i], in0=ps[:, Z + b, i * S:(i + 1) * S], scalar=gain(2 * b + i),
                            in1=xhi[:, 2 * b + i].bitcast(F32), op0=ALU.mult, op1=ALU.subtract)
                ins.then_inc(s_xl, 1)
                if b == 0 and late is not None:
                    lo(dve, late)

        def gainA(layer, j):
            return lambda k: gA[:, (layer * 6 + j) * KT + k:(layer * 6 + j) * KT + k + 1]

        def gainB(c0):
            return lambda k: gB[:, c0 + k:c0 + k + 1]

        def gain_sub(k):
            return gB[:, B_SUB:B_SUB + 1]

        def pre_act(act, r):
            for t in range(NT):
                nc.scalar.activation(sqa[:], h[:, t], ACT.Square, accum_out=ssx[:, t:t + 1]).then_inc(s_ssx, 1)
                act.wait_ge(s_ssx, 2 * r + t + 1)

        class Steps:
            def __init__(self, eng, s):
                self.eng, self.s, self.n = eng, s, 0

            def done(self, ins):
                ins.then_inc(self.s, 1)
                self.n += 1
                self.eng.wait_ge(self.s, self.n)

        def rstd(steps, out_, ss, n, factor=1.0):
            g = 1.0 / (factor * factor)
            w = out_.shape[-1]
            steps.done(nc.gpsimd.tensor_scalar(out_, ss, g / n, EPS * g, ALU.mult, ALU.add))
            return nc.gpsimd.tensor_tensor(out_, out_, nh[:, 0:w], ALU.pow)

        def pre_pool(pool, steps, r):
            pool.wait_ge(s_ssx, 2 * r + 2)
            rstd(steps, rx[:], ssx[:], D).then_inc(s_rx, 1)

        def post_act(act, q, yt, last):
            act.wait_ge(s_yt, yt)
            for t in range(NT):
                if t:
                    act.wait_ge(s_used, used(last))
                    act.wait_ge(s_ssy, 2 * q + t)
                nc.scalar.activation(sqa[:], bank(Y + 2 * t), ACT.Square, accum_out=ssy[:, t:t + 1]).then_inc(s_ssy, 1)
                hi(act, last - 1 + t + RING)

        def zero_pool(pool, m, r):
            pool.wait_ge(s_rx, r + 1)
            nc.gpsimd.memset(kT[HD:P], 0.0).then_inc(s_kz, 1)
            pool.wait_ge(s_kz, 2 * m + 1)
            nc.gpsimd.memset(kT1[0:HD], 0.0).then_inc(s_kz, 1)
            pool.wait_ge(s_kz, 2 * m + 2)

        def post_pool(pool, steps, q, factor):
            for t in range(NT):
                pool.wait_ge(s_ssy, 2 * q + t + 1)
                rstd(steps, ry[:, t:t + 1], ssy[:, t:t + 1], D, factor).then_inc(s_ry, 1)

        def post_dve(dve, steps, q, last):
            dve.wait_ge(s_gp, 16 * (q + 1))
            for t in range(NT):
                dve.wait_ge(s_ssy, 2 * q + t + 1)
                steps.done(nc.vector.tensor_tensor(osb[:, t], bank(Y + 2 * t), gpost[:], ALU.mult))
                dve.wait_ge(s_ry, 2 * q + t + 1)
                nc.vector.scalar_tensor_tensor(out=h[:, t], in0=osb[:, t], scalar=ry[:, t:t + 1], in1=h[:, t],
                                               op0=ALU.mult, op1=ALU.add).then_inc(s_src, 1)
            lo(dve, last - 1 + RING)

        def chunks(eng, n0, body):
            more = n0 + 66 < N_UNITS
            with eng.Fori(0, NCH - 1 if more else NCH - 2) as it:
                body(it)
            if not more:
                body(NCH - 2)

        def gu_unit(sp, n0, it, j, c, wg, wu):
            def parts(dst):
                return [(dst[:, :, 0:FC], wg.rearrange("(k p) f -> p k f", p=P)[:, 2 * j:2 * j + 2, bass.ds(c * FC, FC)]),
                        (dst[:, :, FC:2 * FC], wu.rearrange("(k p) f -> p k f", p=P)[:, 2 * j:2 * j + 2, bass.ds(c * FC, FC)])]
            load(sp, n0, it, parts)

        def down_unit(sp, n0, it, w, row):
            def parts(dst):
                return [(dst[:, i], w[bass.ds(row, P), i * 512:(i + 1) * 512]) for i in range(2)]
            load(sp, n0, it, parts)

        def ffn_sp(sp, n0, wg, wu, wd, gain=None):
            for j in range(UP):
                gu_unit(sp, n0 + j, 0, j, 0, wg, wu)
            with sp.Fori(0, NCH - 1) as it:
                for j in range(UP):
                    gu_unit(sp, n0 + 4 + j, it, j, it + 1, wg, wu)
                for j in range(2):
                    down_unit(sp, n0 + 8 + j, it, wd, it * FC + j * P)
            if gain is not None:
                post_gain(sp, gain)
            for j in range(2):
                down_unit(sp, n0 + 64 + j, 0, wd, (NCH - 1) * FC + j * P)

        def gate_up(pe, n0, it, r=None):
            for j in range(UP):
                col_unit(pe, n0 + j, it, j, [Z, Z + 1], r)

        def down(pe, n0, it, start, stop):
            for j in range(2):
                row_unit(pe, n0 + j, it, thi[:, j], tlo[:, j], Y, start and j == 0, stop and j == 1)

        def ffn_pe(pe, f, n0, r):
            b = NCH * f

            def hidden_t(c):
                pe.wait_ge(s_hc, 2 * b + 2 * c + 2)
                for j in range(2):
                    for t in range(NT):
                        ins = nc.tensor.transpose(ps[:, Z + 2, j * S + t * P:j * S + (t + 1) * P],
                                                  hs[:, t, j * P:(j + 1) * P], ident)
                ins.then_inc(s_ht, 1)

            gate_up(pe, n0, 0, r)
            hidden_t(0)

            def body(it, start):
                gate_up(pe, n0 + 4, it)
                pe.wait_ge(s_htl, b + it + 1)
                down(pe, n0 + 8, it, start, False)
                hidden_t(it + 1)
            body(0, True)
            with pe.Fori(1, NCH - 1) as it:
                body(it, False)
            pe.wait_ge(s_htl, b + NCH)
            last_rows(pe, n0 + 64, [(thi[:, j], tlo[:, j]) for j in range(2)], Y)

        def ffn_act(act, f, n0, r):
            b = NCH * f

            def swish(last):
                act.wait_ge(s_used, used(last))
                for t in range(NT):
                    nc.scalar.activation(silu[:, t], ps[:, Z + t, 0:FC], ACT.Silu, scale=rx[:, t:t + 1]).then_inc(s_si, 1)

            def hidden(c):
                act.wait_ge(s_ht, b + c + 1)
                nc.scalar.copy(thi[:, :, :].rearrange("p f c -> p (f c)"), ps[:, Z + 2]).then_inc(s_hth, 1)
            for j in range(3):
                hi(act, n0 + RING + j)
            act.wait_ge(s_rx, r + 1)
            swish(n0 + 3)
            hi(act, n0 + RING + 3)
            hidden(0)

            def body(it):
                for j in range(3):
                    hi(act, n0 + RING + 4 + j, it)
                swish(n0 + 7 + RING * it)
                for j in range(3, 6):
                    hi(act, n0 + RING + 4 + j, it)
                hidden(it + 1)
            chunks(act, n0, body)

        def ffn_dve(dve, f, n0):
            b = NCH * f

            def gated(c):
                for t in range(NT):
                    dve.wait_ge(s_si, 2 * b + 2 * c + t + 1)
                    nc.vector.scalar_tensor_tensor(out=hs[:, t], in0=ps[:, Z + t, FC:2 * FC], scalar=rx[:, t:t + 1],
                                                   in1=silu[:, t], op0=ALU.mult, op1=ALU.mult).then_inc(s_hc, 1)

            def hidden(c):
                dve.wait_ge(s_hth, b + c + 1)
                nc.vector.tensor_tensor(tlo[:, :, :].rearrange("p f c -> p (f c)"), ps[:, Z + 2],
                                        thi[:, :, :].rearrange("p f c -> p (f c)").bitcast(F32), ALU.subtract).then_inc(s_htl, 1)
            for j in range(3):
                lo(dve, n0 + RING + j)
            gated(0)
            lo(dve, n0 + RING + 3)
            hidden(0)

            def body(it):
                for j in range(3):
                    lo(dve, n0 + RING + 4 + j, it)
                gated(it + 1)
                for j in range(3, 6):
                    lo(dve, n0 + RING + 4 + j, it)
                hidden(it + 1)
            chunks(dve, n0, body)

        def chunk_sp(sp, n0, w, cols):
            for c, c0 in enumerate(cols):
                for j in range(UP):
                    load(sp, n0 + UP * c + j, 0, lambda dst: [
                        (dst[:, i], w[(2 * j + i) * P:(2 * j + i + 1) * P, c0:c0 + 512]) for i in range(2)])

        def row_sp(sp, n0, w, rows):
            for j in range(rows // P):
                down_unit(sp, n0 + j, 0, w, j * P)

        def chunk_pe(pe, m, n0, e, units, r=None):
            if e >= 2:
                pe.wait_ge(s_qa, 6 * m + e - 1)
                pe.wait_ge(s_qv, 6 * m + e - 1)
            for j in units:
                col_unit(pe, n0 + UP * e + j, 0, j, [Z + 2 * (e % 2), Z + 2 * (e % 2) + 1], r)

        def tops_act(act, n0):
            for j in range(UP):
                hi(act, n0 + RING + j)

        def tops_dve(dve, n0):
            for j in range(UP):
                lo(dve, n0 + RING + j)

        def evac_act(act, m, n0, e, r, order):
            act.wait_ge(s_used, used(n0 + UP * e + 3))
            if e == 0:
                act.wait_ge(s_rx, r + 1)
            nc.scalar.activation(qkv[:, 0, order[e] * 512:(order[e] + 1) * 512], ps[:, Z + 2 * (e % 2)], ACT.Copy,
                                 scale=rx[:, 0:1]).then_inc(s_qa, 1)

        def evac_dve(dve, m, n0, e, r, order):
            dve.wait_ge(s_used, used(n0 + UP * e + 3))
            if e == 0:
                dve.wait_ge(s_rx, r + 1)
            nc.vector.tensor_scalar(qkv[:, 1, order[e] * 512:(order[e] + 1) * 512], ps[:, Z + 2 * (e % 2) + 1],
                                    rx[:, 1:2], None, ALU.mult).then_inc(s_qv, 1)

        def proj_pe(pe, n0, r, kts, base, first=0, early=True):
            plain = kts - 2 if early else kts
            for j in range(plain):
                pe.wait_ge(s_xl, 4 * r + (first + j) // 2 + 1)
                row_unit(pe, n0 + j, 0, xhi[:, first + j], xlo[:, first + j], base, j == 0, j == kts - 1)
            if early:
                pe.wait_ge(s_xl, 4 * r + (first + kts - 1) // 2 + 1)
                last_rows(pe, n0 + plain, [(xhi[:, first + j], xlo[:, first + j]) for j in (plain, plain + 1)], base)

        IN_ORDER = [0, 1, 2, 3, 4, 5]
        B2_ORDER = [0, 1, 3, 4, 2, 5]

        TASKS = [(p, t) for t in range(NT) for p in range(8)]
        NTASK = len(TASKS)
        NEX = 3

        def qk_cols(kind, p):
            if kind == "b2":
                b = 0 if p < 4 else 3 * 512
                return b + (p % 4) * P, b + 512 + (p % 4) * P, b + 1024 + (p % 4) * P
            return p * P, D + p * P, 2 * D + p * P

        def keys(kind, t):
            return t + 1 if kind == "b2" else NT

        def qk_turn(pe, m, kind, which):
            for bk in range(4):
                if which == 1:
                    pe.wait_ge(s_qta, 4 * m + bk + 1)
                for p in (2 * bk, 2 * bk + 1):
                    c0 = qk_cols(kind, p)[which]
                    for t in range(NT):
                        o = ps[:, Y + bk, (p % 2) * S + t * P:(p % 2) * S + (t + 1) * P]
                        a = qkv[:, t, c0:c0 + P]
                        if kind == "na" and which == 0:
                            ins = nc.tensor.matmul(o, a, flip, start=True, stop=True)
                        else:
                            ins = nc.tensor.transpose(o, a, ident)
                ins.then_inc(s_qt, 1)

        def qT_act(act, m):
            for bk in range(4):
                act.wait_ge(s_qt, 8 * m + bk + 1)
                nc.scalar.activation(qT[:, 2 * bk:2 * bk + 2, :].rearrange("p k c -> p (k c)"), ps[:, Y + bk],
                                     ACT.Copy, scale=HD ** -0.5).then_inc(s_qta, 1)

        def kT_act(act, m):
            for bk in range(4):
                act.wait_ge(s_qt, 8 * m + 4 + bk + 1)
                nc.scalar.copy(kT1[HD:P, 2 * bk:2 * bk + 2, :].rearrange("p k c -> p (k c)"),
                               ps[HD:P, Y + bk]).then_inc(s_kta, 1)

        def kT_dve(dve, m):
            for bk in range(4):
                dve.wait_ge(s_qt, 8 * m + 4 + bk + 1)
                nc.vector.tensor_copy(kT[0:HD, 2 * bk:2 * bk + 2, :].rearrange("p k c -> p (k c)"),
                                      ps[0:HD, Y + bk]).then_inc(s_ktv, 1)

        def attn_pe(pe, m, kind):
            b = NTASK * m
            pe.wait_ge(s_qta, 4 * (m + 1))
            pe.wait_ge(s_ktv, 4 * (m + 1))
            pe.wait_ge(s_kta, 4 * (m + 1))
            pe.wait_ge(s_kz, 2 * (m + 1))
            if kind == "b2":
                pe.wait_ge(s_idr, 2)
                pe.wait_ge(s_g, 8)

            def scores(i):
                p, t = TASKS[i]
                if i >= 2:
                    pe.wait_ge(s_ex, 2 * (b + i - 1))
                w = keys(kind, t) * P
                for c in range(2):
                    o = ps[:, Z + i % 2, c * S:c * S + w]
                    fox = kind == "b2" and p >= 4
                    ins = nc.tensor.matmul(o, qT[:, p, t * P:(t + 1) * P], (kT, kT1)[c][:, p, 0:w], start=True, stop=not fox)
                    if fox:
                        pe.wait_ge(s_fr, 1)
                        ins = nc.tensor.matmul(o, cL[:, t * P:(t + 1) * P], cR[:, 2 * (p - 4) + c, 0:w], start=False, stop=True)
                    if kind == "b2":
                        ins = nc.tensor.matmul(ps[:, Z + i % 2, c * S + t * P:c * S + (t + 1) * P], identr, causr,
                                               start=False, stop=True, skip_group_check=True)
                ins.then_inc(s_sc, 1)

            def turn(i):
                p, t = TASKS[i]
                if i == 0:
                    pe.wait_ge(s_qa, 6 * m + 6)
                    pe.wait_ge(s_qv, 6 * m + 6)
                if kind == "diff":
                    pe.wait_ge(s_a, b + i + 1)
                else:
                    pe.wait_ge(s_ex, 2 * (b + i + 1))
                if i >= 2:
                    pe.wait_ge(s_ate, b + i - 1)
                for c in range(1 if kind == "diff" else 2):
                    for st in range(keys(kind, t)):
                        ins = nc.tensor.transpose(ps[:, Z + 2 + i % 2, (2 * c + st) * P:(2 * c + st + 1) * P],
                                                  ex[:, i % NEX, c, st * P:(st + 1) * P], ident)
                ins.then_inc(s_at, 1)

            def pv(i):
                p, t = TASKS[i]
                pe.wait_ge(s_ate, b + i + 1)
                v0 = qk_cols(kind, p)[2]
                n, w = (1, P) if kind == "diff" else (2, HD)
                for c in range(n):
                    for st in range(keys(kind, t)):
                        ins = nc.tensor.matmul(ps[:, Y + 2 * t + p // 4, (p % 4) * P + c * w:(p % 4) * P + (c + 1) * w],
                                               aT[:, i % 2, 2 * c + st], qkv[:, st, v0 + c * w:v0 + (c + 1) * w],
                                               start=st == 0, stop=st == keys(kind, t) - 1)
                ins.then_inc(s_pv, 1)

            for i in range(NTASK + 3):
                if i < NTASK:
                    scores(i)
                if 2 <= i < NTASK + 2:
                    turn(i - 2)
                if i >= 3:
                    pv(i - 3)

        def attn_act(act, m, kind):
            b = NTASK * m

            def squares(t):
                act.wait_ge(s_pv, b + 8 * (t + 1))
                if t:
                    act.wait_ge(s_ss, t)
                nc.scalar.activation(sqa[:], bank(Y + 2 * t), ACT.Square).then_inc(s_sq, 1)

            for i in range(NTASK + 2):
                if i < NTASK:
                    p, t = TASKS[i]
                    w = keys(kind, t) * P
                    act.wait_ge(s_mx, b + i + 1)
                    if i >= NEX:
                        act.wait_ge(s_at, b + i - 2)
                    src = ex[:, i % NEX] if kind == "na" else ps[:, Z + i % 2].rearrange("p (c k) -> p c k", c=2)
                    for c in range(2):
                        nc.scalar.activation(ex[:, i % NEX, c, 0:w], src[:, c, 0:w], ACT.Exp,
                                             bias=nmx[:, i % 2, c:c + 1],
                                             accum_out=rs[:, t, 2 * p + c:2 * p + c + 1]).then_inc(s_ex, 1)
                if i >= 2:
                    j = i - 2
                    act.wait_ge(s_at, b + j + 1)
                    if j >= 2:
                        act.wait_ge(s_pv, b + j - 1)
                    n = 1 if kind == "diff" else 2
                    k = keys(kind, TASKS[j][1])
                    src = ps[:, Z + 2 + j % 2].rearrange("p (c s q) -> p c s q", c=2, s=2)
                    dst = aT[:, j % 2].rearrange("p (c s) q -> p c s q", c=2)
                    nc.scalar.copy(dst[:, 0:n, 0:k], src[:, 0:n, 0:k]).then_inc(s_ate, 1)
                if i == 12 and kind == "diff":
                    squares(0)
            if kind == "diff":
                squares(1)

        def attn_dve(dve, steps, m, kind):
            b = NTASK * m

            def head_sums(t):
                dve.wait_ge(s_sq, t + 1)
                steps.done(nc.vector.reciprocal(ri[:, t, 0:8], rs[:, t, 0:16:2]))
                steps.done(nc.vector.tensor_reduce(sso[:, t, 0:8], sqa[:].rearrange("p (g c) -> p g c", c=P), AX_X, ALU.add))
                for _ in range(2):
                    ins = nc.vector.tensor_tensor(sso[:, t, 0:8], sso[:, t, 0:8], ri[:, t, 0:8], ALU.mult)
                    if _ == 0:
                        steps.done(ins)
                ins.then_inc(s_ss, 1)

            def head_norm(t):
                dve.wait_ge(s_ro, t + 1)
                steps.done(nc.vector.tensor_tensor(ri[:, t, 8:16], ro[:, t, 0:8], ri[:, t, 0:8], ALU.mult))
                scaled(t, ri[:, t, 8:16], 8)

            def normal(t):
                dve.wait_ge(s_pv, b + 8 * (t + 1))
                dve.wait_ge(s_ex, 2 * (b + 8 * (t + 1)))
                steps.done(nc.vector.reciprocal(ri[:, t], rs[:, t]))
                scaled(t, ri[:, t], 16)

            def scaled(t, by, groups):
                nc.vector.tensor_tensor(o_sb[:, t].rearrange("p (g c) -> p g c", g=groups),
                                        bank(Y + 2 * t).rearrange("p (g c) -> p g c", g=groups),
                                        by.unsqueeze(2).broadcast_to([P, groups, D // groups]),
                                        ALU.mult).then_inc(s_src, 1)

            for i in range(NTASK + 1):
                if i < NTASK:
                    p, t = TASKS[i]
                    w = keys(kind, t) * P
                    dve.wait_ge(s_sc, b + i + 1)
                    sc = ps[:, Z + i % 2].rearrange("p (c k) -> p c k", c=2)[:, :, 0:w]
                    if kind == "na":
                        if i >= NEX:
                            dve.wait_ge(s_at, b + i - 2)
                        steps.done(nc.vector.tensor_tensor(ex[:, i % NEX], sc, nab[:, t, 2 * p:2 * p + 2, :], ALU.add))
                        sc = ex[:, i % NEX]
                    if i >= 2:
                        dve.wait_ge(s_ex, 2 * (b + i - 1))
                    nc.vector.tensor_reduce(nmx[:, i % 2], sc, AX_X, ALU.max, negate=True).then_inc(s_mx, 1)
                if i >= 1 and kind == "diff":
                    j = i - 1
                    p, t = TASKS[j]
                    dve.wait_ge(s_ex, 2 * (b + j + 1))
                    steps.done(nc.vector.reciprocal(wgt[:, 0:1], rs[:, t, 2 * p + 1:2 * p + 2]))
                    steps.done(nc.vector.tensor_scalar(wgt[:, 1:2], rs[:, t, 2 * p:2 * p + 1], wgt[:, 0:1], lam[:, 4:5],
                                                       ALU.mult, ALU.mult))
                    nc.vector.scalar_tensor_tensor(out=ex[:, j % NEX, 0], in0=ex[:, j % NEX, 1], scalar=wgt[:, 1:2],
                                                   in1=ex[:, j % NEX, 0], op0=ALU.mult, op1=ALU.add).then_inc(s_a, 1)
                if kind == "diff" and i == 13:
                    head_sums(0)
                if kind == "diff" and i == 15:
                    head_norm(0)
                if kind != "diff" and i == 13:
                    normal(0)
            if kind == "diff":
                head_sums(1)
                head_norm(1)
            else:
                normal(1)

        def rope_dve(dve, steps, c0, groups):
            tmp = [qT[:, 0:4, :].rearrange("p k c -> p (k c)")[:, 0:groups * 16].rearrange("p (g c) -> p g c", c=16),
                   qT[:, 4:8, :].rearrange("p k c -> p (k c)")[:, 0:groups * 16].rearrange("p (g c) -> p g c", c=16)]
            for t in range(NT):
                v = qkv[:, t, c0:c0 + groups * HD].rearrange("p (g c) -> p g c", c=HD)
                cos = rope[:, t, 0:16].unsqueeze(1).broadcast_to([P, groups, 16])
                nsin = rope[:, t, 16:24].unsqueeze(1).broadcast_to([P, groups, 8])
                psin = rope[:, t, 24:32].unsqueeze(1).broadcast_to([P, groups, 8])
                steps.done(nc.vector.tensor_tensor(tmp[0], v[:, :, 0:16], cos, ALU.mult))
                steps.done(nc.vector.tensor_tensor(tmp[1][:, :, 0:8], v[:, :, 8:16], nsin, ALU.mult))
                steps.done(nc.vector.tensor_tensor(tmp[1][:, :, 8:16], v[:, :, 0:8], psin, ALU.mult))
                last = nc.vector.tensor_tensor(v[:, :, 0:16], tmp[0], tmp[1], ALU.add)
                if t == 0:
                    steps.done(last)
            last.then_inc(s_qr, 1)

        def add_dve(dve, yt, last):
            dve.wait_ge(s_yt, yt)
            for t in range(NT):
                if t:
                    dve.wait_ge(s_used, used(last))
                nc.vector.tensor_tensor(h[:, t], h[:, t], bank(Y + 2 * t), ALU.add).then_inc(s_src, 1)

        def conv_ffn_pe(pe):
            b, n0 = NCH * 4, n["f4"]

            def turn(c):
                pe.wait_ge(s_ug, 2 * c + 2)
                for g in range(2):
                    for j in range(2):
                        for t in range(NT):
                            ins = nc.tensor.transpose(ps[:, Z + 2 + g, j * S + t * P:j * S + (t + 1) * P],
                                                      ug[:, t, g * FC + j * P:g * FC + (j + 1) * P], ident)
                ins.then_inc(s_ut, 1)

            gate_up(pe, n0, 0, 11)
            turn(0)

            def body(it, start):
                gate_up(pe, n0 + 4, it)
                pe.wait_ge(s_htl, b + it + 1)
                down(pe, n0 + 8, it, start, False)
                turn(it + 1)
            body(0, True)
            with pe.Fori(1, NCH - 1) as it:
                body(it, False)
            pe.wait_ge(s_htl, b + NCH)
            last_rows(pe, n0 + 64, [(thi[:, j], tlo[:, j]) for j in range(2)], Y)

        def conv_ffn_act(act):
            b, n0 = NCH * 4, n["f4"]

            def copy_up(last):
                act.wait_ge(s_used, used(last))
                for t in range(NT):
                    nc.scalar.activation(ug[:, t], ps[:, Z + t], ACT.Copy, scale=rx[:, t:t + 1]).then_inc(s_ug, 1)

            def conv(c):
                act.wait_ge(s_ut, c + 1)
                act.wait_ge(s_cw, c + 1)
                for j in range(2):
                    nc.scalar.activation(cv0[:, j], ps[:, Z + 3, j * S:(j + 1) * S], ACT.Identity,
                                         scale=cw[:, 2, j:j + 1], bias=cw[:, 3, j:j + 1]).then_inc(s_c0, 1)
                act.wait_ge(s_c1, c + 1)
                nc.scalar.activation(cv1, cv0, ACT.Silu).then_inc(s_si2, 1)
                act.wait_ge(s_cc, c + 1)
                nc.scalar.copy(thi[:], cv2).then_inc(s_hth, 1)

            act.wait_ge(s_rx, 8)
            for j in range(3):
                hi(act, n0 + RING + j)
            copy_up(n0 + 3)
            hi(act, n0 + RING + 3)
            conv(0)

            def body(it):
                for j in range(3):
                    hi(act, n0 + RING + 4 + j, it)
                copy_up(n0 + 7 + RING * it)
                for j in range(3, 6):
                    hi(act, n0 + RING + 4 + j, it)
                conv(it + 1)
            chunks(act, n0, body)

        def conv_ffn_dve(dve, steps):
            b, n0 = NCH * 4, n["f4"]
            taps = gB[:, B_CONV:B_END].rearrange("p (k f) -> p k f", k=TAPS + 1)

            def conv(c):
                nc.vector.tensor_copy(cw[:], taps[:, :, bass.ds(2 * c, 2)]).then_inc(s_cw, 1)
                dve.wait_ge(s_cw, c + 1)
                dve.wait_ge(s_c0, 2 * c + 2)
                for j in range(2):
                    nc.vector.scalar_tensor_tensor(out=cv0[:, j, 1:S], in0=ps[:, Z + 3, j * S:(j + 1) * S - 1],
                                                   scalar=cw[:, 1, j:j + 1], in1=cv0[:, j, 1:S],
                                                   op0=ALU.mult, op1=ALU.add).then_inc(s_t1, 1)
                for j in range(2):
                    dve.wait_ge(s_t1, 2 * c + 1 + j)
                    ins = nc.vector.scalar_tensor_tensor(out=cv0[:, j, 2:S], in0=ps[:, Z + 3, j * S:(j + 1) * S - 2],
                                                         scalar=cw[:, 0, j:j + 1], in1=cv0[:, j, 2:S],
                                                         op0=ALU.mult, op1=ALU.add)
                ins.then_inc(s_c1, 1)
                dve.wait_ge(s_si2, c + 1)
                nc.vector.tensor_tensor(cv2, cv1, ps[:, Z + 2].rearrange("p (f c) -> p f c", f=2), ALU.mult).then_inc(s_cc, 1)
                dve.wait_ge(s_hth, b + c + 1)
                nc.vector.tensor_tensor(tlo[:], cv2, thi[:].bitcast(F32), ALU.subtract).then_inc(s_htl, 1)

            for j in range(4):
                lo(dve, n0 + RING + j)
            conv(0)

            def body(it):
                for j in range(6):
                    lo(dve, n0 + RING + 4 + j, it)
                conv(it + 1)
            chunks(dve, n0, body)
            add_dve(dve, 9, n0 + 65)

        n = {}
        at = 0
        for name, count in (("f0", 66), ("qkv0", 24), ("out0", 8), ("f1", 66), ("f2", 66), ("qkv1", 24), ("out1", 8),
                            ("f3", 66), ("qkv2", 24), ("gates", 16), ("brb", 4), ("bra", 4), ("out2", 8), ("f4", 66)):
            n[name] = at
            at += count
        ends = {1: 66, 2: 98, 3: 164, 4: 230, 5: 262, 6: 328, 7: 384, 8: 450}
        N_UNITS = ends.get(stage, 450)
        ffn_w = [(ffn1_wg[0], ffn1_wu[0], ffn1_wd[0]), (ffn2_wg[0], ffn2_wu[0], ffn2_wd[0]),
                 (ffn1_wg[1], ffn1_wu[1], ffn1_wd[1]), (ffn2_wg[1], ffn2_wu[1], ffn2_wd[1])]
        POST = [(0, 1), (0, 3), (0, 5), (1, 1), (1, 3), (1, 5)]
        POST_SRC = [2 * r for r in (1, 3, 4, 5, 7, 8)]
        FINAL_SRC = {1: 2, 2: 6, 3: 8, 4: 10, 5: 14, 6: 16, 7: 22}.get(stage, 24)

        def post_gain(sp, q):
            if q >= 1:
                sp.wait_ge(s_src, POST_SRC[q - 1])
            i, j = POST[q]
            sp.dma_start(gpost[:], norm_g[i, j:j + 1, :].broadcast_to([P, D])).then_inc(s_gp, 16)

        @block.sync
        def _(sp):
            sp.dma_start(cst[:, 0:P], const_pack[:, 0:P]).then_inc(s_cst, 16)
            sp.dma_start(rowsA, norm_g.rearrange("i j (k c) -> (i j k) c", c=P)).then_inc(s_rows, 16)
            for t in range(NT):
                sp.dma_start(h[:, t], x[0, t * P:(t + 1) * P, :]).then_inc(s_x, 16)
            ffn_sp(sp, n["f0"], *ffn_w[0], 0)
            if stage >= 2:
                chunk_sp(sp, n["qkv0"], diff_w_in[0], [512 * c for c in range(6)])
                post_gain(sp, 1)
                row_sp(sp, n["out0"], diff_w_out[0], D)
            if stage >= 3:
                ffn_sp(sp, n["f1"], *ffn_w[1], 2)
            if stage >= 4:
                ffn_sp(sp, n["f2"], *ffn_w[2], 3)
            if stage >= 5:
                chunk_sp(sp, n["qkv1"], na_w_in[0], [512 * c for c in range(6)])
                post_gain(sp, 4)
                row_sp(sp, n["out1"], na_w_out[0], D)
            if stage >= 6:
                ffn_sp(sp, n["f3"], *ffn_w[3], 5)
            if stage >= 7:
                chunk_sp(sp, n["qkv2"], w_in_2[0], [512 * c for c in B2_ORDER])
                chunk_sp(sp, n["gates"], w_in_2[0], [3080 + 512 * c for c in range(4)])
                row_sp(sp, n["brb"], w_branch_fox_2[0], 512)
                row_sp(sp, n["bra"], w_branch_moba_2[0], 512)
                row_sp(sp, n["out2"], w_out_2[0], D)
            if stage >= 8:
                up = w_ffn_up_2[0]
                ffn_sp(sp, n["f4"], up[:, 0:F], up[:, F:2 * F], w_ffn_down_2[0])
            for t in range(NT):
                sp.wait_ge(s_src, FINAL_SRC - 1 + t)
                sp.dma_start(out[0, t * P:(t + 1) * P, :], h[:, t]).then_inc(s_out, 16)
            sp.wait_ge(s_out, 32)

        @block.gpsimd
        def _(pool):
            steps = Steps(pool, s_p)
            pool.dma_start(rowsB[B_ATTN:B_ATTN + 8], attn_norm_g_2.rearrange("a (k c) -> (a k) c", c=P)).then_inc(s_rowsB, 16)
            pool.dma_start(rowsB[B_FFN:B_FFN + 8], ffn_norm_g_2.rearrange("a (k c) -> (a k) c", c=P)).then_inc(s_rowsB, 16)
            pool.dma_start(rowsB[B_SUB:B_SUB + 1], diff_subln).then_inc(s_rowsB, 16)
            pool.dma_start(rowsB[B_CONV:B_CONV + 66], ffn_conv_w_2.rearrange("a j (k c) -> (a j k) c", c=P)).then_inc(s_rowsB, 16)
            pool.dma_start(rowsB[B_CONV + 66:B_CONV + 88], ffn_conv_b_2.rearrange("a (k c) -> (a k) c", c=P)).then_inc(s_rowsB, 16)
            pool.dma_start(cst[:, P:], const_pack[:, P:]).then_inc(s_cst2, 16)
            nc.gpsimd.memset(nh[:], -0.5).then_inc(s_nh, 1)
            pool.wait_ge(s_nh, 1)
            pre_pool(pool, steps, 0)
            if stage >= 5:
                nc.gpsimd.memset(pad, MASKED).then_inc(s_pad, 1)
                pool.wait_ge(s_pad, 1)
                pool.dma_start(pad[:, :, 48:79], na_rpb[0].rearrange("h d c -> (h d) c").rearrange("(p a) c -> p a c", a=2)).then_inc(s_rp, 16)
                pool.wait_ge(s_rp, 16)
                pool.dma_start(scratch.rearrange("(p a) c -> p a c", a=2), pad).then_inc(s_scr, 16)
                pool.wait_ge(s_scr, 16)
                for r in range(GR):
                    t, half = r // 2, r % 2
                    for kr in range(GR):
                        src = bass.AP(scratch.tensor, (7 - r + kr) * 127, [[1, GW], [15 * 127, NAH], [1, GW]])
                        dst = nab[half * GW:(half + 1) * GW, t, :, kr * GW:(kr + 1) * GW]
                        pool.dma_start(dst, src).then_inc(s_nab, 16)
            if stage >= 2:
                pool.dma_start(lamv[:].rearrange("p a c -> p (a c)"), diff_lambda.rearrange("a b c -> a (b c)").broadcast_to([P, 4 * HD])).then_inc(s_lam, 16)
            if stage >= 7:
                for i, g in enumerate((moba_q_norm_g_2, moba_k_norm_g_2, fox_q_norm_g_2, fox_k_norm_g_2)):
                    pool.dma_start(qkg[:, i], g.broadcast_to([P, HD])).then_inc(s_b2, 16)
                pool.dma_start(bfg[:], b_forget_2.broadcast_to([P, 8])).then_inc(s_b2, 16)
                pool.dma_start(wf[:], w_in_2[0, :, 3072:3080].rearrange("(k p) c -> p k c", p=P)).then_inc(s_wf, 16)
            post_pool(pool, steps, 0, 0.5)
            if stage >= 2:
                pre_pool(pool, steps, 1)
                zero_pool(pool, 0, 1)
                for t in range(NT):
                    pool.wait_ge(s_ss, t + 1)
                    rstd(steps, ro[:, t, 0:8], sso[:, t, 0:8], P).then_inc(s_ro, 1)
                post_pool(pool, steps, 1, 1.0)
            if stage >= 3:
                pre_pool(pool, steps, 2)
                post_pool(pool, steps, 2, 0.5)
            if stage >= 4:
                pre_pool(pool, steps, 3)
                post_pool(pool, steps, 3, 0.5)
            if stage >= 5:
                pre_pool(pool, steps, 4)
                zero_pool(pool, 1, 4)
                pool.wait_ge(s_nab, 16 * GR * GR)
                pool.wait_ge(s_cst2, 16)
                for t in range(NT):
                    v = nab[:, t].rearrange("p h (r c) -> p (h r) c", r=GR)
                    nc.gpsimd.tensor_tensor(v, v, win.unsqueeze(1).broadcast_to([P, NAH * GR, GW]), ALU.add).then_inc(s_nar, 1)
                post_pool(pool, steps, 4, 1.0)
            if stage >= 6:
                pre_pool(pool, steps, 5)
                post_pool(pool, steps, 5, 0.5)
            if stage >= 7:
                pool.dma_start(bgate, b_gate_2.rearrange("a b c -> a (b c)").broadcast_to([P, 2 * D])).then_inc(s_aux2, 16)
                pre_pool(pool, steps, 6)
                zero_pool(pool, 2, 6)
                nc.gpsimd.memset(lf4, 0.0).then_inc(s_one, 1)
                pool.wait_ge(s_one, 1)
                nc.gpsimd.memset(cL[HD:P].bitcast(F32), 1.0).then_inc(s_one, 1)
                pool.wait_ge(s_one, 2)
                nc.gpsimd.memset(cB[0:HD], 1.0).then_inc(s_one, 1)
                pool.wait_ge(s_one, 3)
                for t in range(NT):
                    pool.wait_ge(s_ss, 2 + 2 * (t + 1))
                    rstd(steps, ro[:, t], sso[:, t], HD).then_inc(s_ro, 1)
            if stage >= 8:
                pre_pool(pool, steps, 7)

        @block.scalar
        def _(act):
            act.wait_ge(s_gT, 1)
            nc.scalar.copy(gA[:], ps[:, Y, 0:96]).then_inc(s_gev, 1)
            act.wait_ge(s_gev, 1)
            xt_act(act, 0, gainA(0, 0))
            for i in range(2):
                act.wait_ge(s_dma[i], DMA2)
                nc.scalar.copy(whi[:, i], raw[:, i]).then_inc(s_hi, 1)
            act.wait_ge(s_gT, 2)
            nc.scalar.copy(gB[:], ps[:, Y + 1, 0:B_END]).then_inc(s_gev, 1)
            act.wait_ge(s_x, 32)
            pre_act(act, 0)
            for i in range(2, RING):
                act.wait_ge(s_dma[i], DMA2)
                nc.scalar.copy(whi[:, i], raw[:, i]).then_inc(s_hi, 1)
            ffn_act(act, 0, n["f0"], 0)
            post_act(act, 0, 1, n["f0"] + 65)

            def qkv_act(m, n0, r):
                for e in range(5):
                    tops_act(act, n0 + UP * e)
                    evac_act(act, m, n0, e, r, IN_ORDER)
                if m == 0 and stage >= 5:
                    act.wait_ge(s_scr, 16)
                qT_act(act, m)
                tops_act(act, n0 + UP * 5)
                kT_act(act, m)
                evac_act(act, m, n0, 5, r, IN_ORDER)

            if stage >= 2:
                xt_act(act, 1, gainA(0, 2))
                pre_act(act, 1)
                act.wait_ge(s_lsum, 1)
                nc.scalar.activation(lam[:, 2:4], lam[:, 0:2], ACT.Exp).then_inc(s_lexp, 1)
                qkv_act(0, n["qkv0"], 1)
                attn_act(act, 0, "diff")
                act.wait_ge(s_sub, 1)
                xt_act(act, 2, gain_sub)
                for j in range(6):
                    hi(act, n["out0"] + RING + j)
                post_act(act, 1, 2, n["out0"] + 7)
            if stage >= 3:
                xt_act(act, 3, gainA(0, 4))
                pre_act(act, 2)
                ffn_act(act, 1, n["f1"], 2)
                post_act(act, 2, 3, n["f1"] + 65)
            if stage >= 4:
                xt_act(act, 4, gainA(1, 0))
                pre_act(act, 3)
                ffn_act(act, 2, n["f2"], 3)
                post_act(act, 3, 4, n["f2"] + 65)
            if stage >= 5:
                xt_act(act, 5, gainA(1, 2))
                pre_act(act, 4)
                qkv_act(1, n["qkv1"], 4)
                attn_act(act, 1, "na")
                xt_act(act, 6, None)
                for j in range(6):
                    hi(act, n["out1"] + RING + j)
                post_act(act, 4, 5, n["out1"] + 7)
            if stage >= 6:
                xt_act(act, 7, gainA(1, 4))
                pre_act(act, 5)
                ffn_act(act, 3, n["f3"], 5)
                post_act(act, 5, 6, n["f3"] + 65)
            if stage >= 7:
                n0, ng = n["qkv2"], n["gates"]
                xt_act(act, 8, gainB(B_ATTN))
                pre_act(act, 6)
                act.wait_ge(s_wf, 16)
                nc.scalar.copy(wfh[:], wf[:]).then_inc(s_wfh, 1)
                for e in range(4):
                    tops_act(act, n0 + UP * e)
                    evac_act(act, 2, n0, e, 6, B2_ORDER)
                act.wait_ge(s_qa, 16)
                act.wait_ge(s_qv, 16)
                for k in range(4):
                    if k == 3:
                        act.wait_ge(s_ss, 3)
                    nc.scalar.activation(sq4[k], qkv[:, k // 2, (k % 2) * 1536:(k % 2) * 1536 + D],
                                         ACT.Square).then_inc(s_sq, 1)
                tops_act(act, n0 + UP * 4)
                evac_act(act, 2, n0, 4, 6, B2_ORDER)
                tops_act(act, n0 + UP * 5)
                evac_act(act, 2, n0, 5, 6, B2_ORDER)
                act.wait_ge(s_fv, 2)
                nc.scalar.activation(lf[:, 1], lf[:, 1], ACT.Exp, scale=-1.0).then_inc(s_fe, 1)
                act.wait_ge(s_fe, 1)
                nc.scalar.activation(lf[:, 1], lf[:, 1], ACT.Ln, bias=1.0).then_inc(s_fe, 1)
                tops_act(act, ng)
                act.wait_ge(s_fc, 1)
                nc.scalar.copy(cH, ps[:, Y, 0:S]).then_inc(s_fh, 1)
                tops_act(act, ng + UP)
                qT_act(act, 2)
                tops_act(act, ng + 2 * UP)
                kT_act(act, 2)
                tops_act(act, ng + 3 * UP)
                attn_act(act, 2, "b2")
                xt_act(act, 9, None)
                act.wait_ge(s_g, 8)
                for g in (1, 0):
                    nc.scalar.activation(gates[:, :, g * D:(g + 1) * D], gates[:, :, g * D:(g + 1) * D],
                                         ACT.Sigmoid).then_inc(s_sg, 1)
                for j in range(8):
                    hi(act, n["brb"] + RING + j)
                xt_act(act, 10, None)
                for j in range(8):
                    hi(act, n["out2"] + RING + j)
            if stage >= 8:
                xt_act(act, 11, gainB(B_FFN))
                pre_act(act, 7)
                conv_ffn_act(act)

        @block.vector
        def _(dve):
            steps = Steps(dve, s_v)
            dve.sem_inc(s_lo, RING)
            dve.wait_ge(s_gev, 1)
            xt_dve(dve, 0, gainA(0, 0))
            for i in range(RING):
                dve.wait_ge(s_hi, i + 1)
                nc.vector.tensor_tensor(wlo[:, i], raw[:, i], whi[:, i].bitcast(F32), ALU.subtract).then_inc(s_lo, 1)
            dve.wait_ge(s_cst, 16)
            dve.wait_ge(s_cst2, 16)
            dve.wait_ge(s_rx, 1)
            ffn_dve(dve, 0, n["f0"])
            post_dve(dve, steps, 0, n["f0"] + 65)

            def qkv_dve(m, n0, r, rotate):
                for e in range(4):
                    tops_dve(dve, n0 + UP * e)
                    evac_dve(dve, m, n0, e, r, IN_ORDER)
                if rotate:
                    dve.wait_ge(s_qa, 6 * m + 4)
                    dve.wait_ge(s_qv, 6 * m + 4)
                    if stage >= 5:
                        dve.wait_ge(s_scr, 16)
                    rope_dve(dve, steps, 0, 32)
                tops_dve(dve, n0 + UP * 4)
                evac_dve(dve, m, n0, 4, r, IN_ORDER)
                tops_dve(dve, n0 + UP * 5)
                kT_dve(dve, m)
                evac_dve(dve, m, n0, 5, r, IN_ORDER)

            if stage >= 2:
                xt_dve(dve, 1, gainA(0, 2), n["f0"] + 65 + RING)
                dve.wait_ge(s_lam, 16)
                steps.done(nc.vector.tensor_tensor(lamp[:], lamv[:].rearrange("p (a b) c -> p a b c", b=2)[:, :, 0],
                                                   lamv[:].rearrange("p (a b) c -> p a b c", b=2)[:, :, 1], ALU.mult))
                nc.vector.tensor_reduce(lam[:, 0:2], lamp[:], AX_X, ALU.add).then_inc(s_lsum, 1)
                dve.wait_ge(s_lexp, 1)
                steps.done(nc.vector.tensor_tensor(lam[:, 5:6], lam[:, 3:4], lam[:, 2:3], ALU.subtract))
                steps.done(nc.vector.tensor_scalar(lam[:, 4:5], lam[:, 5:6], -LAM_INIT, None, ALU.add))
                dve.wait_ge(s_gev, 2)
                nc.vector.tensor_scalar(gB[:, B_SUB:B_SUB + 1], gB[:, B_SUB:B_SUB + 1], 1.0 - LAM_INIT, None,
                                        ALU.mult).then_inc(s_sub, 1)
                qkv_dve(0, n["qkv0"], 1, True)
                attn_dve(dve, steps, 0, "diff")
                xt_dve(dve, 2, gain_sub)
                for j in range(6):
                    lo(dve, n["out0"] + RING + j)
                post_dve(dve, steps, 1, n["out0"] + 7)
            if stage >= 3:
                xt_dve(dve, 3, gainA(0, 4), n["out0"] + 7 + RING)
                dve.wait_ge(s_rx, 3)
                ffn_dve(dve, 1, n["f1"])
                post_dve(dve, steps, 2, n["f1"] + 65)
            if stage >= 4:
                xt_dve(dve, 4, gainA(1, 0), n["f1"] + 65 + RING)
                dve.wait_ge(s_rx, 4)
                ffn_dve(dve, 2, n["f2"])
                post_dve(dve, steps, 3, n["f2"] + 65)
            if stage >= 5:
                xt_dve(dve, 5, gainA(1, 2), n["f2"] + 65 + RING)
                qkv_dve(1, n["qkv1"], 4, False)
                dve.wait_ge(s_nar, 2)
                attn_dve(dve, steps, 1, "na")
                xt_dve(dve, 6, None)
                for j in range(6):
                    lo(dve, n["out1"] + RING + j)
                post_dve(dve, steps, 4, n["out1"] + 7)
            if stage >= 6:
                xt_dve(dve, 7, gainA(1, 4), n["out1"] + 7 + RING)
                dve.wait_ge(s_rx, 6)
                ffn_dve(dve, 3, n["f3"])
                post_dve(dve, steps, 5, n["f3"] + 65)
            if stage >= 7:
                n0, ng = n["qkv2"], n["gates"]
                xt_dve(dve, 8, gainB(B_ATTN), n["f3"] + 65 + RING)
                nc.vector.tensor_copy(identr, ident).then_inc(s_idr, 1)
                nc.vector.tensor_copy(causr, caus).then_inc(s_idr, 1)
                dve.wait_ge(s_wfh, 1)
                nc.vector.tensor_tensor(wfl[:], wf[:], wfh[:].bitcast(F32), ALU.subtract).then_inc(s_wfl, 1)
                for e in range(4):
                    tops_dve(dve, n0 + UP * e)
                    evac_dve(dve, 2, n0, e, 6, B2_ORDER)

                def head_scale(t):
                    dve.wait_ge(s_ro, 2 + t + 1)
                    for half in range(2):
                        v = qkv[:, t, half * 1536:half * 1536 + D].rearrange("p (g c) -> p g c", c=HD)
                        steps.done(nc.vector.tensor_tensor(
                            v, v, ro[:, t, half * 16:(half + 1) * 16].unsqueeze(2).broadcast_to([P, 16, HD]), ALU.mult))
                        for w in range(2):
                            vv = v[:, 8 * w:8 * w + 8]
                            steps.done(nc.vector.tensor_tensor(
                                vv, vv, qkg[:, 2 * half + w].unsqueeze(1).broadcast_to([P, 8, HD]), ALU.mult))

                def gate_logits(c):
                    dve.wait_ge(s_used, used(ng + UP * c + 3))
                    for t in range(NT):
                        nc.vector.scalar_tensor_tensor(out=gates[:, t, c * 512:(c + 1) * 512],
                                                       in0=ps[:, Z + 2 * (c % 2) + t], scalar=rx[:, t:t + 1],
                                                       in1=bgate[:, c * 512:(c + 1) * 512], op0=ALU.mult,
                                                       op1=ALU.add).then_inc(s_g, 1)

                for k in range(4):
                    dve.wait_ge(s_sq, 2 + k + 1)
                    nc.vector.tensor_reduce(sso[:, k // 2, (k % 2) * 16:(k % 2 + 1) * 16],
                                            sq4[k].rearrange("p (g c) -> p g c", c=HD), AX_X, ALU.add).then_inc(s_ss, 1)
                tops_dve(dve, n0 + UP * 4)
                evac_dve(dve, 2, n0, 4, 6, B2_ORDER)
                dve.wait_ge(s_b2, 80)
                head_scale(0)
                tops_dve(dve, n0 + UP * 5)
                evac_dve(dve, 2, n0, 5, 6, B2_ORDER)
                dve.wait_ge(s_fz, 1)
                for t in range(NT):
                    steps.done(nc.vector.scalar_tensor_tensor(out=lf[:, 0, t], in0=ps[:, Y, t * 8:t * 8 + 8],
                                                              scalar=rx[:, t:t + 1], in1=bfg[:], op0=ALU.mult, op1=ALU.add))
                nc.vector.tensor_scalar(lf[:, 2], lf[:, 0], 0.0, None, ALU.min).then_inc(s_fv, 1)
                dve.wait_ge(s_fv, 1)
                nc.vector.scalar_tensor_tensor(out=lf[:, 1], in0=lf[:, 2], scalar=-2.0, in1=lf[:, 0],
                                               op0=ALU.mult, op1=ALU.add).then_inc(s_fv, 1)
                head_scale(1)
                dve.wait_ge(s_fe, 2)
                dve.wait_ge(s_one, 3)
                nc.vector.tensor_tensor(lf4.rearrange("p t (g c) -> p t g c", g=4)[:, :, :, 0:8],
                                        lf[:, 2].unsqueeze(2).broadcast_to([P, NT, 4, 8]),
                                        lf[:, 1].unsqueeze(2).broadcast_to([P, NT, 4, 8]), ALU.subtract).then_inc(s_fv, 1)
                tops_dve(dve, ng)
                dve.wait_ge(s_aux2, 16)
                gate_logits(0)
                rope_dve(dve, steps, 0, 16)
                dve.wait_ge(s_fh, 1)
                steps.done(nc.vector.tensor_copy(cL[0:32], cH[0:32].bitcast(F32)))
                steps.done(nc.vector.tensor_tensor(cL[32:64], ps[32:64, Y, 0:S], cH[32:64].bitcast(F32), ALU.subtract))
                steps.done(nc.vector.tensor_scalar(cB[64:96], cH[64:96].bitcast(F32), -1.0, None, ALU.mult))
                nc.vector.tensor_tensor(cB[96:128], cH[96:128].bitcast(F32), ps[96:128, Y, 0:S], ALU.subtract).then_inc(s_fcv, 1)
                tops_dve(dve, ng + UP)
                gate_logits(1)
                tops_dve(dve, ng + 2 * UP)
                kT_dve(dve, 2)
                gate_logits(2)
                tops_dve(dve, ng + 3 * UP)
                gate_logits(3)
                dve.wait_ge(s_fcv, 1)
                nc.vector.tensor_tensor(cR[:], cB.unsqueeze(1).broadcast_to([P, 8, S]),
                                        head_row.unsqueeze(2).broadcast_to([P, 8, S]), ALU.mult).then_inc(s_fr, 1)
                attn_dve(dve, steps, 2, "b2")
                xt_dve(dve, 9, None)
                for j in range(4):
                    lo(dve, n["brb"] + RING + j)
                dve.wait_ge(s_used, used(n["brb"] + 3))
                dve.wait_ge(s_sg, 2)
                for t in range(NT):
                    steps.done(nc.vector.tensor_tensor(osb[:, t], gates[:, t, D:2 * D], bank(Z + 2 * t), ALU.mult))
                for j in range(2):
                    lo(dve, n["bra"] + RING + j)
                dve.wait_ge(s_yt, 7)
                for t in range(NT):
                    if t:
                        dve.wait_ge(s_used, used(n["bra"] + 3))
                    steps.done(nc.vector.tensor_tensor(sqa[:], gates[:, t, 0:D], bank(Y + 2 * t), ALU.mult))
                    nc.vector.tensor_tensor(osb[:, t], osb[:, t], sqa[:], ALU.add).then_inc(s_src, 1)
                    dve.wait_ge(s_src, 18 + t + 1)
                lo(dve, n["bra"] + RING + 2)
                xt_dve(dve, 10, None, n["bra"] + RING + 3)
                for j in range(6):
                    lo(dve, n["out2"] + RING + j)
                add_dve(dve, 8, n["out2"] + 7)
                lo(dve, n["out2"] + RING + 6)
            if stage >= 8:
                xt_dve(dve, 11, gainB(B_FFN), n["out2"] + RING + 7)
                conv_ffn_dve(dve, steps)

        @block.tensor
        def _(pe):
            pe.sem_inc(s_used, RING)
            pe.wait_ge(s_cst, 16)
            pe.wait_ge(s_rows, 16)
            nc.tensor.transpose(ps[:, Y, 0:96], rowsA, ident[0:96, 0:96]).then_inc(s_gT, 1)
            pe.wait_ge(s_x, 32)
            xt_pe(pe, 0, h)
            pe.wait_ge(s_rowsB, 80)
            nc.tensor.transpose(ps[:, Y + 1, 0:B_END], rowsB, ident[0:B_END, 0:B_END]).then_inc(s_gT, 1)
            ffn_pe(pe, 0, n["f0"], 0)

            def qkv_pe(m, n0, r, kind):
                for e in range(5):
                    chunk_pe(pe, m, n0, e, range(UP), r if e == 0 else None)
                if kind == "diff":
                    pe.wait_ge(s_qr, 1)
                    pe.wait_ge(s_cst2, 16)
                pe.wait_ge(s_qa, 6 * m + 4)
                pe.wait_ge(s_qv, 6 * m + 4)
                qk_turn(pe, m, kind, 0)
                chunk_pe(pe, m, n0, 5, range(2))
                qk_turn(pe, m, kind, 1)
                chunk_pe(pe, m, n0, 5, range(2, UP))

            if stage >= 2:
                xt_pe(pe, 1, h)
                qkv_pe(0, n["qkv0"], 1, "diff")
                attn_pe(pe, 0, "diff")
                xt_pe(pe, 2, o_sb)
                proj_pe(pe, n["out0"], 2, 8, Y)
            if stage >= 3:
                xt_pe(pe, 3, h)
                ffn_pe(pe, 1, n["f1"], 3)
            if stage >= 4:
                xt_pe(pe, 4, h)
                ffn_pe(pe, 2, n["f2"], 4)
            if stage >= 5:
                xt_pe(pe, 5, h)
                qkv_pe(1, n["qkv1"], 5, "na")
                attn_pe(pe, 1, "na")
                xt_pe(pe, 6, o_sb, reverse=True)
                proj_pe(pe, n["out1"], 6, 8, Y)
            if stage >= 6:
                xt_pe(pe, 7, h)
                ffn_pe(pe, 3, n["f3"], 7)
            if stage >= 7:
                n0, ng = n["qkv2"], n["gates"]

                def gate_pe(c, units):
                    if c < 2:
                        pe.wait_ge(s_qa, 17 + c)
                        pe.wait_ge(s_qv, 17 + c)
                    else:
                        pe.wait_ge(s_g, 2 * (c - 1))
                    for j in units:
                        col_unit(pe, ng + UP * c + j, 0, j, [Z + 2 * (c % 2), Z + 2 * (c % 2) + 1])

                xt_pe(pe, 8, h)
                for e in range(5):
                    chunk_pe(pe, 2, n0, e, range(UP), 8 if e == 0 else None)
                pe.wait_ge(s_wfl, 1)
                for t in range(NT):
                    c = slice(t * P, (t + 1) * P)
                    o = ps[:, Y, t * 8:t * 8 + 8]
                    for k in range(KT):
                        nc.tensor.matmul(o, xhi[:, k, c], wfh[:, k], start=k == 0, stop=False)
                        nc.tensor.matmul(o, xhi[:, k, c], wfl[:, k], start=False, stop=False)
                        ins = nc.tensor.matmul(o, xlo[:, k, c], wfh[:, k], start=False, stop=k == KT - 1)
                ins.then_inc(s_fz, 1)
                chunk_pe(pe, 2, n0, 5, range(UP))
                gate_pe(0, range(UP))
                pe.wait_ge(s_fv, 3)
                for t in range(NT):
                    ins = nc.tensor.matmul(ps[:, Y, 0:S], lf4[:, t], tri[:, t], start=t == 0, stop=t == NT - 1)
                ins.then_inc(s_fc, 1)
                gate_pe(1, range(UP))
                pe.wait_ge(s_qr, 2)
                pe.wait_ge(s_fcv, 1)
                qk_turn(pe, 2, "b2", 0)
                gate_pe(2, range(2))
                qk_turn(pe, 2, "b2", 1)
                gate_pe(2, range(2, UP))
                gate_pe(3, range(UP))
                attn_pe(pe, 2, "b2")
                xt_pe(pe, 9, o_sb)
                pe.wait_ge(s_xl, 40)
                proj_pe(pe, n["brb"], 9, 4, Z, 4, early=False)
                proj_pe(pe, n["bra"], 9, 4, Y, 0)
                xt_pe(pe, 10, osb)
                proj_pe(pe, n["out2"], 10, 8, Y)
            if stage >= 8:
                xt_pe(pe, 11, h)
                conv_ffn_pe(pe)


def constants():
    import numpy as np
    c = np.zeros((P, C_END), np.float32)
    c[:, C_ID:C_ID + P] = np.eye(P, dtype=np.float32)
    half = 8
    inv = np.float32(500000.0) ** (-np.arange(0, 16, 2, dtype=np.float32) / np.float32(16))
    ang = np.arange(S, dtype=np.float32)[:, None] * inv[None, :].astype(np.float32)
    cos, sin = np.cos(ang).astype(np.float32), np.sin(ang).astype(np.float32)
    table = np.concatenate([cos, cos, -sin, sin], axis=1).reshape(NT, P, 4 * half)
    for t in range(NT):
        c[:, C_ROPE + 32 * t:C_ROPE + 32 * (t + 1)] = table[t]
    q = np.arange(P)
    c[:, C_FLIP:C_FLIP + P] = (q[:, None] // GW == q[None] // GW) & (q[:, None] % GW == GW - 1 - q[None] % GW)
    start = np.clip(GW - 1 - q % GW - 8, 0, GW - 16)
    k = np.arange(GW)
    c[:, C_WIN:C_WIN + GW] = np.where((k[None] >= start[:, None]) & (k[None] < start[:, None] + 16), 0.0, MASKED)
    c[:, C_CAUS:C_CAUS + P] = np.where(q[None] <= q[:, None], 0.0, MASKED)
    s = np.arange(S)
    for t in range(NT):
        c[:, C_TRI + S * t:C_TRI + S * (t + 1)] = (q[:, None] + t * P <= s[None])
    c[:, C_HEAD:C_HEAD + 8] = q[:, None] % 32 == np.arange(8)[None]
    return c


_INS = ['x', 'norm_g', 'ffn1_wg', 'ffn1_wu', 'ffn1_wd', 'ffn2_wg', 'ffn2_wu', 'ffn2_wd', 'diff_w_in', 'diff_w_out',
        'diff_lambda', 'diff_subln', 'na_w_in', 'na_w_out', 'na_rpb', 'attn_norm_g_2', 'w_in_2', 'b_forget_2',
        'b_gate_2', 'moba_q_norm_g_2', 'moba_k_norm_g_2', 'fox_q_norm_g_2', 'fox_k_norm_g_2',
        'w_branch_moba_2', 'w_branch_fox_2', 'w_out_2', 'ffn_norm_g_2', 'w_ffn_up_2', 'ffn_conv_w_2',
        'ffn_conv_b_2', 'w_ffn_down_2']
_OUTS = [((1, S, D), 'float32')]


def kernel(**inputs):
    import numpy as _np
    import concourse.bacc as _bacc
    from concourse import mybir as _mybir
    from concourse.bass_utils import run_bass_kernel_spmd as _run

    nc = _bacc.Bacc("TRN2", target_bir_lowering=False, num_devices=1)
    arrays, args = {}, []
    given = [(name, _np.ascontiguousarray(inputs[name])) for name in _INS]
    given.append(("const_pack", constants()))
    for name, a in given:
        arrays[f"in_{name}_dram"] = a
        args.append(nc.dram_tensor(f"in_{name}_dram", a.shape, _mybir.dt.from_np(a.dtype), kind="ExternalInput").ap())
    for i, (shape, dtype) in enumerate(_OUTS):
        dt = _mybir.dt.from_np(_np.dtype(dtype))
        args.append(nc.dram_tensor(f"out_{i}_dram", shape, dt, kind="ExternalOutput").ap())
    build(nc, *args)
    r = _run(nc, [arrays], core_ids=[0])
    got = tuple(r.results[0][f"out_{i}_dram"] for i in range(len(_OUTS)))
    return got[0]
```

```python
from contextlib import ExitStack

import concourse.bass as bass
from concourse import mybir

F32 = mybir.dt.float32
F32R = mybir.dt.float32r
ALU = mybir.AluOpType
ACT = mybir.ActivationFunctionType
AX_X = mybir.AxisListType.X

P = 128
S = 256
NT = S // P
D = 1024
KT = D // P
F = 2816
FC = 256
NCH = F // FC
FT = F // P
RING = 6
DMA2 = 32
UP = KT // 2
EPS = 1e-6
LAM_INIT = 0.8 - 0.6 * 1.0
HD = 64
GW = 64
GR = S // GW
NAH = 16
MASKED = -1e30
TAPS = 3

C_ID, C_ROPE, C_WIN, C_CAUS, C_TRI, C_FLIP, C_HEAD, C_END = 0, 128, 192, 256, 384, 896, 1024, 1032
B_ATTN, B_FFN, B_SUB, B_CONV, B_END = 0, 8, 16, 17, 17 + 4 * 22


def build(nc, x, norm_g, ffn1_wg, ffn1_wu, ffn1_wd, ffn2_wg, ffn2_wu, ffn2_wd, diff_w_in, diff_w_out,
          diff_lambda, diff_subln, na_w_in, na_w_out, na_rpb, attn_norm_g_2, w_in_2, b_forget_2,
          b_gate_2, moba_q_norm_g_2, moba_k_norm_g_2, fox_q_norm_g_2, fox_k_norm_g_2,
          w_branch_moba_2, w_branch_fox_2, w_out_2, ffn_norm_g_2, w_ffn_up_2, ffn_conv_w_2,
          ffn_conv_b_2, w_ffn_down_2, const_pack, out):
    ctx = ExitStack()
    with ctx:
        def sb(name, shape, dt=F32):
            return ctx.enter_context(nc.sbuf_tensor(name, shape, dt))

        def sem(name):
            return ctx.enter_context(nc.semaphore(name))

        raw = sb("raw", [P, RING, 2, 512])
        whi = sb("whi", [P, RING, 2, 512], F32R)
        wlo = sb("wlo", [P, RING, 2, 512], F32R)
        h = sb("h", [P, NT, D])
        xhi = sb("xhi", [P, KT, S], F32R)
        xlo = sb("xlo", [P, KT, S], F32R)
        thi = sb("thi", [P, 2, S], F32R)
        tlo = sb("tlo", [P, 2, S], F32R)
        qkv = sb("qkv", [P, NT, 3 * D])
        qT = sb("qT", [P, KT, S])
        kT = sb("kT", [P, KT, S])
        osb = sb("osb", [P, NT, D])
        kT1 = osb[:].rearrange("p t (k s) -> p (t k) s", s=S)
        sqa = sb("sqa", [P, D])
        aux = sb("aux", [P, 8192])
        gpost = sb("gpost", [P, D])
        ex = sb("ex", [P, 3, 2, S])
        aT = sb("aT", [P, 2, 4, P])
        cst = sb("cst", [P, C_END])
        rowsA = sqa[0:96, 0:P]
        rowsB = sqa[0:B_END, P:2 * P]
        o_sb = qkv[:, :, 0:D]
        gA = sb("gA", [P, 96])
        gB = sb("gB", [P, B_END])
        qkg = sb("qkg", [P, 4, HD])
        lamv = sb("lamv", [P, 4, HD])
        lamp = sb("lamp", [P, 2, HD])
        lam = sb("lam", [P, 8])
        nh = sb("nh", [P, 32])
        ssx = sb("ssx", [P, NT])
        rx = sb("rx", [P, NT])
        ssy = sb("ssy", [P, NT, 2])
        ry = sb("ry", [P, NT])
        sso = sb("sso", [P, NT, 32])
        ro = sb("ro", [P, NT, 32])
        nmx = sb("nmx", [P, 2, 2])
        rs = sb("rs", [P, NT, 16])
        ri = sb("ri", [P, NT, 16])
        wf = sb("wf", [P, KT, 8])
        wfx = sb("wfx", [P, KT, 16], F32R)
        bfg = sb("bfg", [P, 8])
        lf = sb("lf", [P, 3, NT, 8])
        lf4 = aux[:, 6144:6144 + NT * P].rearrange("p (t c) -> p t c", t=NT)
        cB = aux[:, 6144 + S:6144 + 2 * S]
        cH = thi[:, 0]
        cL = thi[:, 1]
        cR = xlo
        identr = tlo[:, 0, 0:P]
        causr = tlo[:, 0, P:2 * P]
        wgt = sb("wgt", [P, 2])
        cw = sb("cw", [P, 4, 2])

        ident = cst[:, C_ID:C_ID + P]
        rope = cst[:, C_ROPE:C_ROPE + 64].rearrange("p (t c) -> p t c", t=NT)
        win = cst[:, C_WIN:C_WIN + GW]
        flip = cst[:, C_FLIP:C_FLIP + P]
        caus = cst[:, C_CAUS:C_CAUS + P]
        tri = cst[:, C_TRI:C_TRI + 2 * S].rearrange("p (t c) -> p t c", t=NT)
        silu = qkv[:, 0, 0:512].rearrange("p (t c) -> p t c", t=NT)
        hs = qkv[:, 0, 512:1024].rearrange("p (t c) -> p t c", t=NT)
        ug = qkv[:, 0, 1024:2048].rearrange("p (t c) -> p t c", t=NT)
        cv0 = qkv[:, 1, 0:512].rearrange("p (f c) -> p f c", f=2)
        cv1 = qkv[:, 1, 512:1024].rearrange("p (f c) -> p f c", f=2)
        cv2 = qkv[:, 1, 1024:1536].rearrange("p (f c) -> p f c", f=2)
        nab = aux[:, :].rearrange("p (t h c) -> p t h c", t=NT, h=NAH)
        gates = aux[:, 0:4096].rearrange("p (t c) -> p t c", t=NT)
        bgate = aux[:, 4096:6144]
        head_row = cst[:, C_HEAD:C_HEAD + 8]
        sq4 = [sqa[:]] + [qT[:, 4 * i:4 * i + 4, :].rearrange("p k c -> p (k c)") for i in range(2)] + [sqa[:]]
        pad = qT[0:120, :, :].rearrange("p k c -> p (k c)")[:, 0:254].rearrange("p (a c) -> p a c", a=2)

        ps = ctx.enter_context(nc.psum_tensor("ps", [P, 8, 512], F32))
        Y, Z = 0, 4

        scratch = nc.dram_tensor("rpb_scratch", (240, 127), F32, kind="Internal").ap()

        s_dma = [sem(f"unit_landed{i}") for i in range(RING)]
        s_hi = sem("hi_done")
        s_lo = sem("lo_done")
        s_used = sem("unit_used")
        s_cst = sem("ident_landed")
        s_cst2 = sem("consts_landed")
        s_rowsB = sem("rowsB_landed")
        s_idr = sem("f32r_consts_ready")
        s_yt = sem("y_bank_done")
        s_x = [sem(f"x_landed{t}") for t in range(NT)]
        s_rows = sem("rows_landed")
        s_nh = sem("half_exponent_set")
        s_gT = sem("gains_transposed")
        s_gev = sem("gains_ready")
        s_gp = sem("post_gain_landed")
        s_src = sem("xt_source_ready")
        s_tr = sem("xt_transposed")
        s_xh = sem("xt_hi")
        s_xl = sem("xt_lo")
        s_ssx = sem("pre_norm_sum")
        s_rx = sem("pre_norm_rstd")
        s_si = sem("silu_done")
        s_hc = sem("hidden_ready")
        s_ht = sem("hidden_transposed")
        s_hth = sem("hidden_hi")
        s_htl = sem("hidden_lo")
        s_ssy = sem("post_norm_sum")
        s_ry = sem("post_norm_rstd")
        s_qa = sem("chunk_evac_act")
        s_qv = sem("chunk_evac_dve")
        s_qr = sem("qkv_ready")
        s_qt = sem("qk_transposed")
        s_qta = sem("qT_ready")
        s_ktv = sem("kT_ready")
        s_kta = sem("kT1_ready")
        s_kz = sem("kT_rest_zero")
        s_sc = sem("scores_done")
        s_mx = sem("max_done")
        s_ex = sem("exp_done")
        s_a = sem("probs_ready")
        s_at = sem("probs_transposed")
        s_ate = sem("probsT_ready")
        s_pv = sem("pv_done")
        s_sq = sem("head_squares")
        s_ss = sem("head_sums")
        s_ro = sem("head_rstd")
        s_v = sem("dve_step")
        s_p = sem("pool_step")
        s_pad = sem("pad_set")
        s_rp = sem("rpb_landed")
        s_scr = sem("scratch_written")
        s_nab = sem("bias_landed")
        s_nar = sem("bias_ready")
        s_lam = sem("lambda_landed")
        s_lsum = sem("lambda_sums")
        s_lexp = sem("lambda_exp")
        s_b2 = sem("block2_small_landed")
        s_aux2 = sem("block2_aux_landed")
        s_wf = sem("forget_weights_landed")
        s_wfh = sem("forget_hi")
        s_wfl = sem("forget_lo")
        s_fz = sem("forget_logits")
        s_fe = sem("forget_act")
        s_fv = sem("forget_dve")
        s_fc = sem("forget_cumsum")
        s_fh = sem("forget_cumsum_hi")
        s_fr = sem("forget_terms_ready")
        s_one = sem("forget_ones_set")
        s_fcv = sem("forget_rows_ready")
        s_sub = sem("sublayer_gain_ready")
        s_g = sem("gate_logits")
        s_sg = sem("gates_ready")
        s_cw = sem("conv_taps")
        s_ug = sem("up_copied")
        s_ut = sem("up_transposed")
        s_c0 = sem("conv_tap2")
        s_c1 = sem("conv_tap1")
        s_cc = sem("conv_hidden")
        s_t1 = sem("conv_tap1_half")
        s_si2 = sem("conv_silu")
        s_out = sem("out_written")

        block = ctx.enter_context(nc.Block())

        def bank(b, t=0, w=2):
            return ps[:, b:b + w, :].rearrange("p b c -> p (b c)")

        def used(n0):
            return RING + n0 + 1

        def slot(n0):
            return n0 % RING

        def load(sp, n0, it, dsts_srcs):
            s = slot(n0)
            sp.wait_ge(s_lo, n0 + 1 + RING * it)
            for dst, src in dsts_srcs(raw[:, s]):
                sp.dma_start(dst, src).then_inc(s_dma[s], 16)

        def hi(act, n0, it=0):
            if isinstance(it, int) and n0 + RING * it >= N_UNITS:
                return
            s = slot(n0)
            act.wait_ge(s_dma[s], DMA2 * (n0 // RING + 1) + DMA2 * it)
            act.wait_ge(s_used, n0 + 1 + RING * it)
            nc.scalar.copy(whi[:, s], raw[:, s]).then_inc(s_hi, 1)

        def lo(dve, n0, it=0):
            if isinstance(it, int) and n0 + RING * it >= N_UNITS:
                return
            s = slot(n0)
            dve.wait_ge(s_hi, n0 + 1 + RING * it)
            nc.vector.tensor_tensor(wlo[:, s], raw[:, s], whi[:, s].bitcast(F32), ALU.subtract).then_inc(s_lo, 1)

        def mm3(outs, ahi, alo, s, i, start, stop):
            last = None
            for t in range(NT):
                c = slice(t * P, (t + 1) * P)
                nc.tensor.matmul(outs[t], ahi[:, c], whi[:, s, i], start=start, stop=False)
                nc.tensor.matmul(outs[t], ahi[:, c], wlo[:, s, i], start=False, stop=False)
                last = nc.tensor.matmul(outs[t], alo[:, c], whi[:, s, i], start=False, stop=stop)
            return last

        def rounded_first(pe, r, ins, s):
            pe.wait_ge(s_xh, 4 * r + 1)
            for i, (k, outs, start) in enumerate(ins):
                for t in range(NT):
                    c = slice(t * P, (t + 1) * P)
                    nc.tensor.matmul(outs[t], xhi[:, k, c], whi[:, s, i], start=start, stop=False)
                    nc.tensor.matmul(outs[t], xhi[:, k, c], wlo[:, s, i], start=False, stop=False)
            pe.wait_ge(s_xl, 4 * r + 1)
            for i, (k, outs, start) in enumerate(ins):
                for t in range(NT):
                    last = nc.tensor.matmul(outs[t], xlo[:, k, t * P:(t + 1) * P], whi[:, s, i], start=False, stop=False)
            last.then_inc(s_used, 1)

        def col_unit(pe, n0, it, j, banks, r=None):
            s = slot(n0)
            pe.wait_ge(s_lo, RING + n0 + 1 + RING * it)
            if r is not None and j == 0:
                outs = [ps[:, b] for b in banks]
                return rounded_first(pe, r, [(0, outs, True), (1, outs, False)], s)
            if r is not None:
                pe.wait_ge(s_xl, 4 * r + j + 1)
            for i in range(2):
                k = 2 * j + i
                last = mm3([ps[:, b] for b in banks], xhi[:, k], xlo[:, k], s, i, k == 0, k == KT - 1)
            last.then_inc(s_used, 1)

        def row_unit(pe, n0, it, ahi, alo, base, start, stop, between=None):
            s = slot(n0)
            pe.wait_ge(s_lo, RING + n0 + 1 + RING * it)
            for i in range(2):
                last = mm3([ps[:, base + i], ps[:, base + 2 + i]], ahi, alo, s, i, start, stop)
                if i == 0 and between is not None:
                    between()
            last.then_inc(s_used, 1)

        def last_rows(pe, n0, acts, base, ready=None):
            for u in range(2):
                pe.wait_ge(s_lo, RING + n0 + u + 1)
            for idx, u in ((0, 0), (1, 0), (0, 1), (1, 1), (2, 0), (2, 1), (3, 0), (3, 1)):
                t, i = idx // 2, idx % 2
                c = slice(t * P, (t + 1) * P)
                ahi, alo = acts[u]
                if idx == 0 and u == 1 and ready is not None:
                    pe.wait_ge(*ready)
                o, w = ps[:, base + idx], slot(n0 + u)
                nc.tensor.matmul(o, ahi[:, c], whi[:, w, i], start=False, stop=False)
                nc.tensor.matmul(o, ahi[:, c], wlo[:, w, i], start=False, stop=False)
                last = nc.tensor.matmul(o, alo[:, c], whi[:, w, i], start=False, stop=u == 1)
                if idx == 3:
                    last.then_inc(s_used, 1)
                elif u == 1:
                    last.then_inc(s_yt, 1)

        def y_bank(eng, yt, last, idx):
            if idx < 3:
                eng.wait_ge(s_yt, 3 * (yt - 1) + idx + 1)
            else:
                eng.wait_ge(s_used, used(last))

        def keep_warm(pe, count, out_):
            for _ in range(count):
                nc.tensor.matmul(out_, ident, ident, start=True, stop=True)

        def xt_pe(pe, r, src, reverse=False, base=Z):
            if base == Y:
                pe.wait_ge(s_src, 4 * r)
            for t in range(NT):
                if r == 0:
                    pe.wait_ge(s_x[t], 16)
                elif t:
                    keep_warm(pe, 6, ps[:, base + 3, P:2 * P])
                for k in range(KT):
                    if r and k % 4 == 0:
                        pe.wait_ge(s_src, 4 * (r - 1) + 2 * t + k // 4 + 1)
                    o = ps[:, base + k // 2, (k % 2) * S + t * P:(k % 2) * S + (t + 1) * P]
                    a = src[:, t, k * P:(k + 1) * P]
                    ins = nc.tensor.matmul(o, a, flip, start=True, stop=True) if reverse else nc.tensor.transpose(o, a, ident)
                    if t == NT - 1 and k % 2 == 1:
                        ins.then_inc(s_tr, 1)
            if r == 0:
                keep_warm(pe, 8, ps[:, Y + 2, 0:P])

        def xt_act(act, r, gain, late=None, base=Z):
            for b in range(4):
                act.wait_ge(s_tr, 4 * r + b + 1)
                if gain is None:
                    ins = nc.scalar.copy(xhi[:, 2 * b:2 * b + 2, :].rearrange("p k c -> p (k c)"), ps[:, base + b])
                else:
                    for i in range(2):
                        ins = nc.scalar.activation(xhi[:, 2 * b + i], ps[:, base + b, i * S:(i + 1) * S], ACT.Copy,
                                                   scale=gain(2 * b + i))
                ins.then_inc(s_xh, 1)
                if b == 1 and late is not None:
                    hi(act, late)

        def xt_dve(dve, r, gain, late=None, base=Z):
            for b in range(4):
                dve.wait_ge(s_xh, 4 * r + b + 1)
                if gain is None:
                    ins = nc.vector.tensor_tensor(xlo[:, 2 * b:2 * b + 2, :].rearrange("p k c -> p (k c)"), ps[:, base + b],
                                                  xhi[:, 2 * b:2 * b + 2, :].rearrange("p k c -> p (k c)").bitcast(F32),
                                                  ALU.subtract)
                else:
                    for i in range(2):
                        ins = nc.vector.scalar_tensor_tensor(
                            out=xlo[:, 2 * b + i], in0=ps[:, base + b, i * S:(i + 1) * S], scalar=gain(2 * b + i),
                            in1=xhi[:, 2 * b + i].bitcast(F32), op0=ALU.mult, op1=ALU.subtract)
                ins.then_inc(s_xl, 1)
                if b in (1, 3) and late is not None:
                    lo(dve, late - (b == 1))

        def gainA(layer, j):
            return lambda k: gA[:, (layer * 6 + j) * KT + k:(layer * 6 + j) * KT + k + 1]

        def gainB(c0):
            return lambda k: gB[:, c0 + k:c0 + k + 1]

        def gain_sub(k):
            return gB[:, B_SUB:B_SUB + 1]

        def pre_act(act, r):
            for t in range(NT):
                nc.scalar.activation(sqa[:], h[:, t], ACT.Square, accum_out=ssx[:, t:t + 1]).then_inc(s_ssx, 1)
                act.wait_ge(s_ssx, 2 * r + t + 1)

        class Steps:
            def __init__(self, eng, s):
                self.eng, self.s, self.n = eng, s, 0

            def done(self, ins):
                ins.then_inc(self.s, 1)
                self.n += 1
                self.eng.wait_ge(self.s, self.n)

        def rstd(steps, out_, ss, n, factor=1.0):
            g = 1.0 / (factor * factor)
            w = out_.shape[-1]
            steps.done(nc.gpsimd.tensor_scalar(out_, ss, g / n, EPS * g, ALU.mult, ALU.add))
            return nc.gpsimd.tensor_tensor(out_, out_, nh[:, 0:w], ALU.pow)

        def pre_pool(pool, steps, r):
            pool.wait_ge(s_ssx, 2 * r + 2)
            rstd(steps, rx[:], ssx[:], D).then_inc(s_rx, 1)

        def post_act(act, q, yt, last, factor):
            for idx in range(4):
                t, i = idx // 2, idx % 2
                y_bank(act, yt, last, idx)
                if idx >= 2:
                    act.wait_ge(s_ssy, 4 * q + idx - 1)
                nc.scalar.activation(sqa[:, i * 512:(i + 1) * 512], ps[:, Y + idx], ACT.Square,
                                     scale=D ** -0.5 / factor, accum_out=ssy[:, t, i:i + 1]).then_inc(s_ssy, 1)
            hi(act, last - 1 + RING)

        def zero_pool(pool, m, r):
            pool.wait_ge(s_rx, r + 1)
            nc.gpsimd.memset(kT[HD:P], 0.0).then_inc(s_kz, 1)
            pool.wait_ge(s_kz, 2 * m + 1)
            nc.gpsimd.memset(kT1[0:HD], 0.0).then_inc(s_kz, 1)
            pool.wait_ge(s_kz, 2 * m + 2)

        def post_pool(pool, steps, q, factor):
            for t in range(NT):
                pool.wait_ge(s_ssy, 4 * q + 2 * t + 2)
                steps.done(nc.gpsimd.tensor_scalar(ry[:, t:t + 1], ssy[:, t, 0:1], ssy[:, t, 1:2], EPS / (factor * factor),
                                                   ALU.add, ALU.add))
                nc.gpsimd.tensor_tensor(ry[:, t:t + 1], ry[:, t:t + 1], nh[:, 0:1], ALU.pow).then_inc(s_ry, 1)

        def post_dve(dve, steps, q, last):
            dve.wait_ge(s_gp, 16 * (q + 1))
            for t in range(NT):
                cols = [slice(0, 512), slice(512, 1024)]
                for i in range(2):
                    dve.wait_ge(s_ssy, 4 * q + 2 * t + i + 1)
                    steps.done(nc.vector.tensor_tensor(osb[:, t, cols[i]], ps[:, Y + 2 * t + i], gpost[:, cols[i]], ALU.mult))
                dve.wait_ge(s_ry, 2 * q + t + 1)
                for i in range(2):
                    nc.vector.scalar_tensor_tensor(out=h[:, t, cols[i]], in0=osb[:, t, cols[i]], scalar=ry[:, t:t + 1],
                                                   in1=h[:, t, cols[i]], op0=ALU.mult, op1=ALU.add).then_inc(s_src, 1)

        def chunks(eng, n0, body):
            more = n0 + 66 < N_UNITS
            with eng.Fori(0, NCH - 1 if more else NCH - 2) as it:
                body(it)
            if not more:
                body(NCH - 2)

        def gu_unit(sp, n0, it, j, c, wg, wu):
            def parts(dst):
                return [(dst[:, :, 0:FC], wg.rearrange("(k p) f -> p k f", p=P)[:, 2 * j:2 * j + 2, bass.ds(c * FC, FC)]),
                        (dst[:, :, FC:2 * FC], wu.rearrange("(k p) f -> p k f", p=P)[:, 2 * j:2 * j + 2, bass.ds(c * FC, FC)])]
            load(sp, n0, it, parts)

        def down_unit(sp, n0, it, w, row):
            def parts(dst):
                return [(dst[:, i], w[bass.ds(row, P), i * 512:(i + 1) * 512]) for i in range(2)]
            load(sp, n0, it, parts)

        def ffn_sp(sp, n0, wg, wu, wd, gain=None):
            for j in range(UP):
                gu_unit(sp, n0 + j, 0, j, 0, wg, wu)
            with sp.Fori(0, NCH - 1) as it:
                for j in range(UP):
                    gu_unit(sp, n0 + 4 + j, it, j, it + 1, wg, wu)
                for j in range(2):
                    down_unit(sp, n0 + 8 + j, it, wd, it * FC + j * P)
            if gain is not None:
                post_gain(sp, gain)
            for j in range(2):
                down_unit(sp, n0 + 64 + j, 0, wd, (NCH - 1) * FC + j * P)

        def gate_up(pe, n0, it, units=range(UP), r=None, base=Z):
            for j in units:
                col_unit(pe, n0 + j, it, j, [base, base + 1], r)

        def ffn_pe_with(pe, f, n0, r, turn, early=False):
            b = 2 * NCH * f
            gate_up(pe, n0, 0, r=r, base=Y + 2)
            gate_up(pe, n0 + 4, 0, range(2))
            turn(0)
            gate_up(pe, n0 + 4, 0, range(2, UP))

            def body(it, start):
                pe.wait_ge(s_htl, b + 2 * it + 2)
                if early and not start:
                    row_unit(pe, n0 + 8, it, thi[:, 0], tlo[:, 0], Y, start, False, lambda: turn(it + 1))
                else:
                    row_unit(pe, n0 + 8, it, thi[:, 0], tlo[:, 0], Y, start, False)
                    turn(it + 1)
                row_unit(pe, n0 + 9, it, thi[:, 1], tlo[:, 1], Y, False, False)
            body(0, True)
            with pe.Fori(1, NCH - 1) as it:
                gate_up(pe, n0 + 4, it)
                body(it, False)
            if early:
                keep_warm(pe, 6, ps[:, Z, 0:P])
            pe.wait_ge(s_htl, b + 2 * NCH - 1)
            last_rows(pe, n0 + 64, [(thi[:, j], tlo[:, j]) for j in range(2)], Y, (s_htl, b + 2 * NCH))

        def rows_used(eng, n0, c, j):
            if isinstance(c, int) and c == 0:
                return
            eng.wait_ge(s_used, used(n0 + 8 + j) - RING + RING * c)

        def ffn_pe(pe, f, n0, r):
            b = NCH * f

            def hidden_t(c):
                pe.wait_ge(s_hc, 2 * b + 2 * c + 2)
                for j in range(2):
                    for t in range(NT):
                        ins = nc.tensor.transpose(ps[:, Z + 2 + j, t * P:(t + 1) * P],
                                                  hs[:, t, j * P:(j + 1) * P], ident)
                ins.then_inc(s_ht, 1)

            ffn_pe_with(pe, f, n0, r, hidden_t)

        def ffn_act(act, f, n0, r):
            b = NCH * f

            def swish(last, base=Z):
                act.wait_ge(s_used, used(last))
                for t in range(NT):
                    nc.scalar.activation(silu[:, t], ps[:, base + t, 0:FC], ACT.Silu, scale=rx[:, t:t + 1]).then_inc(s_si, 1)

            def hidden(c, j):
                if j == 0:
                    act.wait_ge(s_ht, b + c + 1)
                rows_used(act, n0, c, j)
                nc.scalar.copy(thi[:, j], ps[:, Z + 2 + j, 0:S]).then_inc(s_hth, 1)
            for j in range(3):
                hi(act, n0 + RING + j)
            act.wait_ge(s_rx, r + 1)
            swish(n0 + 3, Y + 2)
            hi(act, n0 + RING + 3)
            hidden(0, 0)
            hidden(0, 1)

            def body(it):
                for j in range(3):
                    hi(act, n0 + RING + 4 + j, it)
                swish(n0 + 7 + RING * it)
                hi(act, n0 + RING + 7, it)
                for j in range(2):
                    hidden(it + 1, j)
                    hi(act, n0 + RING + 8 + j, it)
            chunks(act, n0, body)

        def ffn_dve(dve, f, n0):
            b = NCH * f

            def gated(c, base=Z):
                for t in range(NT):
                    dve.wait_ge(s_si, 2 * b + 2 * c + t + 1)
                    nc.vector.scalar_tensor_tensor(out=hs[:, t], in0=ps[:, base + t, FC:2 * FC], scalar=rx[:, t:t + 1],
                                                   in1=silu[:, t], op0=ALU.mult, op1=ALU.mult).then_inc(s_hc, 1)

            def hidden(c, j):
                dve.wait_ge(s_hth, 2 * b + 2 * c + j + 1)
                nc.vector.tensor_tensor(tlo[:, j], ps[:, Z + 2 + j, 0:S], thi[:, j].bitcast(F32),
                                        ALU.subtract).then_inc(s_htl, 1)
            for j in range(3):
                lo(dve, n0 + RING + j)
            gated(0, Y + 2)
            lo(dve, n0 + RING + 3)
            hidden(0, 0)
            hidden(0, 1)

            def body(it):
                for j in range(3):
                    lo(dve, n0 + RING + 4 + j, it)
                gated(it + 1)
                lo(dve, n0 + RING + 7, it)
                for j in range(2):
                    hidden(it + 1, j)
                    lo(dve, n0 + RING + 8 + j, it)
            chunks(dve, n0, body)

        def chunk_sp(sp, n0, w, cols):
            for c, c0 in enumerate(cols):
                for j in range(UP):
                    load(sp, n0 + UP * c + j, 0, lambda dst: [
                        (dst[:, i], w[(2 * j + i) * P:(2 * j + i + 1) * P, c0:c0 + 512]) for i in range(2)])

        def row_sp(sp, n0, w, rows):
            for j in range(rows // P):
                down_unit(sp, n0 + j, 0, w, j * P)

        def chunk_bank(e):
            return Y + 2 if e == 0 else Z + 2 * (e % 2)

        def chunk_pe(pe, m, n0, e, units, r=None):
            if e >= 2:
                pe.wait_ge(s_qa, 6 * m + e - 1)
                pe.wait_ge(s_qv, 6 * m + e - 1)
            for j in units:
                col_unit(pe, n0 + UP * e + j, 0, j, [chunk_bank(e), chunk_bank(e) + 1], r)

        def tops_act(act, n0, units=range(UP)):
            for j in units:
                hi(act, n0 + RING + j)

        def tops_dve(dve, n0, units=range(UP)):
            for j in units:
                lo(dve, n0 + RING + j)

        def evac_act(act, m, n0, e, r, order):
            act.wait_ge(s_used, used(n0 + UP * e + 3))
            if e == 0:
                act.wait_ge(s_rx, r + 1)
            nc.scalar.activation(qkv[:, 0, order[e] * 512:(order[e] + 1) * 512], ps[:, chunk_bank(e)], ACT.Copy,
                                 scale=rx[:, 0:1]).then_inc(s_qa, 1)

        def evac_dve(dve, m, n0, e, r, order):
            dve.wait_ge(s_used, used(n0 + UP * e + 3))
            if e == 0:
                dve.wait_ge(s_rx, r + 1)
            nc.vector.tensor_scalar(qkv[:, 1, order[e] * 512:(order[e] + 1) * 512], ps[:, chunk_bank(e) + 1],
                                    rx[:, 1:2], None, ALU.mult).then_inc(s_qv, 1)

        def proj_pe(pe, n0, r, kts, base, first=0, early=True):
            plain = kts - 2 if early else kts
            for j in range(plain):
                if first + j == 0:
                    pe.wait_ge(s_lo, RING + n0 + 1)
                    rounded_first(pe, r, [(0, [ps[:, base + i], ps[:, base + 2 + i]], True) for i in range(2)], slot(n0))
                    continue
                pe.wait_ge(s_xl, 4 * r + (first + j) // 2 + 1)
                row_unit(pe, n0 + j, 0, xhi[:, first + j], xlo[:, first + j], base, j == 0, j == kts - 1)
            if early:
                pe.wait_ge(s_xl, 4 * r + (first + kts - 1) // 2 + 1)
                last_rows(pe, n0 + plain, [(xhi[:, first + j], xlo[:, first + j]) for j in (plain, plain + 1)], base)

        IN_ORDER = [0, 1, 2, 3, 4, 5]
        B2_ORDER = [0, 1, 3, 4, 2, 5]

        TASKS = [(p, t) for t in range(NT) for p in range(8)]
        NTASK = len(TASKS)
        NEX = 3

        def qk_cols(kind, p):
            if kind == "b2":
                b = 0 if p < 4 else 3 * 512
                return b + (p % 4) * P, b + 512 + (p % 4) * P, b + 1024 + (p % 4) * P
            return p * P, D + p * P, 2 * D + p * P

        def keys(kind, t):
            return t + 1 if kind == "b2" else NT

        def qk_turn(pe, m, kind, which):
            for bk in range(4):
                if which == 1:
                    pe.wait_ge(s_qta, 4 * m + bk + 1)
                for p in (2 * bk, 2 * bk + 1):
                    c0 = qk_cols(kind, p)[which]
                    for t in range(NT):
                        o = ps[:, Y + bk, (p % 2) * S + t * P:(p % 2) * S + (t + 1) * P]
                        a = qkv[:, t, c0:c0 + P]
                        if kind == "na" and which == 0:
                            ins = nc.tensor.matmul(o, a, flip, start=True, stop=True)
                        else:
                            ins = nc.tensor.transpose(o, a, ident)
                ins.then_inc(s_qt, 1)

        def qT_act(act, m):
            for bk in range(4):
                act.wait_ge(s_qt, 8 * m + bk + 1)
                nc.scalar.activation(qT[:, 2 * bk:2 * bk + 2, :].rearrange("p k c -> p (k c)"), ps[:, Y + bk],
                                     ACT.Copy, scale=HD ** -0.5).then_inc(s_qta, 1)

        def kT_act(act, m):
            for bk in range(4):
                act.wait_ge(s_qt, 8 * m + 4 + bk + 1)
                nc.scalar.copy(kT1[HD:P, 2 * bk:2 * bk + 2, :].rearrange("p k c -> p (k c)"),
                               ps[HD:P, Y + bk]).then_inc(s_kta, 1)

        def kT_dve(dve, m):
            for bk in range(4):
                dve.wait_ge(s_qt, 8 * m + 4 + bk + 1)
                nc.vector.tensor_copy(kT[0:HD, 2 * bk:2 * bk + 2, :].rearrange("p k c -> p (k c)"),
                                      ps[0:HD, Y + bk]).then_inc(s_ktv, 1)

        def attn_pe(pe, m, kind, between):
            b = NTASK * m
            pe.wait_ge(s_qta, 4 * (m + 1))
            pe.wait_ge(s_ktv, 4 * (m + 1))
            pe.wait_ge(s_kta, 4 * (m + 1))
            pe.wait_ge(s_kz, 2 * (m + 1))
            if kind == "b2":
                pe.wait_ge(s_idr, 2)
                pe.wait_ge(s_g, 6)
            else:
                pe.wait_ge(s_qa, 6 * m + 5)
                pe.wait_ge(s_qv, 6 * m + 5)

            def scores(i):
                p, t = TASKS[i]
                if i >= 2 and kind == "na":
                    pe.wait_ge(s_mx, b + i - 1)
                elif i >= 2:
                    pe.wait_ge(s_ex, 2 * (b + i - 1))
                w = keys(kind, t) * P
                for c in range(2):
                    o = ps[:, Z + i % 2, c * S:c * S + w]
                    fox = kind == "b2" and p >= 4
                    ins = nc.tensor.matmul(o, qT[:, p, t * P:(t + 1) * P], (kT, kT1)[c][:, p, 0:w], start=True, stop=not fox)
                    if fox:
                        pe.wait_ge(s_fr, (p - 4) // 2 + 1)
                        ins = nc.tensor.matmul(o, cL[:, t * P:(t + 1) * P], cR[:, 2 * (p - 4) + c, 0:w], start=False, stop=True)
                    if kind == "b2":
                        ins = nc.tensor.matmul(ps[:, Z + i % 2, c * S + t * P:c * S + (t + 1) * P], identr, causr,
                                               start=False, stop=True, skip_group_check=True)
                ins.then_inc(s_sc, 1)

            def turn(i):
                p, t = TASKS[i]
                if i == 0:
                    pe.wait_ge(s_qa, 6 * m + 6)
                    pe.wait_ge(s_qv, 6 * m + 6)
                    if kind == "b2":
                        pe.wait_ge(s_g, 8)
                if kind == "diff":
                    pe.wait_ge(s_a, b + i + 1)
                else:
                    pe.wait_ge(s_ex, 2 * (b + i + 1))
                if i >= 2:
                    pe.wait_ge(s_ate, b + i - 1)
                for c in range(1 if kind == "diff" else 2):
                    for st in range(keys(kind, t)):
                        ins = nc.tensor.transpose(ps[:, Z + 2 + i % 2, (2 * c + st) * P:(2 * c + st + 1) * P],
                                                  ex[:, i % NEX, c, st * P:(st + 1) * P], ident)
                ins.then_inc(s_at, 1)

            def pv(i):
                p, t = TASKS[i]
                pe.wait_ge(s_ate, b + i + 1)
                v0 = qk_cols(kind, p)[2]
                n, w = (1, P) if kind == "diff" else (2, HD)
                for c in range(n):
                    for st in range(keys(kind, t)):
                        ins = nc.tensor.matmul(ps[:, Y + 2 * t + p // 4, (p % 4) * P + c * w:(p % 4) * P + (c + 1) * w],
                                               aT[:, i % 2, 2 * c + st], qkv[:, st, v0 + c * w:v0 + (c + 1) * w],
                                               start=st == 0, stop=st == keys(kind, t) - 1)
                ins.then_inc(s_pv, 1)

            for i in range(NTASK + 3):
                between(i)
                if i < NTASK:
                    scores(i)
                if 2 <= i < NTASK + 2:
                    turn(i - 2)
                if i >= 3:
                    pv(i - 3)

        def attn_act(act, m, kind, between):
            b = NTASK * m

            def squares(g):
                act.wait_ge(s_pv, b + 4 * (g + 1))
                if g >= 2:
                    act.wait_ge(s_sq, g - 1)
                for hd in range(4):
                    ins = nc.scalar.activation(sqa[:, (g % 2) * 512 + hd * P:(g % 2) * 512 + (hd + 1) * P],
                                               ps[:, Y + g, hd * P:(hd + 1) * P], ACT.Square,
                                               accum_out=sso[:, g // 2, 4 * (g % 2) + hd:4 * (g % 2) + hd + 1])
                ins.then_inc(s_sq, 1)

            for i in range(NTASK + 2):
                between(i)
                if i >= 2:
                    j = i - 2
                    act.wait_ge(s_at, b + j + 1)
                    if j >= 2:
                        act.wait_ge(s_pv, b + j - 1)
                    n = 1 if kind == "diff" else 2
                    k = keys(kind, TASKS[j][1])
                    src = ps[:, Z + 2 + j % 2].rearrange("p (c s q) -> p c s q", c=2, s=2)
                    dst = aT[:, j % 2].rearrange("p (c s) q -> p c s q", c=2)
                    nc.scalar.copy(dst[:, 0:n, 0:k], src[:, 0:n, 0:k]).then_inc(s_ate, 1)
                if i < NTASK:
                    p, t = TASKS[i]
                    w = keys(kind, t) * P
                    act.wait_ge(s_mx, b + i + 1)
                    if i >= NEX:
                        act.wait_ge(s_at, b + i - 2)
                    src = ex[:, i % NEX] if kind == "na" else ps[:, Z + i % 2].rearrange("p (c k) -> p c k", c=2)
                    for c in range(2):
                        nc.scalar.activation(ex[:, i % NEX, c, 0:w], src[:, c, 0:w], ACT.Exp,
                                             bias=nmx[:, i % 2, c:c + 1],
                                             accum_out=rs[:, t, 2 * p + c:2 * p + c + 1]).then_inc(s_ex, 1)
                if kind == "diff" and i in (8, 12, 16):
                    squares(i // 4 - 2)
            if kind == "diff":
                squares(3)

        def attn_dve(dve, steps, m, kind, between):
            b = NTASK * m

            def head_sums(g):
                t, c = g // 2, slice(4 * (g % 2), 4 * (g % 2) + 4)
                inv2 = slice(8 + c.start, 12 + c.start)
                steps.done(nc.vector.reciprocal(ri[:, t, c], rs[:, t, 8 * (g % 2):8 * (g % 2) + 8:2]))
                steps.done(nc.vector.tensor_tensor(ri[:, t, inv2], ri[:, t, c], ri[:, t, c], ALU.mult))
                dve.wait_ge(s_sq, g + 1)
                nc.vector.tensor_tensor(sso[:, t, c], sso[:, t, c], ri[:, t, inv2], ALU.mult).then_inc(s_ss, 1)

            def head_norm(g):
                t, c = g // 2, 4 * (g % 2)
                dve.wait_ge(s_ro, g + 1)
                steps.done(nc.vector.tensor_tensor(ri[:, t, 8 + c:12 + c], ro[:, t, c:c + 4], ri[:, t, c:c + 4], ALU.mult))
                scaled(g, ri[:, t, 8 + c:12 + c])

            def normal(g):
                t, c = g // 2, slice(8 * (g % 2), 8 * (g % 2) + 8)
                dve.wait_ge(s_pv, b + 4 * (g + 1))
                dve.wait_ge(s_ex, 2 * (b + 4 * (g + 1)))
                steps.done(nc.vector.reciprocal(ri[:, t, c], rs[:, t, c]))
                scaled(g, ri[:, t, c])

            def scaled(g, by):
                n = by.shape[-1]
                nc.vector.tensor_tensor(o_sb[:, g // 2, (g % 2) * 512:(g % 2 + 1) * 512].rearrange("p (g c) -> p g c", g=n),
                                        ps[:, Y + g].rearrange("p (g c) -> p g c", g=n),
                                        by.unsqueeze(2).broadcast_to([P, n, 512 // n]), ALU.mult).then_inc(s_src, 1)

            for i in range(NTASK + 1):
                between(i)
                if i in (3, 4) and kind == "b2":
                    heads = slice(4 * (i - 3), 4 * (i - 2))
                    dve.wait_ge(s_fcv, 1)
                    nc.vector.tensor_tensor(cR[:, heads], cB.unsqueeze(1).broadcast_to([P, 4, S]),
                                            head_row[:, heads].unsqueeze(2).broadcast_to([P, 4, S]), ALU.mult).then_inc(s_fr, 1)
                if i < NTASK:
                    p, t = TASKS[i]
                    w = keys(kind, t) * P
                    dve.wait_ge(s_sc, b + i + 1)
                    sc = ps[:, Z + i % 2].rearrange("p (c k) -> p c k", c=2)[:, :, 0:w]
                    if kind == "na":
                        if i >= NEX:
                            dve.wait_ge(s_at, b + i - 2)
                        steps.done(nc.vector.tensor_tensor(ex[:, i % NEX], sc, nab[:, t, 2 * p:2 * p + 2, :], ALU.add))
                        sc = ex[:, i % NEX]
                    if i >= 2:
                        dve.wait_ge(s_ex, 2 * (b + i - 1))
                    nc.vector.tensor_reduce(nmx[:, i % 2], sc, AX_X, ALU.max, negate=True).then_inc(s_mx, 1)
                if i >= 1 and kind == "diff":
                    j = i - 1
                    p, t = TASKS[j]
                    dve.wait_ge(s_ex, 2 * (b + j + 1))
                    steps.done(nc.vector.reciprocal(wgt[:, 0:1], rs[:, t, 2 * p + 1:2 * p + 2]))
                    steps.done(nc.vector.tensor_scalar(wgt[:, 1:2], rs[:, t, 2 * p:2 * p + 1], wgt[:, 0:1], lam[:, 4:5],
                                                       ALU.mult, ALU.mult))
                    nc.vector.scalar_tensor_tensor(out=ex[:, j % NEX, 0], in0=ex[:, j % NEX, 1], scalar=wgt[:, 1:2],
                                                   in1=ex[:, j % NEX, 0], op0=ALU.mult, op1=ALU.add).then_inc(s_a, 1)
                if kind == "diff" and i in (9, 13, 16):
                    head_sums(i // 4 - 2 if i < 16 else 2)
                if kind == "diff" and i in (11, 15):
                    head_norm(i // 4 - 2)
                if kind != "diff" and i in (8, 12, 16):
                    normal(i // 4 - 2)
            if kind == "diff":
                head_norm(2)
                head_sums(3)
                head_norm(3)
            else:
                normal(3)

        def rope_dve(dve, steps, c0, groups):
            tmp = [qT[:, 0:4, :].rearrange("p k c -> p (k c)")[:, 0:groups * 16].rearrange("p (g c) -> p g c", c=16),
                   qT[:, 4:8, :].rearrange("p k c -> p (k c)")[:, 0:groups * 16].rearrange("p (g c) -> p g c", c=16)]
            for t in range(NT):
                v = qkv[:, t, c0:c0 + groups * HD].rearrange("p (g c) -> p g c", c=HD)
                cos = rope[:, t, 0:16].unsqueeze(1).broadcast_to([P, groups, 16])
                nsin = rope[:, t, 16:24].unsqueeze(1).broadcast_to([P, groups, 8])
                psin = rope[:, t, 24:32].unsqueeze(1).broadcast_to([P, groups, 8])
                steps.done(nc.vector.tensor_tensor(tmp[0], v[:, :, 0:16], cos, ALU.mult))
                steps.done(nc.vector.tensor_tensor(tmp[1][:, :, 0:8], v[:, :, 8:16], nsin, ALU.mult))
                steps.done(nc.vector.tensor_tensor(tmp[1][:, :, 8:16], v[:, :, 0:8], psin, ALU.mult))
                last = nc.vector.tensor_tensor(v[:, :, 0:16], tmp[0], tmp[1], ALU.add)
                if t == 0:
                    steps.done(last)
            last.then_inc(s_qr, 1)

        def add_dve(dve, yt, last):
            for idx in range(4):
                c = slice((idx % 2) * 512, (idx % 2 + 1) * 512)
                y_bank(dve, yt, last, idx)
                nc.vector.tensor_tensor(h[:, idx // 2, c], h[:, idx // 2, c], ps[:, Y + idx], ALU.add).then_inc(s_src, 1)

        def conv_ffn_pe(pe):
            n0 = n["f4"]

            def turn(c):
                pe.wait_ge(s_ug, 2 * c + 2)
                for g in range(2):
                    for j in range(2):
                        for t in range(NT):
                            ins = nc.tensor.transpose(ps[:, Z + 2 + g, j * S + t * P:j * S + (t + 1) * P],
                                                      ug[:, t, g * FC + j * P:g * FC + (j + 1) * P], ident)
                ins.then_inc(s_ut, 1)

            ffn_pe_with(pe, 4, n0, 11, turn, early=True)

        def conv_ffn_act(act):
            n0 = n["f4"]

            def copy_up(last, base=Z):
                act.wait_ge(s_used, used(last))
                for t in range(NT):
                    nc.scalar.activation(ug[:, t], ps[:, base + t], ACT.Copy, scale=rx[:, t:t + 1]).then_inc(s_ug, 1)

            def conv(c):
                act.wait_ge(s_ut, c + 1)
                act.wait_ge(s_cw, c + 1)
                for j in range(2):
                    nc.scalar.activation(cv0[:, j], ps[:, Z + 3, j * S:(j + 1) * S], ACT.Identity,
                                         scale=cw[:, 2, j:j + 1], bias=cw[:, 3, j:j + 1]).then_inc(s_c0, 1)
                for j in range(2):
                    act.wait_ge(s_c1, 2 * c + j + 1)
                    nc.scalar.activation(cv1[:, j], cv0[:, j], ACT.Silu).then_inc(s_si2, 1)

            def hidden(c, j):
                act.wait_ge(s_cc, 2 * c + j + 1)
                rows_used(act, n0, c, j)
                nc.scalar.copy(thi[:, j], cv2[:, j]).then_inc(s_hth, 1)

            act.wait_ge(s_rx, 8)
            for j in range(3):
                hi(act, n0 + RING + j)
            copy_up(n0 + 3, Y + 2)
            hi(act, n0 + RING + 3)
            conv(0)
            hidden(0, 0)
            hidden(0, 1)

            def body(it):
                for j in range(3):
                    hi(act, n0 + RING + 4 + j, it)
                copy_up(n0 + 7 + RING * it)
                hi(act, n0 + RING + 7, it)
                conv(it + 1)
                for j in range(2):
                    hidden(it + 1, j)
                    hi(act, n0 + RING + 8 + j, it)
            chunks(act, n0, body)

        def conv_ffn_dve(dve, steps):
            b, n0 = NCH * 4, n["f4"]
            taps = gB[:, B_CONV:B_END].rearrange("p (k f) -> p k f", k=TAPS + 1)

            def conv(c):
                nc.vector.tensor_copy(cw[:], taps[:, :, bass.ds(2 * c, 2)]).then_inc(s_cw, 1)
                dve.wait_ge(s_cw, c + 1)
                dve.wait_ge(s_c0, 2 * c + 2)
                for j in range(2):
                    nc.vector.scalar_tensor_tensor(out=cv0[:, j, 1:S], in0=ps[:, Z + 3, j * S:(j + 1) * S - 1],
                                                   scalar=cw[:, 1, j:j + 1], in1=cv0[:, j, 1:S],
                                                   op0=ALU.mult, op1=ALU.add).then_inc(s_t1, 1)
                for j in range(2):
                    dve.wait_ge(s_t1, 2 * c + 1 + j)
                    nc.vector.scalar_tensor_tensor(out=cv0[:, j, 2:S], in0=ps[:, Z + 3, j * S:(j + 1) * S - 2],
                                                   scalar=cw[:, 0, j:j + 1], in1=cv0[:, j, 2:S],
                                                   op0=ALU.mult, op1=ALU.add).then_inc(s_c1, 1)
                for j in range(2):
                    dve.wait_ge(s_si2, 2 * c + j + 1)
                    nc.vector.tensor_tensor(cv2[:, j], cv1[:, j], ps[:, Z + 2, j * S:(j + 1) * S], ALU.mult).then_inc(s_cc, 1)

            def hidden(c, j):
                dve.wait_ge(s_hth, 2 * b + 2 * c + j + 1)
                nc.vector.tensor_tensor(tlo[:, j], cv2[:, j], thi[:, j].bitcast(F32), ALU.subtract).then_inc(s_htl, 1)

            for j in range(4):
                lo(dve, n0 + RING + j)
            conv(0)
            hidden(0, 0)
            hidden(0, 1)

            def body(it):
                for j in range(4):
                    lo(dve, n0 + RING + 4 + j, it)
                conv(it + 1)
                for j in range(2):
                    hidden(it + 1, j)
                    lo(dve, n0 + RING + 8 + j, it)
            chunks(dve, n0, body)
            add_dve(dve, 9, n0 + 65)

        n = {}
        at = 0
        for name, count in (("f0", 66), ("qkv0", 24), ("out0", 8), ("f1", 66), ("f2", 66), ("qkv1", 24), ("out1", 8),
                            ("f3", 66), ("qkv2", 24), ("gates", 16), ("bra", 4), ("brb", 4), ("out2", 8), ("f4", 66)):
            n[name] = at
            at += count
        N_UNITS = at
        ffn_w = [(ffn1_wg[0], ffn1_wu[0], ffn1_wd[0]), (ffn2_wg[0], ffn2_wu[0], ffn2_wd[0]),
                 (ffn1_wg[1], ffn1_wu[1], ffn1_wd[1]), (ffn2_wg[1], ffn2_wu[1], ffn2_wd[1])]
        POST = [(0, 1), (0, 3), (0, 5), (1, 1), (1, 3), (1, 5)]
        POST_SRC = [4 * r for r in (1, 3, 4, 5, 7, 8)]
        FINAL_SRC = 4 * 12

        def post_gain(sp, q):
            if q >= 1:
                sp.wait_ge(s_src, POST_SRC[q - 1])
            i, j = POST[q]
            sp.dma_start(gpost[:], norm_g[i, j:j + 1, :].broadcast_to([P, D])).then_inc(s_gp, 16)

        @block.sync
        def _(sp):
            sp.dma_start(cst[:, 0:P], const_pack[:, 0:P]).then_inc(s_cst, 16)
            sp.dma_start(rowsA, norm_g.rearrange("i j (k c) -> (i j k) c", c=P)).then_inc(s_rows, 16)
            for t in range(NT):
                sp.dma_start(h[:, t], x[0, t * P:(t + 1) * P, :]).then_inc(s_x[t], 16)
            ffn_sp(sp, n["f0"], *ffn_w[0], 0)
            chunk_sp(sp, n["qkv0"], diff_w_in[0], [512 * c for c in range(6)])
            post_gain(sp, 1)
            row_sp(sp, n["out0"], diff_w_out[0], D)
            ffn_sp(sp, n["f1"], *ffn_w[1], 2)
            ffn_sp(sp, n["f2"], *ffn_w[2], 3)
            chunk_sp(sp, n["qkv1"], na_w_in[0], [512 * c for c in range(6)])
            post_gain(sp, 4)
            row_sp(sp, n["out1"], na_w_out[0], D)
            ffn_sp(sp, n["f3"], *ffn_w[3], 5)
            chunk_sp(sp, n["qkv2"], w_in_2[0], [512 * c for c in B2_ORDER])
            chunk_sp(sp, n["gates"], w_in_2[0], [3080 + 512 * c for c in range(4)])
            row_sp(sp, n["bra"], w_branch_moba_2[0], 512)
            row_sp(sp, n["brb"], w_branch_fox_2[0], 512)
            row_sp(sp, n["out2"], w_out_2[0], D)
            up = w_ffn_up_2[0]
            ffn_sp(sp, n["f4"], up[:, 0:F], up[:, F:2 * F], w_ffn_down_2[0])
            for idx in range(4):
                t, c = idx // 2, slice((idx % 2) * 512, (idx % 2 + 1) * 512)
                sp.wait_ge(s_src, FINAL_SRC - 3 + idx)
                sp.dma_start(out[0, t * P:(t + 1) * P, c], h[:, t, c]).then_inc(s_out, 16)
            sp.wait_ge(s_out, 64)

        @block.gpsimd
        def _(pool):
            steps = Steps(pool, s_p)
            pool.dma_start(rowsB[B_ATTN:B_ATTN + 8], attn_norm_g_2.rearrange("a (k c) -> (a k) c", c=P)).then_inc(s_rowsB, 16)
            pool.dma_start(rowsB[B_FFN:B_FFN + 8], ffn_norm_g_2.rearrange("a (k c) -> (a k) c", c=P)).then_inc(s_rowsB, 16)
            pool.dma_start(rowsB[B_SUB:B_SUB + 1], diff_subln).then_inc(s_rowsB, 16)
            pool.dma_start(rowsB[B_CONV:B_CONV + 66], ffn_conv_w_2.rearrange("a j (k c) -> (a j k) c", c=P)).then_inc(s_rowsB, 16)
            pool.dma_start(rowsB[B_CONV + 66:B_CONV + 88], ffn_conv_b_2.rearrange("a (k c) -> (a k) c", c=P)).then_inc(s_rowsB, 16)
            pool.dma_start(cst[:, P:], const_pack[:, P:]).then_inc(s_cst2, 16)
            nc.gpsimd.memset(nh[:], -0.5).then_inc(s_nh, 1)
            pool.wait_ge(s_nh, 1)
            pre_pool(pool, steps, 0)
            nc.gpsimd.memset(pad, MASKED).then_inc(s_pad, 1)
            pool.wait_ge(s_pad, 1)
            pool.dma_start(pad[:, :, 48:79], na_rpb[0].rearrange("h d c -> (h d) c").rearrange("(p a) c -> p a c", a=2)).then_inc(s_rp, 16)
            pool.wait_ge(s_rp, 16)
            pool.dma_start(scratch.rearrange("(p a) c -> p a c", a=2), pad).then_inc(s_scr, 16)
            pool.wait_ge(s_scr, 16)
            for r in range(GR):
                t, half = r // 2, r % 2
                for kr in range(GR):
                    src = bass.AP(scratch.tensor, (7 - r + kr) * 127, [[1, GW], [15 * 127, NAH], [1, GW]])
                    dst = nab[half * GW:(half + 1) * GW, t, :, kr * GW:(kr + 1) * GW]
                    if kr % 2 == 0:
                        pool.wait_ge(s_ht, (r * GR + kr) // 2 + 1)
                    pool.dma_start(dst, src).then_inc(s_nab, 16)
            pool.dma_start(lamv[:].rearrange("p a c -> p (a c)"), diff_lambda.rearrange("a b c -> a (b c)").broadcast_to([P, 4 * HD])).then_inc(s_lam, 16)
            for i, g in enumerate((moba_q_norm_g_2, moba_k_norm_g_2, fox_q_norm_g_2, fox_k_norm_g_2)):
                pool.dma_start(qkg[:, i], g.broadcast_to([P, HD])).then_inc(s_b2, 16)
            pool.dma_start(bfg[:], b_forget_2.broadcast_to([P, 8])).then_inc(s_b2, 16)
            pool.dma_start(wf[:], w_in_2[0, :, 3072:3080].rearrange("(k p) c -> p k c", p=P)).then_inc(s_wf, 16)
            post_pool(pool, steps, 0, 0.5)
            pre_pool(pool, steps, 1)
            zero_pool(pool, 0, 1)
            for g in range(4):
                pool.wait_ge(s_ss, g + 1)
                c = slice(4 * (g % 2), 4 * (g % 2) + 4)
                rstd(steps, ro[:, g // 2, c], sso[:, g // 2, c], P).then_inc(s_ro, 1)
            post_pool(pool, steps, 1, 1.0)
            pre_pool(pool, steps, 2)
            post_pool(pool, steps, 2, 0.5)
            pre_pool(pool, steps, 3)
            post_pool(pool, steps, 3, 0.5)
            pre_pool(pool, steps, 4)
            zero_pool(pool, 1, 4)
            pool.wait_ge(s_nab, 16 * GR * GR)
            pool.wait_ge(s_cst2, 16)
            for t in range(NT):
                v = nab[:, t].rearrange("p h (r c) -> p (h r) c", r=GR)
                nc.gpsimd.tensor_tensor(v, v, win.unsqueeze(1).broadcast_to([P, NAH * GR, GW]), ALU.add).then_inc(s_nar, 1)
            post_pool(pool, steps, 4, 1.0)
            pre_pool(pool, steps, 5)
            post_pool(pool, steps, 5, 0.5)
            pool.dma_start(bgate, b_gate_2.rearrange("a b c -> a (b c)").broadcast_to([P, 2 * D])).then_inc(s_aux2, 16)
            pre_pool(pool, steps, 6)
            zero_pool(pool, 2, 6)
            nc.gpsimd.memset(lf4, 0.0).then_inc(s_one, 1)
            pool.wait_ge(s_one, 1)
            nc.gpsimd.memset(cL[HD:P].bitcast(F32), 1.0).then_inc(s_one, 1)
            pool.wait_ge(s_one, 2)
            nc.gpsimd.memset(cB[0:HD], 1.0).then_inc(s_one, 1)
            pool.wait_ge(s_one, 3)
            for t in range(NT):
                pool.wait_ge(s_ss, 4 + 2 * (t + 1))
                rstd(steps, ro[:, t], sso[:, t], HD).then_inc(s_ro, 1)
            pre_pool(pool, steps, 7)

        @block.scalar
        def _(act):
            act.wait_ge(s_gT, 1)
            nc.scalar.copy(gA[:], ps[:, Y, 0:96]).then_inc(s_gev, 1)
            act.wait_ge(s_gev, 1)
            hi(act, 0)
            xt_act(act, 0, gainA(0, 0), 1)
            for i in range(2, 4):
                hi(act, i)
            act.wait_ge(s_gT, 2)
            nc.scalar.copy(gB[:], ps[:, Y + 1, 0:B_END]).then_inc(s_gev, 1)
            for t in range(NT):
                act.wait_ge(s_x[t], 16)
            pre_act(act, 0)
            for i in range(4, RING):
                hi(act, i)
            ffn_act(act, 0, n["f0"], 0)
            post_act(act, 0, 1, n["f0"] + 65, 0.5)

            def qkv_act(m, n0, r):
                for e in range(5):
                    tops_act(act, n0 + UP * e)
                    evac_act(act, m, n0, e, r, IN_ORDER)
                if m == 0:
                    act.wait_ge(s_scr, 16)
                qT_act(act, m)
                tops_act(act, n0 + UP * 5, range(2))
                kT_act(act, m)
                tops_act(act, n0 + UP * 5, range(2, 3))


                def between(i):
                    if i == 2:
                        evac_act(act, m, n0, 5, r, IN_ORDER)
                    if i == 4:
                        tops_act(act, n0 + UP * 5, range(3, UP))
                return between

            xt_act(act, 1, gainA(0, 2), n["f0"] + 65 + RING)
            pre_act(act, 1)
            act.wait_ge(s_lsum, 1)
            nc.scalar.activation(lam[:, 2:4], lam[:, 0:2], ACT.Exp).then_inc(s_lexp, 1)
            attn_act(act, 0, "diff", qkv_act(0, n["qkv0"], 1))
            act.wait_ge(s_sub, 1)
            xt_act(act, 2, gain_sub)
            for j in range(6):
                hi(act, n["out0"] + RING + j)
            post_act(act, 1, 2, n["out0"] + 7, 1.0)
            xt_act(act, 3, gainA(0, 4), n["out0"] + 7 + RING)
            pre_act(act, 2)
            ffn_act(act, 1, n["f1"], 2)
            post_act(act, 2, 3, n["f1"] + 65, 0.5)
            xt_act(act, 4, gainA(1, 0), n["f1"] + 65 + RING)
            pre_act(act, 3)
            ffn_act(act, 2, n["f2"], 3)
            post_act(act, 3, 4, n["f2"] + 65, 0.5)
            xt_act(act, 5, gainA(1, 2), n["f2"] + 65 + RING)
            pre_act(act, 4)
            attn_act(act, 1, "na", qkv_act(1, n["qkv1"], 4))
            xt_act(act, 6, None)
            for j in range(6):
                hi(act, n["out1"] + RING + j)
            post_act(act, 4, 5, n["out1"] + 7, 1.0)
            xt_act(act, 7, gainA(1, 4), n["out1"] + 7 + RING)
            pre_act(act, 5)
            ffn_act(act, 3, n["f3"], 5)
            post_act(act, 5, 6, n["f3"] + 65, 0.5)
            n0, ng = n["qkv2"], n["gates"]
            xt_act(act, 8, gainB(B_ATTN), n["f3"] + 65 + RING)
            pre_act(act, 6)
            act.wait_ge(s_wf, 16)
            nc.scalar.copy(wfx[:, :, 0:8], wf[:]).then_inc(s_wfh, 1)
            for e in range(4):
                tops_act(act, n0 + UP * e)
                evac_act(act, 2, n0, e, 6, B2_ORDER)
            act.wait_ge(s_qa, 16)
            act.wait_ge(s_qv, 16)
            for k in range(4):
                if k == 3:
                    act.wait_ge(s_ss, 5)
                nc.scalar.activation(sq4[k], qkv[:, k // 2, (k % 2) * 1536:(k % 2) * 1536 + D],
                                     ACT.Square).then_inc(s_sq, 1)
            tops_act(act, n0 + UP * 4)
            evac_act(act, 2, n0, 4, 6, B2_ORDER)
            tops_act(act, n0 + UP * 5)
            evac_act(act, 2, n0, 5, 6, B2_ORDER)
            act.wait_ge(s_fv, 2)
            nc.scalar.activation(lf[:, 1], lf[:, 1], ACT.Exp, scale=-1.0).then_inc(s_fe, 1)
            act.wait_ge(s_fe, 1)
            nc.scalar.activation(lf[:, 1], lf[:, 1], ACT.Ln, bias=1.0).then_inc(s_fe, 1)
            tops_act(act, ng)
            act.wait_ge(s_fc, 1)
            nc.scalar.copy(cH, ps[:, Y, 0:S]).then_inc(s_fh, 1)
            tops_act(act, ng + UP)
            qT_act(act, 2)
            tops_act(act, ng + 2 * UP)
            kT_act(act, 2)
            tops_act(act, ng + 3 * UP, range(3))

            def between_act(i):
                if i == 4:
                    tops_act(act, ng + 3 * UP, range(3, UP))
            attn_act(act, 2, "b2", between_act)
            xt_act(act, 9, None, base=Y)
            act.wait_ge(s_g, 8)
            for g in (0, 1):
                nc.scalar.activation(gates[:, :, g * D:(g + 1) * D], gates[:, :, g * D:(g + 1) * D],
                                     ACT.Sigmoid).then_inc(s_sg, 1)
            for j in range(7):
                hi(act, n["bra"] + RING + j)
            xt_act(act, 10, None, n["brb"] + RING + 3)
            for j in range(7):
                hi(act, n["out2"] + RING + j)
            xt_act(act, 11, gainB(B_FFN), n["out2"] + RING + 7)
            pre_act(act, 7)
            conv_ffn_act(act)

        @block.vector
        def _(dve):
            steps = Steps(dve, s_v)
            dve.sem_inc(s_lo, RING)
            dve.wait_ge(s_gev, 1)
            lo(dve, 0)
            xt_dve(dve, 0, gainA(0, 0), 2)
            for i in range(3, RING):
                lo(dve, i)
            dve.wait_ge(s_cst, 16)
            dve.wait_ge(s_cst2, 16)
            dve.wait_ge(s_rx, 1)
            ffn_dve(dve, 0, n["f0"])
            post_dve(dve, steps, 0, n["f0"] + 65)

            def qkv_dve(m, n0, r, rotate):
                for e in range(4):
                    tops_dve(dve, n0 + UP * e)
                    evac_dve(dve, m, n0, e, r, IN_ORDER)
                if rotate:
                    dve.wait_ge(s_qa, 6 * m + 4)
                    dve.wait_ge(s_qv, 6 * m + 4)
                    dve.wait_ge(s_scr, 16)
                    rope_dve(dve, steps, 0, 32)
                tops_dve(dve, n0 + UP * 4)
                evac_dve(dve, m, n0, 4, r, IN_ORDER)
                tops_dve(dve, n0 + UP * 5, range(1))
                kT_dve(dve, m)

                def between(i):
                    if i == 2:
                        evac_dve(dve, m, n0, 5, r, IN_ORDER)
                    if i in (4, 6, 8):
                        lo(dve, n0 + UP * 5 + RING + i // 2 - 1)
                return between

            xt_dve(dve, 1, gainA(0, 2), n["f0"] + 65 + RING)
            dve.wait_ge(s_lam, 16)
            steps.done(nc.vector.tensor_tensor(lamp[:], lamv[:].rearrange("p (a b) c -> p a b c", b=2)[:, :, 0],
                                               lamv[:].rearrange("p (a b) c -> p a b c", b=2)[:, :, 1], ALU.mult))
            nc.vector.tensor_reduce(lam[:, 0:2], lamp[:], AX_X, ALU.add).then_inc(s_lsum, 1)
            dve.wait_ge(s_lexp, 1)
            steps.done(nc.vector.tensor_tensor(lam[:, 5:6], lam[:, 3:4], lam[:, 2:3], ALU.subtract))
            steps.done(nc.vector.tensor_scalar(lam[:, 4:5], lam[:, 5:6], -LAM_INIT, None, ALU.add))
            dve.wait_ge(s_gev, 2)
            nc.vector.tensor_scalar(gB[:, B_SUB:B_SUB + 1], gB[:, B_SUB:B_SUB + 1], 1.0 - LAM_INIT, None,
                                    ALU.mult).then_inc(s_sub, 1)
            attn_dve(dve, steps, 0, "diff", qkv_dve(0, n["qkv0"], 1, True))
            xt_dve(dve, 2, gain_sub)
            for j in range(6):
                lo(dve, n["out0"] + RING + j)
            post_dve(dve, steps, 1, n["out0"] + 7)
            xt_dve(dve, 3, gainA(0, 4), n["out0"] + 7 + RING)
            dve.wait_ge(s_rx, 3)
            ffn_dve(dve, 1, n["f1"])
            post_dve(dve, steps, 2, n["f1"] + 65)
            xt_dve(dve, 4, gainA(1, 0), n["f1"] + 65 + RING)
            dve.wait_ge(s_rx, 4)
            ffn_dve(dve, 2, n["f2"])
            post_dve(dve, steps, 3, n["f2"] + 65)
            xt_dve(dve, 5, gainA(1, 2), n["f2"] + 65 + RING)
            between = qkv_dve(1, n["qkv1"], 4, False)
            dve.wait_ge(s_nar, 2)
            attn_dve(dve, steps, 1, "na", between)
            xt_dve(dve, 6, None)
            for j in range(6):
                lo(dve, n["out1"] + RING + j)
            post_dve(dve, steps, 4, n["out1"] + 7)
            xt_dve(dve, 7, gainA(1, 4), n["out1"] + 7 + RING)
            dve.wait_ge(s_rx, 6)
            ffn_dve(dve, 3, n["f3"])
            post_dve(dve, steps, 5, n["f3"] + 65)
            n0, ng = n["qkv2"], n["gates"]
            xt_dve(dve, 8, gainB(B_ATTN), n["f3"] + 65 + RING)
            nc.vector.tensor_copy(identr, ident).then_inc(s_idr, 1)
            nc.vector.tensor_copy(causr, caus).then_inc(s_idr, 1)
            dve.wait_ge(s_wfh, 1)
            nc.vector.tensor_tensor(wfx[:, :, 8:16], wf[:], wfx[:, :, 0:8].bitcast(F32), ALU.subtract).then_inc(s_wfl, 1)
            for e in range(4):
                tops_dve(dve, n0 + UP * e)
                evac_dve(dve, 2, n0, e, 6, B2_ORDER)

            def head_scale(t):
                dve.wait_ge(s_ro, 4 + t + 1)
                for half in range(2):
                    v = qkv[:, t, half * 1536:half * 1536 + D].rearrange("p (g c) -> p g c", c=HD)
                    steps.done(nc.vector.tensor_tensor(
                        v, v, ro[:, t, half * 16:(half + 1) * 16].unsqueeze(2).broadcast_to([P, 16, HD]), ALU.mult))
                    for w in range(2):
                        vv = v[:, 8 * w:8 * w + 8]
                        steps.done(nc.vector.tensor_tensor(
                            vv, vv, qkg[:, 2 * half + w].unsqueeze(1).broadcast_to([P, 8, HD]), ALU.mult))

            def gate_logits(c):
                dve.wait_ge(s_used, used(ng + UP * c + 3))
                for t in range(NT):
                    nc.vector.scalar_tensor_tensor(out=gates[:, t, c * 512:(c + 1) * 512],
                                                   in0=ps[:, Z + 2 * (c % 2) + t], scalar=rx[:, t:t + 1],
                                                   in1=bgate[:, c * 512:(c + 1) * 512], op0=ALU.mult,
                                                   op1=ALU.add).then_inc(s_g, 1)

            for k in range(4):
                dve.wait_ge(s_sq, 4 + k + 1)
                nc.vector.tensor_reduce(sso[:, k // 2, (k % 2) * 16:(k % 2 + 1) * 16],
                                        sq4[k].rearrange("p (g c) -> p g c", c=HD), AX_X, ALU.add).then_inc(s_ss, 1)
            tops_dve(dve, n0 + UP * 4)
            evac_dve(dve, 2, n0, 4, 6, B2_ORDER)
            dve.wait_ge(s_b2, 80)
            head_scale(0)
            tops_dve(dve, n0 + UP * 5)
            evac_dve(dve, 2, n0, 5, 6, B2_ORDER)
            dve.wait_ge(s_fz, 2)
            steps.done(nc.vector.tensor_reduce(lf[:, 1], ps[:, Y, 0:32].rearrange("p (t w c) -> p t c w", t=NT, w=2),
                                               AX_X, ALU.add))
            for t in range(NT):
                steps.done(nc.vector.scalar_tensor_tensor(out=lf[:, 0, t], in0=lf[:, 1, t],
                                                          scalar=rx[:, t:t + 1], in1=bfg[:], op0=ALU.mult, op1=ALU.add))
            nc.vector.tensor_scalar(lf[:, 2], lf[:, 0], 0.0, None, ALU.min).then_inc(s_fv, 1)
            dve.wait_ge(s_fv, 1)
            nc.vector.scalar_tensor_tensor(out=lf[:, 1], in0=lf[:, 2], scalar=-2.0, in1=lf[:, 0],
                                           op0=ALU.mult, op1=ALU.add).then_inc(s_fv, 1)
            head_scale(1)
            dve.wait_ge(s_fe, 2)
            dve.wait_ge(s_one, 3)
            nc.vector.tensor_tensor(lf4.rearrange("p t (g c) -> p t g c", g=4)[:, :, :, 0:8],
                                    lf[:, 2].unsqueeze(2).broadcast_to([P, NT, 4, 8]),
                                    lf[:, 1].unsqueeze(2).broadcast_to([P, NT, 4, 8]), ALU.subtract).then_inc(s_fv, 1)
            tops_dve(dve, ng)
            dve.wait_ge(s_aux2, 16)
            gate_logits(0)
            rope_dve(dve, steps, 0, 16)
            dve.wait_ge(s_fh, 1)
            steps.done(nc.vector.tensor_copy(cL[0:32], cH[0:32].bitcast(F32)))
            steps.done(nc.vector.tensor_tensor(cL[32:64], ps[32:64, Y, 0:S], cH[32:64].bitcast(F32), ALU.subtract))
            steps.done(nc.vector.tensor_scalar(cB[64:96], cH[64:96].bitcast(F32), -1.0, None, ALU.mult))
            nc.vector.tensor_tensor(cB[96:128], cH[96:128].bitcast(F32), ps[96:128, Y, 0:S], ALU.subtract).then_inc(s_fcv, 1)
            tops_dve(dve, ng + UP)
            gate_logits(1)
            tops_dve(dve, ng + 2 * UP)
            kT_dve(dve, 2)
            gate_logits(2)
            tops_dve(dve, ng + 3 * UP, range(2))

            def between_dve(i):
                if i == 2:
                    gate_logits(3)
                if i in (6, 8):
                    lo(dve, ng + 3 * UP + RING + i // 2 - 1)
            attn_dve(dve, steps, 2, "b2", between_dve)
            xt_dve(dve, 9, None, base=Y)
            for j in range(4):
                lo(dve, n["bra"] + RING + j)
            dve.wait_ge(s_used, used(n["bra"] + 3))
            dve.wait_ge(s_sg, 2)
            for t in range(NT):
                steps.done(nc.vector.tensor_tensor(osb[:, t], gates[:, t, 0:D], bank(Z + 2 * t), ALU.mult))
            for j in range(2):
                lo(dve, n["brb"] + RING + j)
            for idx in range(4):
                t, c = idx // 2, slice((idx % 2) * 512, (idx % 2 + 1) * 512)
                y_bank(dve, 7, n["brb"] + 3, idx)
                if idx >= 2:
                    dve.wait_ge(s_src, 36 + idx - 1)
                steps.done(nc.vector.tensor_tensor(sqa[:, c], gates[:, t, D + (idx % 2) * 512:D + (idx % 2 + 1) * 512], ps[:, Y + idx], ALU.mult))
                nc.vector.tensor_tensor(osb[:, t, c], osb[:, t, c], sqa[:, c], ALU.add).then_inc(s_src, 1)
            xt_dve(dve, 10, None, n["brb"] + RING + 3)
            for j in range(6):
                lo(dve, n["out2"] + RING + j)
            add_dve(dve, 8, n["out2"] + 7)
            xt_dve(dve, 11, gainB(B_FFN), n["out2"] + RING + 7)
            conv_ffn_dve(dve, steps)

        @block.tensor
        def _(pe):
            pe.sem_inc(s_used, RING)
            pe.wait_ge(s_cst, 16)
            keep_warm(pe, 5, ps[:, Y + 2, 0:P])
            pe.wait_ge(s_rows, 16)
            nc.tensor.transpose(ps[:, Y, 0:96], rowsA, ident[0:96, 0:96]).then_inc(s_gT, 1)
            xt_pe(pe, 0, h)
            pe.wait_ge(s_rowsB, 80)
            nc.tensor.transpose(ps[:, Y + 1, 0:B_END], rowsB, ident[0:B_END, 0:B_END]).then_inc(s_gT, 1)
            ffn_pe(pe, 0, n["f0"], 0)

            def qkv_pe(m, n0, r, kind):
                for e in range(5):
                    chunk_pe(pe, m, n0, e, range(UP), r if e == 0 else None)
                if kind == "diff":
                    pe.wait_ge(s_qr, 1)
                    pe.wait_ge(s_cst2, 16)
                pe.wait_ge(s_qa, 6 * m + 4)
                pe.wait_ge(s_qv, 6 * m + 4)
                qk_turn(pe, m, kind, 0)
                chunk_pe(pe, m, n0, 5, range(2))
                qk_turn(pe, m, kind, 1)
                chunk_pe(pe, m, n0, 5, range(2, 3))

                def between(i):
                    if i == 2:
                        chunk_pe(pe, m, n0, 5, range(3, UP))
                return between

            xt_pe(pe, 1, h)
            attn_pe(pe, 0, "diff", qkv_pe(0, n["qkv0"], 1, "diff"))
            xt_pe(pe, 2, o_sb)
            proj_pe(pe, n["out0"], 2, 8, Y)
            xt_pe(pe, 3, h)
            ffn_pe(pe, 1, n["f1"], 3)
            xt_pe(pe, 4, h)
            ffn_pe(pe, 2, n["f2"], 4)
            xt_pe(pe, 5, h)
            attn_pe(pe, 1, "na", qkv_pe(1, n["qkv1"], 5, "na"))
            xt_pe(pe, 6, o_sb, reverse=True)
            proj_pe(pe, n["out1"], 6, 8, Y)
            xt_pe(pe, 7, h)
            ffn_pe(pe, 3, n["f3"], 7)
            n0, ng = n["qkv2"], n["gates"]

            def gate_pe(c, units):
                if c < 2:
                    pe.wait_ge(s_qa, 17 + c)
                    pe.wait_ge(s_qv, 17 + c)
                else:
                    pe.wait_ge(s_g, 2 * (c - 1))
                for j in units:
                    col_unit(pe, ng + UP * c + j, 0, j, [Z + 2 * (c % 2), Z + 2 * (c % 2) + 1])

            xt_pe(pe, 8, h)

            def forget_logits(t):
                c = slice(t * P, (t + 1) * P)
                o = ps[:, Y, t * 16:t * 16 + 16]
                for k in range(KT):
                    nc.tensor.matmul(o, xhi[:, k, c], wfx[:, k], start=k == 0, stop=False)
                    ins = nc.tensor.matmul(o, xlo[:, k, c], wfx[:, k], start=False, stop=k == KT - 1)
                ins.then_inc(s_fz, 1)

            for e in range(4):
                chunk_pe(pe, 2, n0, e, range(UP), 8 if e == 0 else None)
            pe.wait_ge(s_wfl, 1)
            forget_logits(0)
            chunk_pe(pe, 2, n0, 4, range(UP))
            forget_logits(1)
            chunk_pe(pe, 2, n0, 5, range(UP))
            gate_pe(0, range(UP))
            pe.wait_ge(s_fv, 3)
            for t in range(NT):
                ins = nc.tensor.matmul(ps[:, Y, 0:S], lf4[:, t], tri[:, t], start=t == 0, stop=t == NT - 1)
            ins.then_inc(s_fc, 1)
            gate_pe(1, range(UP))
            pe.wait_ge(s_qr, 2)
            pe.wait_ge(s_fcv, 1)
            qk_turn(pe, 2, "b2", 0)
            gate_pe(2, range(2))
            qk_turn(pe, 2, "b2", 1)
            gate_pe(2, range(2, UP))
            gate_pe(3, range(3))

            def between_pe(i):
                if i == 2:
                    gate_pe(3, range(3, UP))
            attn_pe(pe, 2, "b2", between_pe)
            xt_pe(pe, 9, o_sb, base=Y)
            proj_pe(pe, n["bra"], 9, 4, Z, 0, early=False)
            pe.wait_ge(s_xl, 40)
            proj_pe(pe, n["brb"], 9, 4, Y, 4)
            xt_pe(pe, 10, osb)
            proj_pe(pe, n["out2"], 10, 8, Y)
            xt_pe(pe, 11, h)
            conv_ffn_pe(pe)


def constants():
    import numpy as np
    c = np.zeros((P, C_END), np.float32)
    c[:, C_ID:C_ID + P] = np.eye(P, dtype=np.float32)
    half = 8
    inv = np.float32(500000.0) ** (-np.arange(0, 16, 2, dtype=np.float32) / np.float32(16))
    ang = np.arange(S, dtype=np.float32)[:, None] * inv[None, :].astype(np.float32)
    cos, sin = np.cos(ang).astype(np.float32), np.sin(ang).astype(np.float32)
    table = np.concatenate([cos, cos, -sin, sin], axis=1).reshape(NT, P, 4 * half)
    for t in range(NT):
        c[:, C_ROPE + 32 * t:C_ROPE + 32 * (t + 1)] = table[t]
    q = np.arange(P)
    c[:, C_FLIP:C_FLIP + P] = (q[:, None] // GW == q[None] // GW) & (q[:, None] % GW == GW - 1 - q[None] % GW)
    start = np.clip(GW - 1 - q % GW - 8, 0, GW - 16)
    k = np.arange(GW)
    c[:, C_WIN:C_WIN + GW] = np.where((k[None] >= start[:, None]) & (k[None] < start[:, None] + 16), 0.0, MASKED)
    c[:, C_CAUS:C_CAUS + P] = np.where(q[None] <= q[:, None], 0.0, MASKED)
    s = np.arange(S)
    for t in range(NT):
        c[:, C_TRI + S * t:C_TRI + S * (t + 1)] = (q[:, None] + t * P <= s[None])
    c[:, C_HEAD:C_HEAD + 8] = q[:, None] % 32 == np.arange(8)[None]
    return c


_INS = ['x', 'norm_g', 'ffn1_wg', 'ffn1_wu', 'ffn1_wd', 'ffn2_wg', 'ffn2_wu', 'ffn2_wd', 'diff_w_in', 'diff_w_out',
        'diff_lambda', 'diff_subln', 'na_w_in', 'na_w_out', 'na_rpb', 'attn_norm_g_2', 'w_in_2', 'b_forget_2',
        'b_gate_2', 'moba_q_norm_g_2', 'moba_k_norm_g_2', 'fox_q_norm_g_2', 'fox_k_norm_g_2',
        'w_branch_moba_2', 'w_branch_fox_2', 'w_out_2', 'ffn_norm_g_2', 'w_ffn_up_2', 'ffn_conv_w_2',
        'ffn_conv_b_2', 'w_ffn_down_2']
_OUTS = [((1, S, D), 'float32')]


def kernel(**inputs):
    import numpy as _np
    import concourse.bacc as _bacc
    from concourse import mybir as _mybir
    from concourse.bass_utils import run_bass_kernel_spmd as _run

    nc = _bacc.Bacc("TRN2", target_bir_lowering=False, num_devices=1)
    arrays, args = {}, []
    given = [(name, _np.ascontiguousarray(inputs[name])) for name in _INS]
    given.append(("const_pack", constants()))
    for name, a in given:
        arrays[f"in_{name}_dram"] = a
        args.append(nc.dram_tensor(f"in_{name}_dram", a.shape, _mybir.dt.from_np(a.dtype), kind="ExternalInput").ap())
    for i, (shape, dtype) in enumerate(_OUTS):
        dt = _mybir.dt.from_np(_np.dtype(dtype))
        args.append(nc.dram_tensor(f"out_{i}_dram", shape, dt, kind="ExternalOutput").ap())
    build(nc, *args)
    r = _run(nc, [arrays], core_ids=[0])
    got = tuple(r.results[0][f"out_{i}_dram"] for i in range(len(_OUTS)))
    return got[0]
```
